# Optimizing a Trainium2 kernel written in Bass

```python
import jax, jax.numpy as jnp
from jax import lax
import numpy as np

D_MODEL = 1024
BATCH = 1
SEQ = 512
DEPTH = 2

CHUNK = 64

D_RWKV = D_MODEL // 2
HEAD_SIZE = 64
N_HEADS = D_RWKV // HEAD_SIZE
D_DECAY_LORA = max(32, int(round(1.8 * D_MODEL ** 0.5 / 32)) * 32)
D_AAA_LORA = max(32, int(round(1.8 * D_MODEL ** 0.5 / 32)) * 32)
D_MV_LORA = max(32, int(round(0.7 * D_MODEL ** 0.5 / 32)) * 32)
D_GATE_LORA = max(32, int(round(0.6 * D_MODEL ** 0.8 / 32)) * 32)

D_POOL = D_MODEL // 2
POOL_WINDOWS = (2, 4, 8, 16)
N_POOL_GROUPS = len(POOL_WINDOWS)
POOL_GROUP = D_POOL // N_POOL_GROUPS

D_FF = ((8 * D_MODEL // 3 + 255) // 256) * 256

N_SHIFT = 3 * D_RWKV + D_DECAY_LORA + D_AAA_LORA + D_GATE_LORA
N_IN = N_SHIFT + D_POOL + 2 * D_MODEL
N_MOD = 6 * D_MODEL

EPS_RMS = 1e-6
EPS_GN = 64e-5


def rms_norm(x, g):
    xf = x.astype(jnp.float32)
    y = xf * lax.rsqrt(jnp.mean(xf * xf, axis=-1, keepdims=True) + EPS_RMS)
    return (y * g.astype(jnp.float32)).astype(x.dtype)

def token_shift(z, mu):
    prev = jnp.pad(z, ((0, 0), (1, 0), (0, 0)))[:, :-1]
    return z + (prev - z) * mu

def wkv7_scan(r, w, k, v, kk, a):
    B, S, H, N = r.shape

    def to_chunks(t):
        return jnp.moveaxis(t, 1, 0).reshape(S // CHUNK, CHUNK, B, H, N)

    def step(state, inp):
        r_t, w_t, k_t, v_t, kk_t, a_t = inp
        sk = jnp.einsum('bhvk,bhk->bhv', state, kk_t)
        state = (state * w_t[:, :, None, :]
                 - sk[..., None] * (a_t * kk_t)[:, :, None, :]
                 + v_t[..., None] * k_t[:, :, None, :])
        return state, jnp.einsum('bhvk,bhk->bhv', state, r_t)

    def chunk_step(state, chunk_inp):
        return lax.scan(step, state, chunk_inp)

    state0 = jnp.zeros((B, H, N, N), jnp.float32)
    _, ys = lax.scan(chunk_step, state0, tuple(to_chunks(t) for t in (r, w, k, v, kk, a)))
    return jnp.moveaxis(ys.reshape(S, B, H, N), 0, 1)

def rwkv7_time_mix(ps, vl, v_first, w0, w_up, a0, a_up, v0, v_up, g_up, k_k, k_a, r_k, lnx_g, lnx_b):
    B, S, _ = ps.shape
    dt = ps.dtype
    f32 = jnp.float32
    o = 0
    r = ps[..., o:o + D_RWKV]; o += D_RWKV
    k = ps[..., o:o + D_RWKV]; o += D_RWKV
    v = ps[..., o:o + D_RWKV]; o += D_RWKV
    wl = ps[..., o:o + D_DECAY_LORA]; o += D_DECAY_LORA
    al = ps[..., o:o + D_AAA_LORA]; o += D_AAA_LORA
    gl = ps[..., o:o + D_GATE_LORA]

    log_w = -jax.nn.softplus(-(w0 + jnp.tanh(wl) @ w_up)) - 0.5
    decay = jnp.exp(-jnp.exp(log_w.astype(f32)))
    a = jax.nn.sigmoid(a0 + al @ a_up)
    g = jax.nn.sigmoid(gl) @ g_up
    if vl is None:
        v_first = v
    else:
        v = v + (v_first - v) * jax.nn.sigmoid(v0 + vl @ v_up)

    def heads(t):
        return t.reshape(B, S, N_HEADS, HEAD_SIZE).astype(f32)

    kk = heads(k * k_k)
    kk = kk / jnp.maximum(jnp.sqrt(jnp.sum(kk * kk, axis=-1, keepdims=True)), 1e-12)
    k = k * (1 + (a - 1) * k_a)
    r_h, k_h, v_h, a_h, w_h = heads(r), heads(k), heads(v), heads(a), heads(decay)

    y = wkv7_scan(r_h, w_h, k_h, v_h, kk, a_h)
    mean = jnp.mean(y, axis=-1, keepdims=True)
    var = jnp.mean(jnp.square(y - mean), axis=-1, keepdims=True)
    y = (y - mean) * lax.rsqrt(var + EPS_GN)
    y = y.reshape(B, S, D_RWKV) * lnx_g.astype(f32) + lnx_b.astype(f32)
    bonus = jnp.sum(r_h * k_h * r_k.astype(f32), axis=-1, keepdims=True) * v_h
    y = (y + bonus.reshape(B, S, D_RWKV)) * g.astype(f32)
    return y.astype(dt), v_first

def multiscale_pool(z, pool_w, pool_scale):
    B, S, _ = z.shape
    zg = z.reshape(B, S, N_POOL_GROUPS, POOL_GROUP).astype(jnp.float32)
    cs = jnp.cumsum(zg, axis=1)
    pos = jnp.arange(1, S + 1, dtype=jnp.float32)
    means = []
    for gi, win in enumerate(POOL_WINDOWS):
        cg = cs[:, :, gi]
        lower = jnp.pad(cg, ((0, 0), (win, 0), (0, 0)))[:, :S]
        count = jnp.minimum(pos, float(win))[None, :, None]
        means.append((cg - lower) / count)
    pooled = (jnp.stack(means, axis=2) - zg).astype(z.dtype)
    y = jnp.einsum('bsgc,gcd->bsgd', pooled, pool_w)
    return y.reshape(B, S, D_POOL) * pool_scale

def first_inputs(seed: int = 0) -> dict:
    key = jax.random.key(seed)
    ks = iter(jax.random.split(key, 32))
    f32 = jnp.float32

    def nrm(shape, s):
        return jax.random.normal(next(ks), shape, f32) * s

    def uni(shape, lo, hi):
        return jax.random.uniform(next(ks), shape, f32, lo, hi)

    L, Lv = DEPTH, DEPTH - 1
    return {
        "x": nrm((BATCH, SEQ, D_MODEL), 1.0),
        "c": nrm((BATCH, D_MODEL), 1.0),
        "ada_w": nrm((L, D_MODEL, N_MOD), 0.5 * D_MODEL ** -0.5),
        "ada_b": nrm((L, N_MOD), 0.1),
        "norm1_g": 1.0 + nrm((L, D_MODEL), 0.1),
        "w_in": nrm((L, D_MODEL, N_IN), D_MODEL ** -0.5),
        "v_down": nrm((Lv, D_MODEL, D_MV_LORA), D_MODEL ** -0.5),
        "mu_shift": uni((L, N_SHIFT), 0.0, 1.0),
        "mu_v": uni((Lv, D_MV_LORA), 0.0, 1.0),
        "w0": uni((L, D_RWKV), -6.0, -1.0),
        "w_up": nrm((L, D_DECAY_LORA, D_RWKV), 0.5 * D_DECAY_LORA ** -0.5),
        "a0": nrm((L, D_RWKV), 0.1),
        "a_up": nrm((L, D_AAA_LORA, D_RWKV), 0.5 * D_AAA_LORA ** -0.5),
        "v0": nrm((Lv, D_RWKV), 0.1),
        "v_up": nrm((Lv, D_MV_LORA, D_RWKV), 0.5 * D_MV_LORA ** -0.5),
        "g_up": nrm((L, D_GATE_LORA, D_RWKV), D_GATE_LORA ** -0.5),
        "k_k": 0.85 + nrm((L, D_RWKV), 0.05),
        "k_a": 1.0 + nrm((L, D_RWKV), 0.05),
        "r_k": nrm((L, N_HEADS, HEAD_SIZE), 0.1),
        "lnx_g": 1.0 + nrm((L, D_RWKV), 0.1),
        "lnx_b": nrm((L, D_RWKV), 0.02),
        "pool_w": nrm((L, N_POOL_GROUPS, POOL_GROUP, POOL_GROUP), POOL_GROUP ** -0.5),
        "pool_scale": 1.0 + nrm((L, D_POOL), 0.1),
        "proj_a": nrm((L, D_RWKV, D_MODEL), D_RWKV ** -0.5),
        "proj_b": nrm((L, D_POOL, D_MODEL), D_POOL ** -0.5),
        "w_out": nrm((L, D_MODEL, D_MODEL), D_MODEL ** -0.5),
        "norm2_g": 1.0 + nrm((L, D_MODEL), 0.1),
        "w_gu": nrm((L, D_MODEL, 2 * D_FF), D_MODEL ** -0.5),
        "w_down": nrm((L, D_FF, D_MODEL), D_FF ** -0.5),
        "final_g": 1.0 + nrm((D_MODEL,), 0.1),
    }

def first_block(x, c, ada_w, ada_b, norm1_g, w_in, v_down, mu_shift, mu_v, w0, w_up, a0, a_up, v0, v_up,
              g_up, k_k, k_a, r_k, lnx_g, lnx_b, pool_w, pool_scale, proj_a, proj_b, w_out, norm2_g,
              w_gu, w_down, final_g):
    B, S, D = x.shape
    c_act = jax.nn.silu(c)
    v_first = None
    for l in range(DEPTH):
        mod = c_act @ ada_w[l] + ada_b[l]
        sh1, sc1, gt1, sh2, sc2, gt2 = [m[:, None, :] for m in jnp.split(mod, 6, axis=-1)]

        h = rms_norm(x, norm1_g[l]) * (1 + sc1) + sh1
        if l == 0:
            p = h @ w_in[0]
            vl = None
        else:
            p = h @ jnp.concatenate([w_in[l], v_down[l - 1]], axis=1)
            vl = token_shift(p[..., N_IN:], mu_v[l - 1])
        ps = token_shift(p[..., :N_SHIFT], mu_shift[l])
        z_pool = p[..., N_SHIFT:N_SHIFT + D_POOL]
        br_gate = jax.nn.sigmoid(p[..., N_SHIFT + D_POOL:N_IN]).reshape(B, S, 2, D)

        y_a, v_first = rwkv7_time_mix(ps, vl, v_first, w0[l], w_up[l], a0[l], a_up[l],
                                      None if l == 0 else v0[l - 1], None if l == 0 else v_up[l - 1],
                                      g_up[l], k_k[l], k_a[l], r_k[l], lnx_g[l], lnx_b[l])
        y_b = multiscale_pool(z_pool, pool_w[l], pool_scale[l])
        mixed = br_gate[:, :, 0] * (y_a @ proj_a[l]) + br_gate[:, :, 1] * (y_b @ proj_b[l])
        x = x + gt1 * (mixed @ w_out[l])

        h2 = rms_norm(x, norm2_g[l]) * (1 + sc2) + sh2
        gate, up = jnp.split(h2 @ w_gu[l], 2, axis=-1)
        x = x + gt2 * ((jax.nn.silu(gate) * up) @ w_down[l])
    return rms_norm(x, final_g)


GRID_W = 64
PLE_DIM = 256
EPS = 1e-6
GLA_HEADS = 4
GLA_DK = 128
GLA_DV = 256
GLA_KEY = GLA_HEADS * GLA_DK
GLA_VAL = GLA_HEADS * GLA_DV
GLA_RANK = 16
GLA_TAU = 16.0
GLA_CHUNK = 64
ATTN_HEADS = 8
ATTN_KV_HEADS = 2
HEAD_DIM = 128
ATTN_Q = ATTN_HEADS * HEAD_DIM
ATTN_KV = ATTN_KV_HEADS * HEAD_DIM
Q_BLOCK = 128
ROPE_THETA = 10000.0
ROPE_AXIS_DIM = HEAD_DIM // 2
FFN_HIDDEN = -(-8 * D_MODEL // (3 * 256)) * 256
IN_SPLITS = (GLA_KEY, GLA_KEY, GLA_VAL, GLA_VAL, GLA_RANK, GLA_RANK,
             ATTN_Q, ATTN_KV, ATTN_KV, D_MODEL, D_MODEL)
IN_WIDTH = sum(IN_SPLITS)


def rms_norm_2(x, g):
    xf = x.astype(jnp.float32)
    y = xf * lax.rsqrt(jnp.mean(xf * xf, axis=-1, keepdims=True) + EPS)
    return (y * g.astype(jnp.float32)).astype(x.dtype)

def axial_rope_tables(seq_len):
    rows = seq_len // GRID_W
    row = jnp.repeat(jnp.arange(rows, dtype=jnp.float32), GRID_W)
    col = jnp.tile(jnp.arange(GRID_W, dtype=jnp.float32), rows)
    inv = ROPE_THETA ** (-jnp.arange(0, ROPE_AXIS_DIM, 2, dtype=jnp.float32) / ROPE_AXIS_DIM)
    ang = jnp.stack([row[:, None] * inv, col[:, None] * inv], axis=1)
    return jnp.cos(ang), jnp.sin(ang)

def apply_axial_rope(x, cos, sin):
    b, s, h, d = x.shape
    xr = x.astype(jnp.float32).reshape(b, s, h, 2, 2, d // 4)
    c = cos[None, :, None]
    sn = sin[None, :, None]
    x1, x2 = xr[..., 0, :], xr[..., 1, :]
    out = jnp.stack([x1 * c - x2 * sn, x2 * c + x1 * sn], axis=-2)
    return out.reshape(b, s, h, d).astype(x.dtype)

def gla_chunked(q, k, v, log_a):
    b, s, h, dk = q.shape
    dv = v.shape[-1]
    n = s // GLA_CHUNK
    c = GLA_CHUNK

    def chunks(t):
        return t.reshape(b, n, c, h, t.shape[-1]).transpose(1, 0, 3, 2, 4)

    q, k, v, la = chunks(q), chunks(k), chunks(v), chunks(log_a)
    cum = jnp.cumsum(la, axis=3)
    last = cum[:, :, :, -1:, :]
    q_dec = q * jnp.exp(cum)
    k_intra = k * jnp.exp(-cum)
    k_state = k * jnp.exp(last - cum)
    mask = jnp.tril(jnp.ones((c, c), dtype=bool))
    scores = jnp.where(mask, jnp.einsum('nbhid,nbhjd->nbhij', q_dec, k_intra), 0.0)
    o_intra = jnp.einsum('nbhij,nbhjv->nbhiv', scores, v)

    def step(state, xs):
        qd, ks, vc, lst = xs
        o = jnp.einsum('bhid,bhdv->bhiv', qd, state)
        state = state * jnp.exp(lst[:, :, 0, :])[..., None] + jnp.einsum('bhjd,bhjv->bhdv', ks, vc)
        return state, o

    s0 = jnp.zeros((b, h, dk, dv), jnp.float32)
    _, o_inter = lax.scan(step, s0, (q_dec, k_state, v, last))
    o = o_intra + o_inter
    return o.transpose(1, 0, 3, 2, 4).reshape(b, s, h, dv)

def gqa_attention(q, k, v):
    b, s, hq, hd = q.shape
    hkv = k.shape[2]
    g = hq // hkv
    nb = s // Q_BLOCK
    qb = q.reshape(b, nb, Q_BLOCK, hkv, g, hd).transpose(1, 0, 2, 3, 4, 5)
    scale = hd ** -0.5

    def block(qblk):
        sc = jnp.einsum('bqkgd,bskd->bkgqs', qblk, k).astype(jnp.float32) * scale
        pr = jax.nn.softmax(sc, axis=-1).astype(v.dtype)
        return jnp.einsum('bkgqs,bskd->bqkgd', pr, v)

    out = lax.map(block, qb)
    return out.transpose(1, 0, 2, 3, 4, 5).reshape(b, s, hq * hd)

def hybrid_layer(h, p_i, cos, sin, g_mix_pre, w_in, w_alpha_up, b_alpha, g_gla_out,
                 g_q_norm, g_k_norm, w_o_gla, w_o_attn, w_out, g_mix_post,
                 g_ffn_pre, w_ffn_in, w_ffn_out, g_ffn_post, w_ple_proj, w_ple_gate, g_ple_post):
    b, s, _ = h.shape
    f32 = jnp.float32
    u = rms_norm_2(h, g_mix_pre)
    offsets = np.cumsum(IN_SPLITS)[:-1].tolist()
    (gq, gk, gv, gg, ra_f, ra_b, aq, ak, av, gate_a, gate_b) = jnp.split(u @ w_in, offsets, axis=-1)

    qh = gq.astype(f32).reshape(b, s, GLA_HEADS, GLA_DK) * (GLA_DK ** -0.5)
    kh = gk.astype(f32).reshape(b, s, GLA_HEADS, GLA_DK)
    vh = gv.astype(f32).reshape(b, s, GLA_HEADS, GLA_DV)
    la_f = (jax.nn.log_sigmoid(ra_f.astype(f32) @ w_alpha_up[0].astype(f32) + b_alpha[0].astype(f32))
            / GLA_TAU).reshape(b, s, GLA_HEADS, GLA_DK)
    la_b = (jax.nn.log_sigmoid(ra_b.astype(f32) @ w_alpha_up[1].astype(f32) + b_alpha[1].astype(f32))
            / GLA_TAU).reshape(b, s, GLA_HEADS, GLA_DK)
    o_f = gla_chunked(qh, kh, vh, la_f)
    o_b = gla_chunked(qh[:, ::-1], kh[:, ::-1], vh[:, ::-1], la_b[:, ::-1])[:, ::-1]
    o_gla = rms_norm_2(o_f + o_b, g_gla_out).reshape(b, s, GLA_VAL).astype(h.dtype)
    branch_a = (o_gla * jax.nn.silu(gg)) @ w_o_gla

    q = apply_axial_rope(rms_norm_2(aq.reshape(b, s, ATTN_HEADS, HEAD_DIM), g_q_norm), cos, sin)
    k = apply_axial_rope(rms_norm_2(ak.reshape(b, s, ATTN_KV_HEADS, HEAD_DIM), g_k_norm), cos, sin)
    v = av.reshape(b, s, ATTN_KV_HEADS, HEAD_DIM)
    branch_b = gqa_attention(q, k, v) @ w_o_attn

    mixed = jax.nn.sigmoid(gate_a) * branch_a + jax.nn.sigmoid(gate_b) * branch_b
    h = h + rms_norm_2(mixed @ w_out, g_mix_post)

    gate, up = jnp.split(rms_norm_2(h, g_ffn_pre) @ w_ffn_in, 2, axis=-1)
    h = h + rms_norm_2((jax.nn.silu(gate) * up) @ w_ffn_out, g_ffn_post)

    e = p_i @ w_ple_proj
    h = h + rms_norm_2(jax.nn.sigmoid(h @ w_ple_gate) * e, g_ple_post)
    return h

def second_inputs(seed: int = 0) -> dict:
    key = jax.random.key(seed)
    ks = jax.random.split(key, 24)
    f32 = jnp.float32

    def w(k, shape, fan_in):
        return jax.random.normal(k, shape, f32) * (fan_in ** -0.5)

    def gain(k, shape):
        return 1.0 + 0.05 * jax.random.normal(k, shape, f32)

    return {
        "x": jax.random.normal(ks[0], (BATCH, SEQ, D_MODEL), f32),
        "p": jax.random.normal(ks[1], (DEPTH, BATCH, SEQ, PLE_DIM), f32),
        "g_mix_pre": gain(ks[2], (DEPTH, D_MODEL)),
        "w_in": w(ks[3], (DEPTH, D_MODEL, IN_WIDTH), D_MODEL),
        "w_alpha_up": w(ks[4], (DEPTH, 2, GLA_RANK, GLA_KEY), GLA_RANK),
        "b_alpha": 1.0 + 0.1 * jax.random.normal(ks[5], (DEPTH, 2, GLA_KEY), f32),
        "g_gla_out": gain(ks[6], (DEPTH, GLA_DV)),
        "g_q_norm": gain(ks[7], (DEPTH, HEAD_DIM)),
        "g_k_norm": gain(ks[8], (DEPTH, HEAD_DIM)),
        "w_o_gla": w(ks[9], (DEPTH, GLA_VAL, D_MODEL), GLA_VAL),
        "w_o_attn": w(ks[10], (DEPTH, ATTN_Q, D_MODEL), ATTN_Q),
        "w_out": w(ks[11], (DEPTH, D_MODEL, D_MODEL), D_MODEL),
        "g_mix_post": gain(ks[12], (DEPTH, D_MODEL)),
        "g_ffn_pre": gain(ks[13], (DEPTH, D_MODEL)),
        "w_ffn_in": w(ks[14], (DEPTH, D_MODEL, 2 * FFN_HIDDEN), D_MODEL),
        "w_ffn_out": w(ks[15], (DEPTH, FFN_HIDDEN, D_MODEL), FFN_HIDDEN),
        "g_ffn_post": gain(ks[16], (DEPTH, D_MODEL)),
        "w_ple_proj": w(ks[17], (DEPTH, PLE_DIM, D_MODEL), PLE_DIM),
        "w_ple_gate": w(ks[18], (DEPTH, D_MODEL, D_MODEL), D_MODEL),
        "g_ple_post": gain(ks[19], (DEPTH, D_MODEL)),
    }

def second_block(x, p, g_mix_pre, w_in, w_alpha_up, b_alpha, g_gla_out, g_q_norm, g_k_norm,
              w_o_gla, w_o_attn, w_out, g_mix_post, g_ffn_pre, w_ffn_in, w_ffn_out,
              g_ffn_post, w_ple_proj, w_ple_gate, g_ple_post):
    cos, sin = axial_rope_tables(x.shape[1])
    h = x
    for i in range(DEPTH):
        h = hybrid_layer(h, p[i], cos, sin, g_mix_pre[i], w_in[i], w_alpha_up[i], b_alpha[i],
                         g_gla_out[i], g_q_norm[i], g_k_norm[i], w_o_gla[i], w_o_attn[i],
                         w_out[i], g_mix_post[i], g_ffn_pre[i], w_ffn_in[i], w_ffn_out[i],
                         g_ffn_post[i], w_ple_proj[i], w_ple_gate[i], g_ple_post[i])
    return h


def setup_inputs(seed=0):
    out = dict(first_inputs(seed))
    for name, value in second_inputs(seed + 1).items():
        if name != "x":
            out[name + "_2"] = value
    return out


def reference(
    x, c, ada_w, ada_b, norm1_g, w_in, v_down, mu_shift, mu_v, w0, w_up, a0, a_up, v0, v_up,
    g_up, k_k, k_a, r_k, lnx_g, lnx_b, pool_w, pool_scale, proj_a, proj_b, w_out, norm2_g, w_gu,
    w_down, final_g, p_2, g_mix_pre_2, w_in_2, w_alpha_up_2, b_alpha_2, g_gla_out_2, g_q_norm_2,
    g_k_norm_2, w_o_gla_2, w_o_attn_2, w_out_2, g_mix_post_2, g_ffn_pre_2, w_ffn_in_2,
    w_ffn_out_2, g_ffn_post_2, w_ple_proj_2, w_ple_gate_2, g_ple_post_2,
):
    x = first_block(
        x, c, ada_w, ada_b, norm1_g, w_in, v_down, mu_shift, mu_v, w0, w_up, a0, a_up, v0, v_up,
        g_up, k_k, k_a, r_k, lnx_g, lnx_b, pool_w, pool_scale, proj_a, proj_b, w_out, norm2_g,
        w_gu, w_down, final_g,
    )
    return second_block(
        x, p_2, g_mix_pre_2, w_in_2, w_alpha_up_2, b_alpha_2, g_gla_out_2, g_q_norm_2,
        g_k_norm_2, w_o_gla_2, w_o_attn_2, w_out_2, g_mix_post_2, g_ffn_pre_2, w_ffn_in_2,
        w_ffn_out_2, g_ffn_post_2, w_ple_proj_2, w_ple_gate_2, g_ple_post_2,
    )


_drawn_inputs = setup_inputs


def setup_inputs(seed=0):
    import zlib

    import numpy as np

    out = dict(_drawn_inputs(seed))
    spreads = {}
    factors = {'mu_v': 2.956,
     'w_up': 4.793,
     'a0': 4.62,
     'v0': 5.582,
     'lnx_b': 8.0,
     'g_q_norm_2': 8.0,
     'g_k_norm_2': 8.0}
    for name, (base, spread) in spreads.items():
        noise = np.random.default_rng([zlib.crc32(name.encode()), seed]).standard_normal(out[name].shape)
        drawn = base * np.exp(spread * noise) if base else spread * noise
        out[name] = __import__('jax').numpy.asarray(drawn.astype(out[name].dtype))
    for name, factor in factors.items():
        out[name] = (out[name] * factor).astype(out[name].dtype)
    return out
```

```python
from contextlib import ExitStack

import numpy as np

import concourse.bass as bass
from concourse import mybir

F32 = mybir.dt.float32
F32R = mybir.dt.float32r
ALU = mybir.AluOpType
ACT = mybir.ActivationFunctionType
AX = mybir.AxisListType

P = 128
T = 512
NCH = T // P
D = 1024
DT = D // P
DEPTH = 2
SLAB = 16
D_R = 512
RT = D_R // P
HEAD = 64
NH = D_R // HEAD
HID = 2816
HT = HID // P
HALF = HT // 2
WINDOWS = (2, 4, 8, 16)
EXP_MHALF = float(np.exp(np.float32(-0.5)))
EPS_RMS = 1e-6
EPS_GN = 64e-5
GH = 4
GDK = 128
GDV = 256
TAU = 16.0
QH = 8
KVH = 2
LEVELS = (1, 2, 4, 8, 16, 32, 64)

C1 = {}
_at = 0
for _n, _w in (("ada_b", 48), ("norm1_g", 8), ("norm2_g", 8), ("mu", 15), ("w0", 4), ("a0", 4), ("v0", 4),
               ("k_k", 4), ("k_a", 4), ("r_k", 4), ("lnx_g", 4), ("lnx_b", 4), ("pool_scale", 4)):
    C1[_n] = _at
    _at += _w
W1C = _at
C2 = {}
_at = 0
for _n, _w in (("g_mix_pre", 8), ("b_alpha", 8), ("g_gla", 2), ("g_q", 1), ("g_k", 1), ("g_mix_post", 8),
               ("g_ffn_pre", 8), ("g_ffn_post", 8), ("g_ple_post", 8)):
    C2[_n] = _at
    _at += _w
W2C = _at
NCOL = 2 * W1C + 8 + 2 * W2C

K_ID, K_ONES, K_HEADS, K_ROT, K_STRICT, K_INCL, K_INCLREV, K_LEVEL = 0, 1, 2, 3, 4, 5, 6, 7
NK = K_LEVEL + len(LEVELS)

M_R, M_K, M_V, M_WA, M_GL, M_GLV, M_POOL, M_GA, M_GB = 0, 4, 8, 12, 13, 14, 15, 19, 27
N_GQ, N_GK, N_GV, N_GG, N_RA, N_AQ, N_AK, N_AV, N_GA, N_GB = 0, 4, 8, 16, 24, 25, 33, 35, 37, 45


class Signals:

    def __init__(self, nc, ctx, known):
        self.nc, self.ctx, self.known = nc, ctx, known
        self.sems, self.count, self.at = {}, {}, {}

    def sem(self, name):
        if name not in self.sems:
            self.sems[name] = self.ctx.enter_context(self.nc.semaphore(name))
            self.count[name] = 0
        return self.sems[name]

    def passed(self, name, key=None, by=1):
        self.sem(name)
        self.count[name] += by
        if key is not None:
            self.at[(name, key)] = self.count[name]
        return self.count[name]

    def value(self, name, key):
        return self.known[(name, key)] if self.known else 1


def emit(nc, known, wstream, xT, cT, cols, consts, rope, inv_count, small, out):
    with ExitStack() as ctx:
        sig = Signals(nc, ctx, known)
        psum = [ctx.enter_context(nc.psum_tensor(f"psum{i}", [P, 512], F32)) for i in range(8)]
        place = [nc.sbuf_base + (-nc.sbuf_base) % 64]

        def fixed(name, shape, dt=F32):
            o = place[0]
            place[0] += (int(np.prod(shape[1:])) * 4 + 31) // 32 * 32
            return nc.alloc_sbuf_tensor_at(name, shape, dt, offset=o)

        x = fixed("x", [P, DT, T])
        in_hi = fixed("in_hi", [P, DT, T], F32R)
        in_lo = fixed("in_lo", [P, DT, T], F32R)
        raw = [fixed(f"raw{i}", [P, SLAB, P]) for i in range(2)]
        w_hi = [fixed(f"w_hi{i}", [P, SLAB, P], F32R) for i in range(2)]
        w_lo = [fixed(f"w_lo{i}", [P, SLAB, P], F32R) for i in range(2)]
        col = fixed("col", [P, NCOL])
        kst = fixed("kst", [P, NK, P])
        inv_cnt = fixed("inv_cnt", [P, 4, 16])
        sml = fixed("sml", [P, 4, 512])
        mod = fixed("mod", [P, 48])
        gsc = fixed("gsc", [P, 16])
        omk = fixed("omk", [P, 8])
        c_act = fixed("c_act", [P, 8])
        gate2 = fixed("gate2", [P, 8])
        eps = fixed("eps", [P, 4])
        order1 = [M_WA, M_GL, M_GLV] + [m + d for m in (M_K, M_R, M_V) for d in range(RT)]
        arena = place[0]

        def ar(name, kb, shape, dt=F32):
            o = arena + int(kb * 1024)
            assert o + int(np.prod(shape[1:])) * 4 <= nc.sbuf_usable_end, name
            return nc.alloc_sbuf_tensor_at(name, shape, dt, offset=o)

        qr = ar("qr", 0, [P, RT, 2, T])
        b_f = ar("b_f", 16, [P, RT, T])
        k_f = ar("k_f", 24, [P, RT, T])
        v_f = ar("v_f", 32, [P, RT, T])
        bonus = ar("bonus", 40, [P, RT, T])
        gl_s = ar("gl_s", 48, [P, 2, T])
        zbuf = [ar(f"zbuf{i}", 52 + 2.5 * i, [P, 640]) for i in range(2)]
        wa = ar("wa", 57, [P, T])
        lcum = ar("lcum", 59, [P, RT, T])
        sgw = ar("sgw", 67, [P, RT, T])
        tmp = ar("tmp", 75, [P, RT, T])
        gate_v = ar("gate_v", 83, [P, RT, T])
        rkk = ar("rkk", 83, [P, RT, T])
        lmid = ar("lmid", 94, [P, RT, NCH])
        sscal = ar("sscal", 94.125, [P, RT, NCH])
        units = ar("units", 52, [P, NH, 4, P])
        mt = [ar(f"mt{g}", 68 + 2 * g, [P, 4, P]) for g in range(2)]
        mi = [ar(f"mi{g}", 72 + 2 * g, [P, 4, P]) for g in range(2)]
        gm = [ar(f"gm{g}", 76 + 2 * g, [P, 4, P]) for g in range(2)]
        bm = [ar(f"bm{g}", 80 + 2 * g, [P, 4, P]) for g in range(2)]
        tok = [ar(f"tok{i}", 84 + 2 * i, [P, T]) for i in range(3)]
        u0 = ar("u0", 76, [P, T])
        u1 = ar("u1", 78, [P, T])
        st = ar("st", 90, [P, RT, P])
        ya_hi = ar("ya_hi", 52, [P, RT, T], F32R)
        ya_lo = ar("ya_lo", 60, [P, RT, T], F32R)
        yr = [ar(f"yr{i}", 80 + 2 * i, [P, T]) for i in range(2)]
        nv = ar("nv", 91, [P, T])
        yt = [ar(f"yt{i}", 68 + 2 * i, [P, T]) for i in range(6)]
        zp = ar("zp", 84, [P, 4, 528])
        zs = [ar(f"zs{i}", 16 + 2.25 * i, [P, 528]) for i in range(2)]
        yb_hi = ar("yb_hi", 16, [P, 4, T], F32R)
        yb_lo = ar("yb_lo", 24, [P, 4, T], F32R)
        mx_lo = ar("mx_lo", 0, [P, DT, T], F32R)
        mx_hi = ar("mx_hi", 68, [P, DT, T], F32R)
        mg = [ar(f"mg{i}", 40 + 2 * i, [P, T]) for i in range(4)]
        ssq = ar("ssq", 86, [P, T])
        sqt = ar("sqt", 88, [P, T])
        rs = ar("rs", 90, [P, T])
        nt = ar("nt", 92, [P, T])
        hid_hi = ar("hid_hi", 0, [P, HALF, T], F32R)
        hid_lo = ar("hid_lo", 40, [P, HALF, T], F32R)
        hs = [ar(f"hs{i}", 64 + 4 * i, [P, 2, T]) for i in range(2)]

        rope_t = ar("rope_t", 0, [P, 2, T])
        go_hi = ar("go_hi", 4, [P, DT, T], F32R)
        go_lo = ar("go_lo", 20, [P, DT, T], F32R)
        ra = ar("ra", 36, [P, T])
        gq = [ar(f"gq{i}", 38 + 2 * i, [P, T]) for i in range(2)]
        gk = [ar(f"gk{i}", 42 + 2 * i, [P, T]) for i in range(2)]
        gv = [ar(f"gv{i}", 46 + 4 * i, [P, NCH, GDV]) for i in range(2)]
        sg = [ar(f"sg{i}", 54 + 4 * i, [P, 2, T]) for i in range(2)]
        la = [ar(f"la{i}", 62 + 2 * i, [P, NCH, P]) for i in range(2)]
        ln = [ar(f"ln{i}", 66 + 2 * i, [P, NCH, P]) for i in range(2)]
        qd = [ar(f"qd{i}", 70 + 4 * i, [P, NCH, P]) for i in range(2)]
        kd = [ar(f"kd{i}", 72 + 4 * i, [P, NCH, P]) for i in range(2)]
        kt_ = [ar(f"kt{i}", 78 + 2 * i, [P, NCH, P]) for i in range(2)]
        sc = ar("sc", 82, [P, NCH, P])
        sc2 = ar("sc2", 92, [P, NCH, P])
        gs = [ar(f"gs{i}", 84 + 3 * i, [P, NCH - 1, GDV]) for i in range(2)]
        osq = ar("osq", 78, [P, 2, T])
        rsg = ar("rsg", 82, [P, T])
        ot = ar("ot", 90, [P, T])
        mid = [ar(f"mid{i}", 94 + i / 16, [P, NCH]) for i in range(2)]
        dsc = [ar(f"dsc{i}", 94.25 + i / 16, [P, NCH]) for i in range(2)]
        ma = ar("ma", 36, [P, DT, T])
        ao_hi = ar("ao_hi", 4, [P, DT, T], F32R)
        ao_lo = ar("ao_lo", 20, [P, DT, T], F32R)
        ak = ar("ak", 52, [P, KVH, T])
        av = ar("av", 56, [P, NCH, KVH * P])
        aq = [ar(f"aq{i}", 60 + 2 * i, [P, T]) for i in range(2)]
        pr = ar("pr", 64, [P, NCH, T])
        prt = ar("prt", 72, [P, NCH, T])
        qraw = ar("qraw", 80, [P, T])
        asq = ar("asq", 82, [P, T])
        ars = ar("ars", 84, [P, T])
        qn = ar("qn", 86, [P, T])
        qt_ = ar("qt", 88, [P, T])
        stat = ar("stat", 90, [P, 3, NCH])
        m2_hi = ar("m2_hi", 52, [P, DT, T], F32R)
        m2_lo = ar("m2_lo", 68, [P, DT, T], F32R)
        mgs = [ar(f"mgs{i}", 84 + 2 * i, [P, T]) for i in range(2)]
        yy = ar("yy", 4, [P, DT, T])
        h2_hi = ar("h2_hi", 36, [P, HALF, T], F32R)
        h2_lo = ar("h2_lo", 58, [P, HALF, T], F32R)
        hs2 = [ar(f"hs2{i}", 80 + 4 * i, [P, 2, T]) for i in range(2)]
        mgt = ar("mgt", 88, [P, T])
        mg2 = [ar(f"mg2{i}", 80 + 2 * i, [P, T]) for i in range(2)]
        pp_hi = ar("pp_hi", 20, [P, 2, T], F32R)
        pp_lo = ar("pp_lo", 24, [P, 2, T], F32R)

        slabs = []
        slab_end = {}
        jobs = {}
        used = {"lin": 0, "aux": 0}
        BANKS = {"lin": (0, 4), "aux": (4, 4)}
        cursor = {"slab": None, "at": SLAB}
        split_no = {}

        sem, count, passed = sig.sem, sig.value, sig.passed

        def done(job):
            pool, n, _, _ = jobs[job]
            return sem(f"{pool}_done"), n + 1

        def bank_of(job):
            return psum[jobs[job][2]]

        def bank_read(job):
            return sem(f"bank{jobs[job][2]}_read")

        def turn(job):
            return jobs[job][3] + 1

        def moved(job):
            return bank_read(job), turn(job)

        block = ctx.enter_context(nc.Block())

        @block.tensor
        def _(pe):
            seen = set()

            def begin(name, pool):
                n = used[pool]
                first, banks = BANKS[pool]
                b, uses = first + n % banks, n // banks
                if uses:
                    pe.wait_ge(sem(f"bank{b}_read"), uses)
                else:
                    sem(f"bank{b}_read")
                used[pool] += 1
                jobs[name] = (pool, n, b, uses)
                return psum[b]

            def done_sem(name):
                return sem(f"{jobs[name][0]}_done")

            def close(name):
                for s in touched:
                    slab_end[s] = done(name)
                touched.clear()

            touched = set()

            def next_block(desc):
                if cursor["at"] == SLAB:
                    slabs.append(["split", []])
                    cursor["slab"], cursor["at"] = len(slabs) - 1, 0
                    split_no[cursor["slab"]] = len(split_no)
                    pe.wait_ge(sem("slab_split"), len(split_no))
                s, i = cursor["slab"], cursor["at"]
                slabs[s][1].append(desc)
                cursor["at"] += 1
                touched.add(s)
                j = split_no[s] % 2
                return w_hi[j][:, i, :], w_lo[j][:, i, :]

            def linear(name, blocks, hi, lo, ready):
                bank = begin(name, "lin")
                for i, desc in enumerate(blocks):
                    wh, wl = next_block(desc)
                    step = ready(i)
                    if step not in seen:
                        seen.add(step)
                        pe.wait_ge(sem(step[0]), count(*step))
                    pe.matmul(bank[:], wh, hi[:, i, :], start=(i == 0), stop=False)
                    pe.matmul(bank[:], wh, lo[:, i, :], start=False, stop=False)
                    ins = pe.matmul(bank[:], wl, hi[:, i, :], start=False, stop=(i == len(blocks) - 1))
                ins.then_inc(done_sem(name), 1)
                close(name)

            def projection(name, matrix, l, m, ready, kt=DT, hi=in_hi, lo=in_lo, k0=0):
                linear(name, [(matrix, l, k0 + k, m) for k in range(kt)], hi, lo, ready)

            def ada(l, m0):
                slabs.append(["raw", [("ada_w", l, k, m) for m in (m0, m0 + 1) for k in range(DT)]])
                s = len(slabs) - 1
                name = ("ada", l, m0)
                bank = begin(name, "lin")
                pe.wait_ge(sem(f"slab_in{s % 2}"), count(f"slab_in{s % 2}", s))
                pe.wait_ge(sem("c_ready"), count("c_ready", 0))
                for j in range(2):
                    for k in range(DT):
                        ins = pe.matmul(bank[:, j:j + 1], raw[s % 2][:, DT * j + k, :], c_act[:, k:k + 1],
                                        start=(k == 0), stop=(k == DT - 1))
                touched.add(s)
                ins.then_inc(done_sem(name), 1)
                close(name)

            def ones_sum(name, src, which, ready=None):
                bank = begin(name, "aux")
                if ready:
                    pe.wait_ge(sem(ready[0]), count(*ready))
                pe.matmul(bank[:], kst[:, which, :], src, start=True, stop=True).then_inc(done_sem(name), 1)
                close(name)

            def norm_sum(key):
                ones_sum(("norm", key), ssq[:], K_ONES, ("ssq_ready", key))

            def wkv_chunk(l, c):
                cs = slice(c * P, (c + 1) * P)
                for i, src in enumerate((b_f, k_f, v_f)):
                    name = ("tok", l, c, i)
                    bank = begin(name, "aux")
                    pe.wait_ge(sem("wkv_in"), count("wkv_in", l))
                    for d in range(RT):
                        ins = pe.transpose(bank[:, d * P:(d + 1) * P], src[:, d, cs], kst[:, K_ID, :])
                    ins.then_inc(done_sem(name), 1)
                    close(name)
                for h in range(NH):
                    name = ("score", l, c, h)
                    d, rows = h // 2, slice(64 * (h % 2), 64 * (h % 2) + 64)
                    bank = begin(name, "aux")
                    rhs = qr[rows, d, :, cs]
                    pe.matmul(bank[:, 0:256].rearrange("p (a t) -> p a t", a=2), b_f[rows, d, cs], rhs,
                              start=True, stop=True)
                    pe.matmul(bank[:, 256:512].rearrange("p (a t) -> p a t", a=2),
                                        k_f[rows, d, cs], rhs, start=True, stop=True).then_inc(done_sem(name), 1)
                    close(name)
                for g in range(2):
                    name = ("inv_t", l, c, g)
                    bank = begin(name, "aux")
                    pe.wait_ge(sem("mt_ready"), count("mt_ready", (l, c, g)))
                    for j in range(4):
                        ins = pe.transpose(bank[:, j * P:(j + 1) * P], mt[g][:, j, :], kst[:, K_ID, :])
                    ins.then_inc(done_sem(name), 1)
                    close(name)
                for v in range(1, len(LEVELS)):
                    last = v == len(LEVELS) - 1
                    for g in range(2):
                        name = ("am", l, c, g, v)
                        bank = begin(name, "aux")
                        pe.wait_ge(sem("bm_ready"), count("bm_ready", (l, c, g, v)))
                        pe.wait_ge(*moved(("mam", l, c, g, v - 1) if v > 1 else ("inv_t", l, c, g)))
                        for j in range(4):
                            ins = pe.matmul(bank[:, j * P:(j + 1) * P], bm[g][:, j, :], mi[g][:, j, :],
                                            start=True, stop=True)
                        ins.then_inc(done_sem(name), 1)
                        close(name)
                    for g in range(2):
                        pe.wait_ge(*moved(("am", l, c, g, v)))
                        if v > 1:
                            pe.wait_ge(*moved(("mamt", l, c, g, v - 1)))
                        if not last:
                            name = ("mam", l, c, g, v)
                            bank = begin(name, "aux")
                            for j in range(4):
                                ins = pe.matmul(bank[:, j * P:(j + 1) * P], mt[g][:, j, :], gm[g][:, j, :],
                                                start=True, stop=True)
                            ins.then_inc(done_sem(name), 1)
                            close(name)
                        name = ("mamt", l, c, g, v)
                        bank = begin(name, "aux")
                        for j in range(4):
                            ins = pe.matmul(bank[:, j * P:(j + 1) * P], gm[g][:, j, :], mt[g][:, j, :],
                                            start=True, stop=True)
                        ins.then_inc(done_sem(name), 1)
                        close(name)
                name = ("w0", l, c)
                bank = begin(name, "aux")
                pe.wait_ge(*moved(("tok", l, c, 2)))
                if c:
                    pe.wait_ge(sem("state_ready"), count("state_ready", (l, c)))
                for h in range(NH):
                    d, hc = h // 2, slice(64 * h, 64 * h + 64)
                    if c and h % 2 == 0:
                        pe.matmul(bank[:, d * P:(d + 1) * P], qr[:, d, 0, cs], st[:, d, :], start=True, stop=False)
                    ins = pe.matmul(bank[:, hc], units[:, h, 2, :], tok[2][:, hc], start=(c == 0),
                                    stop=(c == 0 or h % 2 == 1))
                ins.then_inc(done_sem(name), 1)
                close(name)
                name = ("u", l, c)
                bank = begin(name, "aux")
                pe.wait_ge(*moved(("w0", l, c)))
                for g in range(2):
                    pe.wait_ge(*moved(("mamt", l, c, g, len(LEVELS) - 1)))
                for h in range(NH):
                    hc = slice(64 * h, 64 * h + 64)
                    ins = pe.matmul(bank[:, hc], mt[h // 4][:, h % 4, :], u0[:, hc], start=True, stop=True)
                ins.then_inc(done_sem(name), 1)
                close(name)
                pe.wait_ge(*moved(("u", l, c)))
                if c < NCH - 1:
                    name = ("state", l, c)
                    bank = begin(name, "aux")
                    for h in range(NH):
                        d, rows, hc = h // 2, slice(64 * (h % 2), 64 * (h % 2) + 64), slice(64 * h, 64 * h + 64)
                        o = bank[rows, d * 64:d * 64 + 64]
                        pe.matmul(o, tok[0][:, hc], u1[:, hc], start=True, stop=False)
                        ins = pe.matmul(o, tok[1][:, hc], tok[2][:, hc], start=False, stop=True)
                    ins.then_inc(done_sem(name), 1)
                    close(name)
                name = ("y", l, c)
                bank = begin(name, "aux")
                for h in range(NH):
                    d, rows, hc = h // 2, slice(64 * (h % 2), 64 * (h % 2) + 64), slice(64 * h, 64 * h + 64)
                    o = bank[rows, d * P:(d + 1) * P]
                    if c and h % 2 == 0:
                        pe.matmul(bank[:, d * P:(d + 1) * P], st[:, d, :], qr[:, d, 1, cs], start=True, stop=False)
                    pe.matmul(o, u1[:, hc], units[:, h, 1, :], start=(c == 0), stop=False)
                    ins = pe.matmul(o, tok[2][:, hc], units[:, h, 3, :], start=False, stop=True)
                ins.then_inc(done_sem(name), 1)
                close(name)

            def block1(l):
                h_in = lambda i: ("split_ready", ("n1", l, i))
                if l == 0:
                    for m in range(0, 48, 2):
                        ada(0, m)
                norm_sum(("n1", l))
                projection(("p", l, M_WA), "w_in", l, M_WA, h_in)
                projection(("p", l, M_GL), "w_in", l, M_GL, h_in)
                projection(("p", l, M_GLV), "w_in", l, M_GLV, h_in)
                pe.wait_ge(sem("small_in"), count("small_in", ("b1", l)))
                for d in range(RT):
                    for name, rows, ready in ((("zw", l, d), slice(0, 64), ("tanh_ready", l)),
                                              (("za", l, d), slice(64, 128), ("ps_ready", (l, M_WA)))):
                        bank = begin(name, "aux")
                        pe.wait_ge(sem(ready[0]), count(*ready))
                        pe.matmul(bank[:], sml[rows, 0, d * P:(d + 1) * P], wa[rows, :],
                                            start=True, stop=True).then_inc(done_sem(name), 1)
                        close(name)
                    if l:
                        name = ("zv", l, d)
                        bank = begin(name, "aux")
                        pe.wait_ge(sem("ps_ready"), count("ps_ready", (l, M_GLV)))
                        pe.matmul(bank[:], sml[32:64, 2, d * P:(d + 1) * P], gl_s[32:64, 1, :],
                                            start=True, stop=True).then_inc(done_sem(name), 1)
                        close(name)
                for m in range(M_K, M_K + RT):
                    projection(("p", l, m), "w_in", l, m, h_in)
                for d in range(RT):
                    projection(("p", l, M_R + d), "w_in", l, M_R + d, h_in)
                    ones_sum(("kk", l, d), tmp[:, d, :], K_HEADS, ("kksq_ready", (l, d)))
                for d in range(RT):
                    projection(("p", l, M_V + d), "w_in", l, M_V + d, h_in)
                    ones_sum(("rk", l, d), rkk[:, d, :], K_HEADS, ("rk_ready", (l, d)))
                for c in range(NCH):
                    wkv_chunk(l, c)
                for d in range(4):
                    projection(("p", l, M_POOL + d), "w_in", l, M_POOL + d, h_in)
                for d in range(RT):
                    pe.wait_ge(*moved(("y", l, NCH - 1)))
                    ones_sum(("mean", l, d), qr[:, d, 1, :], K_HEADS)
                    ones_sum(("var", l, d), yt[d % 2][:], K_HEADS, ("var_ready", (l, d)))
                    name = ("g", l, d)
                    bank = begin(name, "aux")
                    pe.wait_ge(sem("sgl_ready"), count("sgl_ready", l))
                    pe.matmul(bank[:], sml[:, 1, d * P:(d + 1) * P], gl_s[:, 0, :], start=True, stop=False)
                    pe.matmul(bank[:], sml[0:32, 2, d * P:(d + 1) * P], gl_s[0:32, 1, :],
                                        start=False, stop=True).then_inc(done_sem(name), 1)
                    close(name)
                for d in range(4):
                    name = ("pool", l, d)
                    bank = begin(name, "aux")
                    pe.wait_ge(sem("pooled_ready"), count("pooled_ready", (l, d)))
                    pe.matmul(bank[:], sml[:, 3, d * P:(d + 1) * P], zp[:, d, 16:528],
                                        start=True, stop=True).then_inc(done_sem(name), 1)
                    close(name)
                for m in range(DT):
                    projection(("ga", l, m), "w_in", l, M_GA + m, h_in)
                    projection(("pa", l, m), "proj_a", l, m, lambda i: ("split_ready", ("ya", l, i)),
                               kt=RT, hi=ya_hi, lo=ya_lo)
                    projection(("gb", l, m), "w_in", l, M_GB + m, h_in)
                    projection(("pb", l, m), "proj_b", l, m, lambda i: ("split_ready", ("yb", l, i)),
                               kt=4, hi=yb_hi, lo=yb_lo)
                for m in range(DT):
                    projection(("wo", l, m), "w_out", l, m, lambda i: ("split_ready", ("mx", l, i)),
                               hi=mx_hi, lo=mx_lo)
                norm_sum(("n2", l))
                h_in = lambda i: ("split_ready", ("n2", l, i))
                for f in range(2):
                    for m in range(HALF):
                        mm = f * HALF + m
                        projection(("fg", l, mm), "w_gu", l, mm, h_in)
                        projection(("fu", l, mm), "w_gu", l, HT + mm, h_in)
                        if l == 0:
                            ada(1, 2 * mm)
                            if mm >= HT - 2:
                                ada(1, 2 * mm + 4)
                    for m in range(DT):
                        projection(("fd", l, f, m), "w_down", l, m,
                                   lambda i: ("split_ready", ("hid", l, f, i)),
                                   kt=HALF, hi=hid_hi, lo=hid_lo, k0=f * HALF)

            for l in range(DEPTH):
                block1(l)
            norm_sum(("nf", 0))

            def token_major(name, l, matrix, m0):
                cursor["at"] = SLAB
                parts = [[next_block((matrix, l, k, m0 + j)) for j in range(2)] for k in range(DT)]
                s, j = cursor["slab"], split_no[cursor["slab"]] % 2
                for t in range(NCH):
                    ts_ = slice(t * P, (t + 1) * P)
                    bank = begin(name + (t,), "lin")
                    for k in range(DT):
                        wh, wl = w_hi[j][:, 2 * k:2 * k + 2, :], w_lo[j][:, 2 * k:2 * k + 2, :]
                        o = bank[:, 0:256].rearrange("p (a c) -> p a c", a=2)
                        pe.matmul(o, in_hi[:, k, ts_], wh, start=(k == 0), stop=False)
                        pe.matmul(o, in_hi[:, k, ts_], wl, start=False, stop=False)
                        ins = pe.matmul(o, in_lo[:, k, ts_], wh, start=False, stop=(k == DT - 1))
                    touched.add(s)
                    ins.then_inc(done_sem(name + (t,)), 1)
                    close(name + (t,))

            def gla_in(l, h, h_in):
                projection(("gq", l, h), "w_in2", l, N_GQ + h, h_in)
                projection(("gk", l, h), "w_in2", l, N_GK + h, h_in)
                token_major(("gv", l, h), l, "w_in2", N_GV + 2 * h)
                for j in range(2):
                    projection(("gg", l, h, j), "w_in2", l, N_GG + 2 * h + j, h_in)

            def gla_decay(l, h):
                pe.wait_ge(sem("small_in"), count("small_in", ("b2", l)))
                pe.wait_ge(*moved(("ra", l)))
                for i in range(2):
                    name = ("gz", l, h, i)
                    bank = begin(name, "aux")
                    rows = slice(32 * i, 32 * i + 16)
                    ins = pe.matmul(bank[:], sml[rows, 0, h * P:(h + 1) * P], ra[rows, :], start=True, stop=True)
                    ins.then_inc(done_sem(name), 1)
                    close(name)

            def gla_core(l, h):
                v = gv[h % 2]
                pe.wait_ge(sem("qd_ready"), count("qd_ready", (l, h)))
                for i in range(2):
                    name = ("gkt", l, h, i)
                    bank = begin(name, "aux")
                    for c in range(NCH):
                        ins = pe.transpose(bank[:, c * P:(c + 1) * P], kd[i][:, c, :], kst[:, K_ID, :])
                    ins.then_inc(done_sem(name), 1)
                    close(name)
                for i in range(2):
                    name = ("gsc", l, h, i)
                    bank = begin(name, "aux")
                    for c in range(NCH):
                        ins = pe.matmul(bank[:, c * P:(c + 1) * P], kd[i][:, c, :], qd[i][:, c, :],
                                        start=True, stop=True)
                    ins.then_inc(done_sem(name), 1)
                    close(name)
                pe.wait_ge(*moved(("gkt", l, h, 1)))
                pe.wait_ge(*moved(("gv", l, h, NCH - 1)))
                for n in range(NCH - 1):
                    name = ("gst", l, h, n)
                    bank = begin(name, "aux")
                    pe.matmul(bank[:, 0:GDV], kt_[0][:, n, :], v[:, n, :], start=True, stop=True)
                    c = NCH - 1 - n
                    ins = pe.matmul(bank[:, GDV:2 * GDV], kt_[1][:, c, :], v[:, c, :], start=True, stop=True)
                    ins.then_inc(done_sem(name), 1)
                    close(name)
                pe.wait_ge(sem("sc_ready"), count("sc_ready", (l, h)))
                for j in range(2):
                    name = ("go", l, h, j)
                    vs = slice(j * P, (j + 1) * P)
                    bank = begin(name, "aux")
                    pe.wait_ge(sem("gs_ready"), count("gs_ready", (l, h)))
                    for c in range(NCH):
                        o = bank[:, c * P:(c + 1) * P]
                        pe.matmul(o, v[:, c, vs], sc[:, c, :], start=True, stop=False)
                        if c:
                            ins = pe.matmul(o, gs[0][:, c - 1, vs], qd[0][:, c, :], start=False, stop=(c == NCH - 1))
                        if c < NCH - 1:
                            ins = pe.matmul(o, gs[1][:, NCH - 2 - c, vs], qd[1][:, c, :], start=False, stop=True)
                    ins.then_inc(done_sem(name), 1)
                    close(name)
                name = ("gn", l, h)
                bank = begin(name, "aux")
                pe.wait_ge(sem("osq_ready"), count("osq_ready", (l, h)))
                pe.matmul(bank[:], kst[:, K_ONES, :], osq[:, 0, :], start=True, stop=False)
                ins = pe.matmul(bank[:], kst[:, K_ONES, :], osq[:, 1, :], start=False, stop=True)
                ins.then_inc(done_sem(name), 1)
                close(name)

            def rope_sum(key):
                ones_sum(("qs",) + key, asq[:], K_ONES, ("asq_ready", key))

            def rope_turn(key):
                name = ("rot",) + key
                bank = begin(name, "aux")
                pe.wait_ge(sem("qn_ready"), count("qn_ready", key))
                pe.matmul(bank[:], kst[:, K_ROT, :], qn[:], start=True, stop=True).then_inc(done_sem(name), 1)
                close(name)

            def block2(l):
                h_in = lambda i: ("split_ready", ("m1", l, i))
                norm_sum(("m1", l))
                projection(("ra", l), "w_in2", l, N_RA, h_in)
                gla_in(l, 0, h_in)
                gla_decay(l, 0)
                for h in range(GH):
                    if h + 1 < GH:
                        gla_in(l, h + 1, h_in)
                    gla_core(l, h)
                    if h + 1 < GH:
                        gla_decay(l, h + 1)
                for m in range(DT):
                    projection(("g2a", l, m), "w_in2", l, N_GA + m, h_in)
                    projection(("p2a", l, m), "w_o_gla", l, m, lambda i: ("split_ready", ("go", l, i)),
                               hi=go_hi, lo=go_lo)
                for i in range(KVH):
                    projection(("k", l, i), "w_in2", l, N_AK + i, h_in)
                    rope_sum(("k", l, i))
                    rope_turn(("k", l, i))
                token_major(("av", l), l, "w_in2", N_AV)
                projection(("q", l, 0), "w_in2", l, N_AQ, h_in)
                rope_sum(("q", l, 0))
                rope_turn(("q", l, 0))
                for h in range(QH):
                    kv = h // (QH // KVH)
                    for t in range(NCH):
                        name = ("as", l, h, t)
                        bank = begin(name, "aux")
                        pe.wait_ge(sem("rope_ready"), count("rope_ready", ("q", l, h)))
                        pe.matmul(bank[:], aq[h % 2][:, t * P:(t + 1) * P], ak[:, kv, :],
                                            start=True, stop=True).then_inc(done_sem(name), 1)
                        close(name)
                    if h + 1 < QH:
                        projection(("q", l, h + 1), "w_in2", l, N_AQ + h + 1, h_in)
                        rope_sum(("q", l, h + 1))
                    for t in range(NCH):
                        name = ("pt", l, h, t)
                        bank = begin(name, "aux")
                        pe.wait_ge(sem("pr_ready"), count("pr_ready", (l, h, t)))
                        for k in range(NCH):
                            ins = pe.transpose(bank[:, k * P:(k + 1) * P], pr[:, t, k * P:(k + 1) * P],
                                               kst[:, K_ID, :])
                        ins.then_inc(done_sem(name), 1)
                        close(name)
                    if h + 1 < QH:
                        rope_turn(("q", l, h + 1))
                    name = ("pv", l, h)
                    bank = begin(name, "aux")
                    pe.wait_ge(*moved(("pt", l, h, NCH - 1)))
                    pe.wait_ge(*moved(("av", l, NCH - 1)))
                    for k in range(NCH):
                        ins = pe.matmul(bank[:], av[:, k, kv * P:(kv + 1) * P], prt[:, k, :],
                                        start=(k == 0), stop=(k == NCH - 1))
                    ins.then_inc(done_sem(name), 1)
                    close(name)
                for m in range(DT):
                    projection(("g2b", l, m), "w_in2", l, N_GB + m, h_in)
                    projection(("p2b", l, m), "w_o_attn", l, m, lambda i: ("split_ready", ("ao", l, i)),
                               hi=ao_hi, lo=ao_lo)
                for m in range(DT):
                    projection(("wo2", l, m), "w_out2", l, m, lambda i: ("split_ready", ("m2", l, i)),
                               hi=m2_hi, lo=m2_lo)
                norm_sum(("m2", l))
                norm_sum(("m3", l))
                h_in3 = lambda i: ("split_ready", ("m3", l, i))
                for f in range(2):
                    for m in range(HALF):
                        mm = f * HALF + m
                        projection(("eg", l, mm), "w_ffn_in", l, mm, h_in3)
                        projection(("eu", l, mm), "w_ffn_in", l, HT + mm, h_in3)
                    for m in range(DT):
                        projection(("ed", l, f, m), "w_ffn_out", l, m,
                                   lambda i: ("split_ready", ("h2", l, f, i)),
                                   kt=HALF, hi=h2_hi, lo=h2_lo, k0=f * HALF)
                norm_sum(("m4", l))
                for m in range(DT):
                    projection(("pe", l, m), "w_ple_proj", l, m, lambda i: ("split_ready", ("pp", l, i)),
                               kt=2, hi=pp_hi, lo=pp_lo)
                    projection(("pg", l, m), "w_ple_gate", l, m, lambda i: ("split_ready", ("pl", l, i)))
                norm_sum(("m5", l))

            for l in range(DEPTH):
                block2(l)

        @block.scalar
        def _(act):
            af = act.activation
            def load_small(l, which):
                act.dma_start(sml[:], small[l + 2 * which]).then_inc(sem("small_in"), 16)
                passed("small_in", (("b1", "b2")[which], l), by=16)

            act.dma_start(col[:], cols).then_inc(sem("const_in"), 16)
            act.dma_start(kst[:], consts).then_inc(sem("const_in"), 16)
            act.dma_start(inv_cnt[:], inv_count).then_inc(sem("const_in"), 16)
            act.dma_start(c_act[:], cT).then_inc(sem("const_in"), 16)
            act.dma_start(x[:], xT).then_inc(sem("x_in"), 16)
            act.wait_ge(sem("const_in"), 64)
            af(c_act[:], c_act[:], ACT.Silu).then_inc(sem("c_ready"), 1)
            act.wait_ge(sem("c_ready"), passed("c_ready", 0))
            load_small(0, 0)
            act.wait_ge(sem("eps_ready"), count("eps_ready", 0))

            def col1(l, name, i):
                o = l * W1C + C1[name] + i
                return col[:, o:o + 1]

            def col2(l, name, i):
                o = 2 * W1C + 8 + l * W2C + C2[name] + i
                return col[:, o:o + 1]

            def root(job, dst, scale, e):
                act.wait_ge(*done(job))
                af(dst, bank_of(job)[:], ACT.Sqrt, bias=eps[:, e:e + 1], scale=scale).then_inc(bank_read(job), 1)
                act.wait_ge(bank_read(job), turn(job))

            def evac_shift(l, m, n):
                if n >= 2:
                    act.wait_ge(sem("ps_ready"), count("ps_ready", (l, order1[n - 2])))
                job = ("p", l, m)
                act.wait_ge(*done(job))
                af(zbuf[n % 2][:, 128:640], bank_of(job)[:], ACT.Copy).then_inc(bank_read(job), 1)
                act.wait_ge(bank_read(job), turn(job))

            def block1(l):
                root(("norm", ("n1", l)), rs[:], 1.0 / D, 0)
                for n in range(3):
                    act.wait_ge(sem("zpad_ready"), count("zpad_ready", l))
                    evac_shift(l, order1[n], n)
                act.wait_ge(sem("ps_ready"), count("ps_ready", (l, M_WA)))
                af(wa[0:64, :], wa[0:64, :], ACT.Tanh).then_inc(sem("tanh_ready"), 1)
                act.wait_ge(sem("tanh_ready"), passed("tanh_ready", l))
                for d in range(RT):
                    job = ("zw", l, d)
                    act.wait_ge(*done(job))
                    af(sgw[:, d, :], bank_of(job)[:], ACT.Sigmoid, bias=col1(l, "w0", d)).then_inc(bank_read(job), 1)
                    act.wait_ge(bank_read(job), turn(job))
                    job = ("za", l, d)
                    act.wait_ge(*done(job))
                    af(b_f[:, d, :], bank_of(job)[:], ACT.Sigmoid, bias=col1(l, "a0", d)).then_inc(bank_read(job), 1)
                    act.wait_ge(bank_read(job), turn(job))
                    if l:
                        job = ("zv", l, d)
                        act.wait_ge(*done(job))
                        ins = af(gate_v[:, d, :], bank_of(job)[:], ACT.Sigmoid, bias=col1(l, "v0", d))
                        ins.then_inc(bank_read(job), 1)
                        act.wait_ge(bank_read(job), turn(job))
                act.wait_ge(sem("ps_ready"), count("ps_ready", (l, M_GLV)))
                af(gl_s[:, 0, :], gl_s[:, 0, :], ACT.Sigmoid).then_inc(sem("scalar_step"), 1)
                act.wait_ge(sem("scalar_step"), passed("scalar_step"))
                af(gl_s[0:32, 1, :], gl_s[0:32, 1, :], ACT.Sigmoid).then_inc(sem("sgl_ready"), 1)
                act.wait_ge(sem("sgl_ready"), passed("sgl_ready", l))
                for n in range(3, 7):
                    evac_shift(l, order1[n], n)
                for d in range(RT):
                    evac_shift(l, order1[7 + d], 7 + d)
                    root(("kk", l, d), tmp[:, d, :], 1.0, 3)
                for d in range(RT):
                    evac_shift(l, order1[11 + d], 11 + d)
                act.wait_ge(sem("lcum_ready"), count("lcum_ready", l))
                af(sscal[:], sscal[:], ACT.Exp, scale=-EXP_MHALF).then_inc(sem("scalar_step"), 1)
                act.wait_ge(sem("scalar_step"), passed("scalar_step"))
                af(sgw[:], sgw[:], ACT.Exp, scale=-EXP_MHALF).then_inc(sem("scalar_step"), 1)
                act.wait_ge(sem("scalar_step"), passed("scalar_step"))
                af(tmp[:], lcum[:], ACT.Exp, scale=-EXP_MHALF).then_inc(sem("scalar_step"), 1)
                act.wait_ge(sem("scalar_step"), passed("scalar_step"))
                af(lcum[:], lcum[:], ACT.Exp, scale=EXP_MHALF).then_inc(sem("decay_ready"), 1)
                act.wait_ge(sem("decay_ready"), passed("decay_ready", l))
                for c in range(NCH):
                    for i in range(3):
                        job = ("tok", l, c, i)
                        act.wait_ge(*done(job))
                        bank = bank_of(job)
                        if i == 0 and c == 0:
                            act.wait_ge(sem("wkv_in"), count("wkv_in", l))
                        af(tok[i][:], bank[:], ACT.Copy).then_inc(bank_read(job), 1)
                        act.wait_ge(bank_read(job), turn(job))
                    for g in range(2):
                        job = ("inv_t", l, c, g)
                        act.wait_ge(*done(job))
                        af(mi[g][:], bank_of(job)[:], ACT.Copy).then_inc(bank_read(job), 1)
                        act.wait_ge(bank_read(job), turn(job))
                    for v in range(1, len(LEVELS)):
                        for g in range(2):
                            job = ("am", l, c, g, v)
                            act.wait_ge(*done(job))
                            af(gm[g][:], bank_of(job)[:], ACT.Copy).then_inc(bank_read(job), 1)
                            act.wait_ge(bank_read(job), turn(job))
                    job = ("w0", l, c)
                    act.wait_ge(*done(job))
                    bank = bank_of(job)
                    af(u0[:], bank[:], ACT.Copy).then_inc(bank_read(job), 1)
                    act.wait_ge(bank_read(job), turn(job))
                    job = ("u", l, c)
                    act.wait_ge(*done(job))
                    af(u1[:], bank_of(job)[:], ACT.Copy, scale=-1.0).then_inc(bank_read(job), 1)
                    act.wait_ge(bank_read(job), turn(job))
                    job = ("y", l, c)
                    act.wait_ge(*done(job))
                    bank = bank_of(job)
                    ins = af(qr[:, :, 1, c * P:(c + 1) * P], bank[:].rearrange("p (d t) -> p d t", d=RT), ACT.Copy)
                    ins.then_inc(bank_read(job), 1)
                    act.wait_ge(bank_read(job), turn(job))
                for d in range(4):
                    job = ("p", l, M_POOL + d)
                    act.wait_ge(*done(job))
                    af(yt[2 + d][:], bank_of(job)[:], ACT.Copy).then_inc(bank_read(job), 1)
                    act.wait_ge(bank_read(job), turn(job))
                for d in range(RT):
                    root(("var", l, d), yr[d % 2][:], 1.0 / HEAD, 1)
                for d in range(4):
                    job = ("pool", l, d)
                    act.wait_ge(sem("split_ready"), count("split_ready", ("ya", l, RT - 1)))
                    if d >= 2:
                        act.wait_ge(sem("split_ready"), count("split_ready", ("yb", l, d - 2)))
                    act.wait_ge(*done(job))
                    ins = af(mg[d % 2][:], bank_of(job)[:], ACT.Copy, scale=col1(l, "pool_scale", d))
                    ins.then_inc(bank_read(job), 1)
                    act.wait_ge(bank_read(job), turn(job))
                load_small(*((1, 0) if l == 0 else (0, 1)))
                for m in range(DT):
                    if m:
                        act.wait_ge(sem("split_ready"), count("split_ready", ("mx", l, m - 1)))
                    else:
                        act.wait_ge(sem("split_ready"), count("split_ready", ("yb", l, 3)))
                    for i, n in enumerate(("ga", "gb")):
                        job = (n, l, m)
                        act.wait_ge(*done(job))
                        af(mg[i][:], bank_of(job)[:], ACT.Sigmoid).then_inc(bank_read(job), 1)
                        act.wait_ge(bank_read(job), turn(job))
                root(("norm", ("n2", l)), rs[:], 1.0 / D, 0)
                ffn(l, "f", "hid")

            def ffn(l, tag, hid):
                for f in range(2):
                    for m in range(HALF):
                        mm = f * HALF + m
                        job = (tag + "g", l, mm)
                        if mm >= 2:
                            act.wait_ge(sem("split_ready"), count("split_ready", (hid, l, (mm - 2) // HALF, (mm - 2) % HALF)))
                        act.wait_ge(*done(job))
                        af(hs[mm % 2][:, 0, :], bank_of(job)[:], ACT.Silu).then_inc(bank_read(job), 1)
                        act.wait_ge(bank_read(job), turn(job))

            for l in range(DEPTH):
                block1(l)
            root(("norm", ("nf", 0)), rs[:], 1.0 / D, 0)
            act.dma_start(rope_t[:], rope).then_inc(sem("rope_in"), 16)

            def gla_in(l, h):
                if h >= 2:
                    act.wait_ge(sem("qd_ready"), count("qd_ready", (l, h - 2)))
                for job, dst in ((("gq", l, h), gq[h % 2]), (("gk", l, h), gk[h % 2])):
                    act.wait_ge(*done(job))
                    af(dst[:], bank_of(job)[:], ACT.Copy).then_inc(bank_read(job), 1)
                    act.wait_ge(bank_read(job), turn(job))
                for t in range(NCH):
                    job = ("gv", l, h, t)
                    act.wait_ge(*done(job))
                    af(gv[h % 2][:, t, :], bank_of(job)[:, 0:GDV], ACT.Copy).then_inc(bank_read(job), 1)
                    act.wait_ge(bank_read(job), turn(job))
                if h >= 2:
                    act.wait_ge(sem("split_ready"), count("split_ready", ("go", l, 2 * (h - 2) + 1)))
                for j in range(2):
                    job = ("gg", l, h, j)
                    act.wait_ge(*done(job))
                    af(sg[h % 2][:, j, :], bank_of(job)[:], ACT.Silu).then_inc(bank_read(job), 1)
                    act.wait_ge(bank_read(job), turn(job))

            def gla_decay(l, h):
                flat = lambda t: t[:].rearrange("p c t -> p (c t)")
                for i in range(2):
                    act.wait_ge(*done(("gz", l, h, i)))
                    ins = af(flat(ln[i]), bank_of(("gz", l, h, i))[:], ACT.Abs, bias=col2(l, "b_alpha", 4 * i + h))
                    ins.then_inc(sem("abs_ready"), 1)
                    act.wait_ge(sem("abs_ready"), passed("abs_ready", (l, h, i)))
                for i in range(2):
                    af(ln[i][:], ln[i][:], ACT.Exp, scale=-1.0).then_inc(sem("scalar_step"), 1)
                    act.wait_ge(sem("scalar_step"), passed("scalar_step"))
                for i in range(2):
                    af(ln[i][:], ln[i][:], ACT.Ln, bias=eps[:, 2:3]).then_inc(sem("log_ready"), 1)
                    act.wait_ge(sem("log_ready"), passed("log_ready", (l, h, i)))

            def gla_core(l, h):
                for i in range(2):
                    s = (1.0, -1.0)[i] / TAU
                    act.wait_ge(sem("cum_ready"), count("cum_ready", (l, h, i)))
                    af(la[i][:], ln[i][:], ACT.Exp, scale=s).then_inc(sem("scalar_step"), 1)
                    act.wait_ge(sem("scalar_step"), passed("scalar_step"))
                    af(ln[i][:], ln[i][:], ACT.Exp, scale=-s).then_inc(sem("scalar_step"), 1)
                    act.wait_ge(sem("scalar_step"), passed("scalar_step"))
                    af(dsc[i][:], dsc[i][:], ACT.Exp, scale=1.0 / TAU).then_inc(sem("ed_ready"), 1)
                    act.wait_ge(sem("ed_ready"), passed("ed_ready", (l, h, i)))
                for i in range(2):
                    job = ("gkt", l, h, i)
                    act.wait_ge(*done(job))
                    af(kt_[i][:].rearrange("p c t -> p (c t)"), bank_of(job)[:], ACT.Copy).then_inc(bank_read(job), 1)
                    act.wait_ge(bank_read(job), turn(job))
                for j in range(2):
                    act.wait_ge(*done(("go", l, h, j)))
                    ins = af(osq[:, j, :], bank_of(("go", l, h, j))[:], ACT.Square)
                    if j:
                        ins.then_inc(sem("osq_ready"), 1)
                        act.wait_ge(sem("osq_ready"), passed("osq_ready", (l, h)))
                    else:
                        ins.then_inc(sem("scalar_step"), 1)
                        act.wait_ge(sem("scalar_step"), passed("scalar_step"))
                root(("gn", l, h), rsg[:], 1.0 / GDV, 0)

            def rope_in(key, n, before):
                if before:
                    act.wait_ge(sem("qn_ready"), count("qn_ready", before))
                act.wait_ge(*done(key))
                af(qraw[:], bank_of(key)[:], ACT.Copy).then_inc(bank_read(key), 1)
                act.wait_ge(bank_read(key), turn(key))
                af(asq[:], qraw[:], ACT.Square).then_inc(sem("asq_ready"), 1)
                act.wait_ge(sem("asq_ready"), passed("asq_ready", key))
                root(("qs",) + key, ars[:], 1.0 / P, 0)

            def block2(l):
                root(("norm", ("m1", l)), rs[:], 1.0 / D, 0)
                job = ("ra", l)
                act.wait_ge(*done(job))
                af(ra[:], bank_of(job)[:], ACT.Copy).then_inc(bank_read(job), 1)
                act.wait_ge(bank_read(job), turn(job))
                gla_in(l, 0)
                gla_decay(l, 0)
                for h in range(GH):
                    if h + 1 < GH:
                        gla_in(l, h + 1)
                    gla_core(l, h)
                    if h + 1 < GH:
                        gla_decay(l, h + 1)
                for m in range(DT):
                    job = ("g2a", l, m)
                    if m >= 2:
                        act.wait_ge(*moved(("p2a", l, m - 2)))
                    else:
                        act.wait_ge(sem("split_ready"), count("split_ready", ("go", l, DT - 1)))
                    act.wait_ge(*done(job))
                    af(mgs[m % 2][:], bank_of(job)[:], ACT.Sigmoid).then_inc(bank_read(job), 1)
                    act.wait_ge(bank_read(job), turn(job))
                act.wait_ge(*moved(("p2a", l, DT - 1)))
                rope_in(("k", l, 0), 0, None)
                rope_in(("k", l, 1), 1, ("k", l, 0))
                for t in range(NCH):
                    job = ("av", l, t)
                    act.wait_ge(*done(job))
                    af(av[:, t, :], bank_of(job)[:, 0:256], ACT.Copy).then_inc(bank_read(job), 1)
                    act.wait_ge(bank_read(job), turn(job))
                rope_in(("q", l, 0), 2, ("k", l, 1))
                for h in range(QH):
                    for t in range(NCH):
                        job = ("as", l, h, t)
                        act.wait_ge(sem("max_ready"), count("max_ready", (l, h, t)))
                        act.wait_ge(*done(job))
                        af(pr[:, t, :], bank_of(job)[:], ACT.Exp, bias=stat[:, 0, t:t + 1],
                                scale=P ** -0.5, accum_out=stat[:, 1, t:t + 1]).then_inc(bank_read(job), 1)
                        act.wait_ge(bank_read(job), turn(job))
                    if h + 1 < QH:
                        rope_in(("q", l, h + 1), 3 + h, ("q", l, h))
                    for t in range(NCH):
                        job = ("pt", l, h, t)
                        act.wait_ge(*done(job))
                        bank = bank_of(job)
                        if h:
                            act.wait_ge(*moved(("pv", l, h - 1)))
                        af(prt[:, :, t * P:(t + 1) * P], bank[:].rearrange("p (k q) -> p k q", k=NCH),
                                ACT.Copy).then_inc(bank_read(job), 1)
                        act.wait_ge(bank_read(job), turn(job))
                for m in range(DT):
                    job = ("g2b", l, m)
                    if m >= 2:
                        act.wait_ge(*moved(("p2b", l, m - 2)))
                    else:
                        act.wait_ge(sem("split_ready"), count("split_ready", ("ao", l, DT - 1)))
                    act.wait_ge(*done(job))
                    af(mgs[m % 2][:], bank_of(job)[:], ACT.Sigmoid).then_inc(bank_read(job), 1)
                    act.wait_ge(bank_read(job), turn(job))
                root(("norm", ("m2", l)), rs[:], 1.0 / D, 0)
                root(("norm", ("m3", l)), rs[:], 1.0 / D, 0)
                for mm in range(HT):
                    job = ("eg", l, mm)
                    if mm >= 2:
                        act.wait_ge(sem("split_ready"), count("split_ready", ("h2", l, (mm - 2) // HALF, (mm - 2) % HALF)))
                    act.wait_ge(*done(job))
                    af(hs2[mm % 2][:, 0, :], bank_of(job)[:], ACT.Silu).then_inc(bank_read(job), 1)
                    act.wait_ge(bank_read(job), turn(job))
                root(("norm", ("m4", l)), rs[:], 1.0 / D, 0)
                for m in range(DT):
                    job = ("pg", l, m)
                    if m >= 2:
                        act.wait_ge(*moved(("pe", l, m - 2)))
                    act.wait_ge(*done(job))
                    af(mg2[m % 2][:], bank_of(job)[:], ACT.Sigmoid).then_inc(bank_read(job), 1)
                    act.wait_ge(bank_read(job), turn(job))
                if l == 0:
                    load_small(1, 1)
                root(("norm", ("m5", l)), rs[:], 1.0 / D, 0)

            for l in range(DEPTH):
                block2(l)

        @block.vector
        def _(dve):
            tt, ts, stt = dve.tensor_tensor, dve.tensor_scalar, dve.scalar_tensor_tensor
            for i, e in enumerate((EPS_RMS, EPS_GN, 1.0, 0.0)):
                ins = dve.memset(eps[:, i:i + 1], e)
                if i == 3:
                    ins.then_inc(sem("eps_ready"), 1)
                    dve.wait_ge(sem("eps_ready"), passed("eps_ready", 0))
                else:
                    ins.then_inc(sem("vector_step"), 1)
                    dve.wait_ge(sem("vector_step"), passed("vector_step"))
            dve.wait_ge(sem("const_in"), 64)

            def col1(l, name, i, n=1):
                o = l * W1C + C1[name] + i
                return col[:, o:o + n]

            def col2(l, name, i, n=1):
                o = 2 * W1C + 8 + l * W2C + C2[name] + i
                return col[:, o:o + n]

            def split(src, hi, lo, key):
                dve.tensor_copy(hi, src).then_inc(sem("vector_step"), 1)
                dve.wait_ge(sem("vector_step"), passed("vector_step"))
                tt(lo, src, hi.bitcast(F32), ALU.subtract).then_inc(sem("split_ready"), 1)
                dve.wait_ge(sem("split_ready"), passed("split_ready", key))

            def square_sum(src, first, key=None):
                if first:
                    tt(ssq[:], src, src, ALU.mult).then_inc(sem("vector_step"), 1)
                    dve.wait_ge(sem("vector_step"), passed("vector_step"))
                else:
                    tt(sqt[:], src, src, ALU.mult).then_inc(sem("vector_step"), 1)
                    dve.wait_ge(sem("vector_step"), passed("vector_step"))
                    ins = tt(ssq[:], ssq[:], sqt[:], ALU.add)
                    if key:
                        ins.then_inc(sem("ssq_ready"), 1)
                        dve.wait_ge(sem("ssq_ready"), passed("ssq_ready", key))
                    else:
                        ins.then_inc(sem("vector_step"), 1)
                        dve.wait_ge(sem("vector_step"), passed("vector_step"))

            def inv_root(job, buf):
                dve.wait_ge(*moved(job))
                dve.reciprocal(buf, buf).then_inc(sem("vector_step"), 1)
                dve.wait_ge(sem("vector_step"), passed("vector_step"))

            def normed_inputs(key, scale_of, shift_of=None):
                inv_root(("norm", key), rs[:])
                for i in range(DT):
                    stt(nt[:], x[:, i, :], scale_of(i), rs[:], ALU.mult, ALU.mult).then_inc(sem("vector_step"), 1)
                    dve.wait_ge(sem("vector_step"), passed("vector_step"))
                    if shift_of:
                        ts(in_hi[:, i, :], nt[:], shift_of(i), None, ALU.add).then_inc(sem("vector_step"), 1)
                        dve.wait_ge(sem("vector_step"), passed("vector_step"))
                        stt(in_lo[:, i, :], nt[:], shift_of(i), in_hi[:, i, :].bitcast(F32), ALU.add,
                               ALU.subtract).then_inc(sem("split_ready"), 1)
                        dve.wait_ge(sem("split_ready"), passed("split_ready", key + (i,)))
                    else:
                        split(nt[:], in_hi[:, i, :], in_lo[:, i, :], key + (i,))

            def ada(l, m):
                job = ("ada", l, m)
                dve.wait_ge(*done(job))
                tt(mod[:, m:m + 2], bank_of(job)[:, 0:2], col1(l, "ada_b", m, 2), ALU.add).then_inc(bank_read(job), 1)
                dve.wait_ge(bank_read(job), turn(job))

            def block1(l):
                if l == 0:
                    for m in range(0, 48, 2):
                        ada(0, m)
                    dve.wait_ge(sem("x_in"), 16)
                    for i in range(DT):
                        square_sum(x[:, i, :], i == 0, ("n1", 0) if i == DT - 1 else None)
                ins = stt(gsc[:, 0:8], mod[:, 8:16], 1.0, col1(l, "norm1_g", 0, 8), ALU.add, ALU.mult)
                ins.then_inc(sem("vector_step"), 1)
                dve.wait_ge(sem("vector_step"), passed("vector_step"))
                ins = stt(gsc[:, 8:16], mod[:, 32:40], 1.0, col1(l, "norm2_g", 0, 8), ALU.add, ALU.mult)
                ins.then_inc(sem("vector_step"), 1)
                dve.wait_ge(sem("vector_step"), passed("vector_step"))
                ts(omk[:, 0:4], col1(l, "k_a", 0, 4), -1.0, 1.0, ALU.mult, ALU.add).then_inc(sem("vector_step"), 1)
                dve.wait_ge(sem("vector_step"), passed("vector_step"))
                ts(omk[:, 4:8], col1(l, "lnx_g", 0, 4), -1.0, None, ALU.mult).then_inc(sem("vector_step"), 1)
                dve.wait_ge(sem("vector_step"), passed("vector_step"))
                for i in range(2):
                    ins = dve.memset(zbuf[i][:, 96:128], 0.0)
                    if i:
                        ins.then_inc(sem("zpad_ready"), 1)
                        dve.wait_ge(sem("zpad_ready"), passed("zpad_ready", l))
                    else:
                        ins.then_inc(sem("vector_step"), 1)
                        dve.wait_ge(sem("vector_step"), passed("vector_step"))
                normed_inputs(("n1", l), lambda i: gsc[:, i:i + 1], lambda i: mod[:, i:i + 1])

                def shift(m, n, dst):
                    dve.wait_ge(*moved(("p", l, m)))
                    z = zbuf[n % 2]
                    tt(dst, z[:, 127:639], z[:, 128:640], ALU.subtract).then_inc(sem("vector_step"), 1)
                    dve.wait_ge(sem("vector_step"), passed("vector_step"))
                    stt(dst, dst, col1(l, "mu", m), z[:, 128:640], ALU.mult, ALU.add).then_inc(sem("ps_ready"), 1)
                    dve.wait_ge(sem("ps_ready"), passed("ps_ready", (l, m)))

                shift(M_WA, 0, wa[:])
                shift(M_GL, 1, gl_s[:, 0, :])
                shift(M_GLV, 2, gl_s[:, 1, :])
                for n in range(RT):
                    shift(M_K + n, 3 + n, k_f[:, n, :])
                for d in range(RT):
                    dve.wait_ge(*moved(("za", l, d)))
                    ins = ts(qr[:, d, 0, :], k_f[:, d, :], col1(l, "k_k", d), None, ALU.mult)
                    ins.then_inc(sem("vector_step"), 1)
                    dve.wait_ge(sem("vector_step"), passed("vector_step"))
                    tt(tmp[:, d, :], qr[:, d, 0, :], qr[:, d, 0, :], ALU.mult).then_inc(sem("kksq_ready"), 1)
                    dve.wait_ge(sem("kksq_ready"), passed("kksq_ready", (l, d)))
                    ins = ts(lcum[:, d, :], b_f[:, d, :], col1(l, "k_a", d), omk[:, d:d + 1], ALU.mult, ALU.add)
                    ins.then_inc(sem("vector_step"), 1)
                    dve.wait_ge(sem("vector_step"), passed("vector_step"))
                    tt(k_f[:, d, :], k_f[:, d, :], lcum[:, d, :], ALU.mult).then_inc(sem("vector_step"), 1)
                    dve.wait_ge(sem("vector_step"), passed("vector_step"))
                for d in range(RT):
                    shift(M_R + d, 7 + d, qr[:, d, 1, :])
                    inv = tmp[:, d, :]
                    dve.wait_ge(*moved(("kk", l, d)))
                    ts(inv, inv, 1e-12, None, ALU.max).then_inc(sem("vector_step"), 1)
                    dve.wait_ge(sem("vector_step"), passed("vector_step"))
                    dve.reciprocal(inv, inv).then_inc(sem("vector_step"), 1)
                    dve.wait_ge(sem("vector_step"), passed("vector_step"))
                    tt(qr[:, d, 0, :], qr[:, d, 0, :], inv, ALU.mult).then_inc(sem("vector_step"), 1)
                    dve.wait_ge(sem("vector_step"), passed("vector_step"))
                    tt(b_f[:, d, :], b_f[:, d, :], qr[:, d, 0, :], ALU.mult).then_inc(sem("vector_step"), 1)
                    dve.wait_ge(sem("vector_step"), passed("vector_step"))
                if l:
                    for d in range(RT):
                        shift(M_V + d, 11 + d, nv[:])
                        tt(v_f[:, d, :], v_f[:, d, :], nv[:], ALU.subtract).then_inc(sem("vector_step"), 1)
                        dve.wait_ge(sem("vector_step"), passed("vector_step"))
                        tt(v_f[:, d, :], v_f[:, d, :], gate_v[:, d, :], ALU.mult).then_inc(sem("vector_step"), 1)
                        dve.wait_ge(sem("vector_step"), passed("vector_step"))
                        tt(v_f[:, d, :], v_f[:, d, :], nv[:], ALU.add).then_inc(sem("vector_step"), 1)
                        dve.wait_ge(sem("vector_step"), passed("vector_step"))
                        bonus_in(l, d)
                else:
                    for d in range(RT):
                        shift(M_V + d, 11 + d, v_f[:, d, :])
                        bonus_in(l, d)
                for d in range(RT):
                    for c in range(NCH):
                        cs = slice(c * P, (c + 1) * P)
                        dve.tensor_tensor_scan(lcum[:, d, cs], kst[:, K_ONES, :], sgw[:, d, cs], 0.0,
                                                  ALU.mult, ALU.add).then_inc(sem("vector_step"), 1)
                        dve.wait_ge(sem("vector_step"), passed("vector_step"))
                lc = lcum[:].rearrange("p d (c t) -> p d c t", c=NCH)
                dve.tensor_copy(lmid[:], lc[:, :, :, 63]).then_inc(sem("vector_step"), 1)
                dve.wait_ge(sem("vector_step"), passed("vector_step"))
                for d in range(RT):
                    lcd = lcum[:, d, :].rearrange("p (c t) -> p c t", c=NCH)
                    ins = tt(lcd, lcd, lmid[:, d, :].unsqueeze(2).to_broadcast([P, NCH, P]), ALU.subtract)
                    ins.then_inc(sem("vector_step"), 1)
                    dve.wait_ge(sem("vector_step"), passed("vector_step"))
                ins = tt(sscal[:, :, 0:NCH - 1], lc[:, :, 0:NCH - 1, P - 1], lmid[:, :, 1:NCH], ALU.add)
                ins.then_inc(sem("vector_step"), 1)
                dve.wait_ge(sem("vector_step"), passed("vector_step"))
                dve.memset(sscal[:, :, NCH - 1:NCH], 0.0).then_inc(sem("vector_step"), 1)
                dve.wait_ge(sem("vector_step"), passed("vector_step"))
                tt(sgw[:], lcum[:], sgw[:], ALU.subtract).then_inc(sem("lcum_ready"), 1)
                dve.wait_ge(sem("lcum_ready"), passed("lcum_ready", l))
                for d in range(RT):
                    job = ("rk", l, d)
                    dve.wait_ge(*done(job))
                    tt(bonus[:, d, :], bank_of(job)[:], v_f[:, d, :], ALU.mult).then_inc(bank_read(job), 1)
                    dve.wait_ge(bank_read(job), turn(job))
                dve.wait_ge(sem("decay_ready"), count("decay_ready", l))
                tt(qr[:, :, 0, :], qr[:, :, 0, :], sgw[:], ALU.mult).then_inc(sem("vector_step"), 1)
                dve.wait_ge(sem("vector_step"), passed("vector_step"))
                tt(qr[:, :, 1, :], qr[:, :, 1, :], tmp[:], ALU.mult).then_inc(sem("vector_step"), 1)
                dve.wait_ge(sem("vector_step"), passed("vector_step"))
                tt(b_f[:], b_f[:], lcum[:], ALU.mult).then_inc(sem("vector_step"), 1)
                dve.wait_ge(sem("vector_step"), passed("vector_step"))
                tt(k_f[:], k_f[:], lcum[:], ALU.mult).then_inc(sem("wkv_in"), 1)
                dve.wait_ge(sem("wkv_in"), passed("wkv_in", l))
                for c in range(NCH):
                    wkv_chunk(l, c)
                pool_windows(l)
                for d in range(RT):
                    y = qr[:, d, 1, :]
                    job = ("mean", l, d)
                    dve.wait_ge(*done(job))
                    stt(y, bank_of(job)[:], 1.0 / HEAD, y, ALU.mult, ALU.subtract).then_inc(bank_read(job), 1)
                    dve.wait_ge(bank_read(job), turn(job))
                    tt(yt[d % 2][:], y, y, ALU.mult).then_inc(sem("var_ready"), 1)
                    dve.wait_ge(sem("var_ready"), passed("var_ready", (l, d)))
                    inv_root(("var", l, d), yr[d % 2][:])
                    tt(y, y, yr[d % 2][:], ALU.mult).then_inc(sem("vector_step"), 1)
                    dve.wait_ge(sem("vector_step"), passed("vector_step"))
                    ins = ts(y, y, omk[:, 4 + d:5 + d], col1(l, "lnx_b", d), ALU.mult, ALU.add)
                    ins.then_inc(sem("vector_step"), 1)
                    dve.wait_ge(sem("vector_step"), passed("vector_step"))
                    tt(y, y, bonus[:, d, :], ALU.add).then_inc(sem("vector_step"), 1)
                    dve.wait_ge(sem("vector_step"), passed("vector_step"))
                    job = ("g", l, d)
                    dve.wait_ge(*done(job))
                    tt(y, y, bank_of(job)[:], ALU.mult).then_inc(bank_read(job), 1)
                    dve.wait_ge(bank_read(job), turn(job))
                    split(y, ya_hi[:, d, :], ya_lo[:, d, :], ("ya", l, d))
                for d in range(4):
                    dve.wait_ge(*moved(("pool", l, d)))
                    split(mg[d % 2][:], yb_hi[:, d, :], yb_lo[:, d, :], ("yb", l, d))
                for m in range(DT):
                    for i, (gn, pn) in enumerate((("ga", "pa"), ("gb", "pb"))):
                        dve.wait_ge(*moved((gn, l, m)))
                        job = (pn, l, m)
                        dve.wait_ge(*done(job))
                        tt(mg[2 + i][:], mg[i][:], bank_of(job)[:], ALU.mult).then_inc(bank_read(job), 1)
                        dve.wait_ge(bank_read(job), turn(job))
                    tt(mg[2][:], mg[2][:], mg[3][:], ALU.add).then_inc(sem("vector_step"), 1)
                    dve.wait_ge(sem("vector_step"), passed("vector_step"))
                    split(mg[2][:], mx_hi[:, m, :], mx_lo[:, m, :], ("mx", l, m))
                for m in range(DT):
                    job = ("wo", l, m)
                    dve.wait_ge(*done(job))
                    ins = stt(x[:, m, :], bank_of(job)[:], mod[:, 16 + m:17 + m], x[:, m, :], ALU.mult, ALU.add)
                    ins.then_inc(bank_read(job), 1)
                    dve.wait_ge(bank_read(job), turn(job))
                    square_sum(x[:, m, :], m == 0, ("n2", l) if m == DT - 1 else None)
                normed_inputs(("n2", l), lambda i: gsc[:, 8 + i:9 + i], lambda i: mod[:, 24 + i:25 + i])
                dve.tensor_copy(gate2[:], mod[:, 40:48]).then_inc(sem("vector_step"), 1)
                dve.wait_ge(sem("vector_step"), passed("vector_step"))
                for f in range(2):
                    for m in range(HALF):
                        mm = f * HALF + m
                        dve.wait_ge(*moved(("fg", l, mm)))
                        job = ("fu", l, mm)
                        h = hs[mm % 2]
                        dve.wait_ge(*done(job))
                        tt(h[:, 1, :], h[:, 0, :], bank_of(job)[:], ALU.mult).then_inc(bank_read(job), 1)
                        dve.wait_ge(bank_read(job), turn(job))
                        split(h[:, 1, :], hid_hi[:, m, :], hid_lo[:, m, :], ("hid", l, f, m))
                        if l == 0:
                            ada(1, 2 * mm)
                            if mm >= HT - 2:
                                ada(1, 2 * mm + 4)
                    for m in range(DT):
                        job = ("fd", l, f, m)
                        dve.wait_ge(*done(job))
                        ins = stt(x[:, m, :], bank_of(job)[:], gate2[:, m:m + 1], x[:, m, :], ALU.mult, ALU.add)
                        ins.then_inc(bank_read(job), 1)
                        dve.wait_ge(bank_read(job), turn(job))
                        if f:
                            key = ("n1", 1) if l == 0 else ("nf", 0)
                            square_sum(x[:, m, :], m == 0, key if m == DT - 1 else None)

            def bonus_in(l, d):
                ins = stt(rkk[:, d, :], qr[:, d, 1, :], col1(l, "r_k", d), k_f[:, d, :], ALU.mult, ALU.mult)
                ins.then_inc(sem("rk_ready"), 1)
                dve.wait_ge(sem("rk_ready"), passed("rk_ready", (l, d)))

            def wkv_chunk(l, c):
                pair = kst[:, K_STRICT:K_INCL + 1, :]
                for h in range(NH):
                    job = ("score", l, c, h)
                    dve.wait_ge(*done(job))
                    bank = bank_of(job)
                    for i in range(2):
                        ins = tt(units[:, h, 2 * i:2 * i + 2, :],
                                 bank[:, 256 * i:256 * i + 256].rearrange("p (a t) -> p a t", a=2), pair, ALU.mult)
                        if i:
                            ins.then_inc(bank_read(job), 1)
                            dve.wait_ge(bank_read(job), turn(job))
                        else:
                            ins.then_inc(sem("vector_step"), 1)
                            dve.wait_ge(sem("vector_step"), passed("vector_step"))
                for g in range(2):
                    ins = tt(mt[g][:], units[:, 4 * g:4 * g + 4, 0, :], four(K_LEVEL), ALU.mult)
                    ins.then_inc(sem("vector_step"), 1)
                    dve.wait_ge(sem("vector_step"), passed("vector_step"))
                    tt(mt[g][:], four(K_ID), mt[g][:], ALU.subtract).then_inc(sem("mt_ready"), 1)
                    dve.wait_ge(sem("mt_ready"), passed("mt_ready", (l, c, g)))
                for v in range(1, len(LEVELS)):
                    for g in range(2):
                        ins = tt(bm[g][:], units[:, 4 * g:4 * g + 4, 0, :], four(K_LEVEL + v), ALU.mult)
                        ins.then_inc(sem("bm_ready"), 1)
                        dve.wait_ge(sem("bm_ready"), passed("bm_ready", (l, c, g, v)))
                    for g in range(2):
                        flat = lambda t: t[:].rearrange("p j t -> p (j t)")
                        if v < len(LEVELS) - 1:
                            job = ("mam", l, c, g, v)
                            dve.wait_ge(*done(job))
                            bank = bank_of(job)
                            dve.wait_ge(*moved(("inv_t", l, c, g)))
                            tt(flat(mi[g]), flat(mi[g]), bank[:], ALU.subtract).then_inc(bank_read(job), 1)
                            dve.wait_ge(bank_read(job), turn(job))
                        job = ("mamt", l, c, g, v)
                        dve.wait_ge(*done(job))
                        bank = bank_of(job)
                        tt(flat(mt[g]), flat(mt[g]), bank[:], ALU.subtract).then_inc(bank_read(job), 1)
                        dve.wait_ge(bank_read(job), turn(job))
                if c < NCH - 1:
                    job = ("state", l, c)
                    dve.wait_ge(*done(job))
                    bank = bank_of(job)
                    dve.wait_ge(*done(("y", l, c)))
                    if not c:
                        dve.memset(st[:], 0.0).then_inc(sem("vector_step"), 1)
                        dve.wait_ge(sem("vector_step"), passed("vector_step"))
                    for i in range(2):
                        rows = slice(64 * i, 64 * i + 64)
                        o = bank[rows, 0:RT * HEAD].rearrange("p (d v) -> p d v", d=RT)
                        s = st[rows, :, rows]
                        ins = tt(s, o, s, ALU.add)
                        if i:
                            ins.then_inc(bank_read(job), 1)
                            dve.wait_ge(bank_read(job), turn(job))
                        else:
                            ins.then_inc(sem("vector_step"), 1)
                            dve.wait_ge(sem("vector_step"), passed("vector_step"))
                    ins = tt(st[:], st[:], sscal[:, :, c:c + 1].to_broadcast([P, RT, P]), ALU.mult)
                    ins.then_inc(sem("state_ready"), 1)
                    dve.wait_ge(sem("state_ready"), passed("state_ready", (l, c + 1)))

            def four(k):
                return kst[:, k, :].unsqueeze(1).to_broadcast([P, 4, P])

            def pool_windows(l):
                dve.wait_ge(*done(("y", l, NCH - 1)))
                dve.memset(zp[:, :, 0:16], 0.0).then_inc(sem("vector_step"), 1)
                dve.wait_ge(sem("vector_step"), passed("vector_step"))
                for i in range(2):
                    dve.memset(zs[i][:, 0:16], 0.0).then_inc(sem("vector_step"), 1)
                    dve.wait_ge(sem("vector_step"), passed("vector_step"))
                for d, win in enumerate(WINDOWS):
                    dve.wait_ge(*moved(("p", l, M_POOL + d)))
                    dve.tensor_copy(zp[:, d, 16:528], yt[2 + d][:]).then_inc(sem("vector_step"), 1)
                    dve.wait_ge(sem("vector_step"), passed("vector_step"))
                    src, span, n = zp[:, d, :], 1, 0
                    while span < win:
                        dst = zs[n % 2]
                        ins = tt(dst[:, 16:528], src[:, 16:528], src[:, 16 - span:528 - span], ALU.add)
                        ins.then_inc(sem("vector_step"), 1)
                        dve.wait_ge(sem("vector_step"), passed("vector_step"))
                        src, span, n = dst, 2 * span, n + 1
                    tt(src[:, 16:32], src[:, 16:32], inv_cnt[:, d, :], ALU.mult).then_inc(sem("vector_step"), 1)
                    dve.wait_ge(sem("vector_step"), passed("vector_step"))
                    ts(src[:, 32:528], src[:, 32:528], 1.0 / win, None, ALU.mult).then_inc(sem("vector_step"), 1)
                    dve.wait_ge(sem("vector_step"), passed("vector_step"))
                    ins = tt(zp[:, d, 16:528], src[:, 16:528], zp[:, d, 16:528], ALU.subtract)
                    ins.then_inc(sem("pooled_ready"), 1)
                    dve.wait_ge(sem("pooled_ready"), passed("pooled_ready", (l, d)))

            for l in range(DEPTH):
                block1(l)
            inv_root(("norm", ("nf", 0)), rs[:])
            for i in range(DT):
                o = 2 * W1C + i
                stt(x[:, i, :], x[:, i, :], col[:, o:o + 1], rs[:], ALU.mult, ALU.mult).then_inc(sem("x_ready"), 1)
                dve.wait_ge(sem("x_ready"), passed("x_ready", i))
                square_sum(x[:, i, :], i == 0, ("m1", 0) if i == DT - 1 else None)
            dve.wait_ge(sem("rope_in"), 16)

            def cols_of(l, name):
                return lambda i: col2(l, name, i)

            def gla_decay(l, h):
                for i in range(2):
                    job = ("gz", l, h, i)
                    dve.wait_ge(*done(job))
                    bank = bank_of(job)
                    dve.wait_ge(sem("abs_ready"), count("abs_ready", (l, h, i)))
                    ts(la[i][:].rearrange("p c t -> p (c t)"), bank[:], col2(l, "b_alpha", 4 * i + h), 0.0,
                            ALU.add, ALU.min).then_inc(bank_read(job), 1)
                    dve.wait_ge(bank_read(job), turn(job))
                for i in range(2):
                    dve.wait_ge(sem("log_ready"), count("log_ready", (l, h, i)))
                    tt(la[i][:], la[i][:], ln[i][:], ALU.subtract).then_inc(sem("vector_step"), 1)
                    dve.wait_ge(sem("vector_step"), passed("vector_step"))
                    for c in range(NCH):
                        dve.tensor_tensor_scan(ln[i][:, c, :], kst[:, K_ONES, :], la[i][:, c, :], 0.0,
                                                  ALU.mult, ALU.add).then_inc(sem("vector_step"), 1)
                        dve.wait_ge(sem("vector_step"), passed("vector_step"))
                    last = ln[i][:, :, P - 1]
                    n = NCH - 1
                    if i:
                        dve.tensor_copy(dsc[1][:, 0:NCH], last).then_inc(sem("vector_step"), 1)
                        dve.wait_ge(sem("vector_step"), passed("vector_step"))
                        tt(ln[1][:], ln[1][:], la[1][:], ALU.subtract).then_inc(sem("vector_step"), 1)
                        dve.wait_ge(sem("vector_step"), passed("vector_step"))
                    dve.tensor_copy(mid[i][:], ln[i][:, :, 63]).then_inc(sem("vector_step"), 1)
                    dve.wait_ge(sem("vector_step"), passed("vector_step"))
                    if i:
                        tt(dsc[1][:, 0:n], dsc[1][:, 0:n], mid[1][:, 1:NCH], ALU.add).then_inc(sem("vector_step"), 1)
                        dve.wait_ge(sem("vector_step"), passed("vector_step"))
                        ins = tt(dsc[1][:, 0:n], dsc[1][:, 0:n], mid[1][:, 0:n], ALU.subtract)
                        ins.then_inc(sem("vector_step"), 1)
                        dve.wait_ge(sem("vector_step"), passed("vector_step"))
                    ins = tt(ln[i][:], ln[i][:], mid[i][:].unsqueeze(2).to_broadcast([P, NCH, P]), ALU.subtract)
                    ins.then_inc(sem("vector_step"), 1)
                    dve.wait_ge(sem("vector_step"), passed("vector_step"))
                    if not i:
                        ins = tt(dsc[0][:, 0:n], ln[0][:, 0:n, P - 1], mid[0][:, 1:NCH], ALU.add)
                        ins.then_inc(sem("vector_step"), 1)
                        dve.wait_ge(sem("vector_step"), passed("vector_step"))
                        dve.memset(dsc[0][:, n:NCH], 0.0).then_inc(sem("cum_ready"), 1)
                        dve.wait_ge(sem("cum_ready"), passed("cum_ready", (l, h, i)))
                    else:
                        dve.memset(dsc[1][:, n:NCH], 0.0).then_inc(sem("cum_ready"), 1)
                        dve.wait_ge(sem("cum_ready"), passed("cum_ready", (l, h, i)))

            def gla_core(l, h):
                q3 = gq[h % 2][:].rearrange("p (c t) -> p c t", c=NCH)
                k3 = gk[h % 2][:].rearrange("p (c t) -> p c t", c=NCH)
                dve.wait_ge(*moved(("gk", l, h)))
                for i in range(2):
                    dve.wait_ge(sem("ed_ready"), count("ed_ready", (l, h, i)))
                    stt(qd[i][:].rearrange("p c t -> p (c t)"), gq[h % 2][:], GDK ** -0.5,
                           la[i][:].rearrange("p c t -> p (c t)"), ALU.mult, ALU.mult).then_inc(sem("vector_step"), 1)
                    dve.wait_ge(sem("vector_step"), passed("vector_step"))
                    ins = tt(kd[i][:], k3, ln[i][:], ALU.mult)
                    if i:
                        ins.then_inc(sem("qd_ready"), 1)
                        dve.wait_ge(sem("qd_ready"), passed("qd_ready", (l, h)))
                    else:
                        ins.then_inc(sem("vector_step"), 1)
                        dve.wait_ge(sem("vector_step"), passed("vector_step"))
                job = ("gsc", l, h, 0)
                dve.wait_ge(*done(job))
                bank = bank_of(job)
                ins = tt(sc[:], bank[:].rearrange("p (c t) -> p c t", c=NCH), four(K_INCL), ALU.mult)
                ins.then_inc(bank_read(job), 1)
                dve.wait_ge(bank_read(job), turn(job))
                job = ("gsc", l, h, 1)
                dve.wait_ge(*done(job))
                bank = bank_of(job)
                ins = tt(sc2[:], bank[:].rearrange("p (c t) -> p c t", c=NCH), four(K_INCLREV), ALU.mult)
                ins.then_inc(bank_read(job), 1)
                dve.wait_ge(bank_read(job), turn(job))
                tt(sc[:], sc[:], sc2[:], ALU.add).then_inc(sem("sc_ready"), 1)
                dve.wait_ge(sem("sc_ready"), passed("sc_ready", (l, h)))
                for n in range(NCH - 1):
                    job = ("gst", l, h, n)
                    dve.wait_ge(*done(job))
                    bank = bank_of(job)
                    for i in range(2):
                        part = bank[:, i * GDV:(i + 1) * GDV]
                        c = n if i == 0 else NCH - 2 - n
                        src = part
                        if n:
                            ins = tt(gs[i][:, n, :], gs[i][:, n - 1, :], part, ALU.add)
                            if i:
                                ins.then_inc(bank_read(job), 1)
                                dve.wait_ge(bank_read(job), turn(job))
                            else:
                                ins.then_inc(sem("vector_step"), 1)
                                dve.wait_ge(sem("vector_step"), passed("vector_step"))
                            src = gs[i][:, n, :]
                        ins = ts(gs[i][:, n, :], src, dsc[i][:, c:c + 1], None, ALU.mult)
                        if n == 0 and i:
                            ins.then_inc(bank_read(job), 1)
                            dve.wait_ge(bank_read(job), turn(job))
                        elif n == NCH - 2 and i:
                            ins.then_inc(sem("gs_ready"), 1)
                            dve.wait_ge(sem("gs_ready"), passed("gs_ready", (l, h)))
                        else:
                            ins.then_inc(sem("vector_step"), 1)
                            dve.wait_ge(sem("vector_step"), passed("vector_step"))
                inv_root(("gn", l, h), rsg[:])
                for j in range(2):
                    job = ("go", l, h, j)
                    dve.wait_ge(*done(job))
                    ins = stt(ot[:], bank_of(job)[:], col2(l, "g_gla", j), rsg[:], ALU.mult, ALU.mult)
                    ins.then_inc(bank_read(job), 1)
                    dve.wait_ge(bank_read(job), turn(job))
                    dve.wait_ge(*moved(("gg", l, h, j)))
                    tt(ot[:], ot[:], sg[h % 2][:, j, :], ALU.mult).then_inc(sem("vector_step"), 1)
                    dve.wait_ge(sem("vector_step"), passed("vector_step"))
                    split(ot[:], go_hi[:, 2 * h + j, :], go_lo[:, 2 * h + j, :], ("go", l, 2 * h + j))

            def rope_norm(key, l, gain):
                inv_root(("qs",) + key, ars[:])
                stt(qn[:], qraw[:], col2(l, gain, 0), ars[:], ALU.mult, ALU.mult).then_inc(sem("qn_ready"), 1)
                dve.wait_ge(sem("qn_ready"), passed("qn_ready", key))

            def rope_out(key, dst):
                tt(qt_[:], qn[:], rope_t[:, 0, :], ALU.mult).then_inc(sem("vector_step"), 1)
                dve.wait_ge(sem("vector_step"), passed("vector_step"))
                job = ("rot",) + key
                dve.wait_ge(*done(job))
                tt(dst, bank_of(job)[:], rope_t[:, 1, :], ALU.mult).then_inc(bank_read(job), 1)
                dve.wait_ge(bank_read(job), turn(job))
                tt(dst, dst, qt_[:], ALU.add).then_inc(sem("rope_ready"), 1)
                dve.wait_ge(sem("rope_ready"), passed("rope_ready", key))

            def post_norm(l, key, gain, then):
                inv_root(("norm", (key, l)), rs[:])
                for i in range(DT):
                    ins = stt(nt[:], yy[:, i, :], col2(l, gain, i), rs[:], ALU.mult, ALU.mult)
                    ins.then_inc(sem("vector_step"), 1)
                    dve.wait_ge(sem("vector_step"), passed("vector_step"))
                    ins = tt(x[:, i, :], x[:, i, :], nt[:], ALU.add)
                    if then == "out":
                        ins.then_inc(sem("x_done"), 1)
                        dve.wait_ge(sem("x_done"), passed("x_done", i))
                    else:
                        ins.then_inc(sem("vector_step"), 1)
                        dve.wait_ge(sem("vector_step"), passed("vector_step"))
                    if then == "split":
                        split(x[:, i, :], in_hi[:, i, :], in_lo[:, i, :], ("pl", l, i))
                    elif then != "out":
                        square_sum(x[:, i, :], i == 0, then if i == DT - 1 else None)

            def block2(l):
                normed_inputs(("m1", l), cols_of(l, "g_mix_pre"))
                gla_decay(l, 0)
                for h in range(GH):
                    gla_core(l, h)
                    if h + 1 < GH:
                        gla_decay(l, h + 1)
                for m in range(DT):
                    dve.wait_ge(*moved(("g2a", l, m)))
                    job = ("p2a", l, m)
                    dve.wait_ge(*done(job))
                    tt(ma[:, m, :], mgs[m % 2][:], bank_of(job)[:], ALU.mult).then_inc(bank_read(job), 1)
                    dve.wait_ge(bank_read(job), turn(job))
                for i in range(KVH):
                    rope_norm(("k", l, i), l, "g_k")
                    rope_out(("k", l, i), ak[:, i, :])
                rope_norm(("q", l, 0), l, "g_q")
                rope_out(("q", l, 0), aq[0][:])
                for h in range(QH):
                    for t in range(NCH):
                        dve.wait_ge(*done(("as", l, h, t)))
                        bank = bank_of(("as", l, h, t))
                        dve.tensor_reduce(stat[:, 2, t:t + 1], bank[:], AX.X, ALU.max).then_inc(sem("vector_step"), 1)
                        dve.wait_ge(sem("vector_step"), passed("vector_step"))
                        ins = ts(stat[:, 0, t:t + 1], stat[:, 2, t:t + 1], -(P ** -0.5), None, ALU.mult)
                        ins.then_inc(sem("max_ready"), 1)
                        dve.wait_ge(sem("max_ready"), passed("max_ready", (l, h, t)))
                    for t in range(NCH):
                        dve.wait_ge(*moved(("as", l, h, t)))
                        dve.reciprocal(stat[:, 2, t:t + 1], stat[:, 1, t:t + 1]).then_inc(sem("vector_step"), 1)
                        dve.wait_ge(sem("vector_step"), passed("vector_step"))
                        ts(pr[:, t, :], pr[:, t, :], stat[:, 2, t:t + 1], None, ALU.mult).then_inc(sem("pr_ready"), 1)
                        dve.wait_ge(sem("pr_ready"), passed("pr_ready", (l, h, t)))
                    if h + 1 < QH:
                        rope_norm(("q", l, h + 1), l, "g_q")
                        rope_out(("q", l, h + 1), aq[(h + 1) % 2][:])
                    job = ("pv", l, h)
                    dve.wait_ge(*done(job))
                    bank = bank_of(job)
                    dve.tensor_copy(qt_[:], bank[:]).then_inc(bank_read(job), 1)
                    dve.wait_ge(bank_read(job), turn(job))
                    split(qt_[:], ao_hi[:, h, :], ao_lo[:, h, :], ("ao", l, h))
                for m in range(DT):
                    dve.wait_ge(*moved(("g2b", l, m)))
                    job = ("p2b", l, m)
                    dve.wait_ge(*done(job))
                    tt(mgt[:], mgs[m % 2][:], bank_of(job)[:], ALU.mult).then_inc(bank_read(job), 1)
                    dve.wait_ge(bank_read(job), turn(job))
                    tt(mgt[:], mgt[:], ma[:, m, :], ALU.add).then_inc(sem("vector_step"), 1)
                    dve.wait_ge(sem("vector_step"), passed("vector_step"))
                    split(mgt[:], m2_hi[:, m, :], m2_lo[:, m, :], ("m2", l, m))
                for m in range(DT):
                    job = ("wo2", l, m)
                    dve.wait_ge(*done(job))
                    dve.tensor_copy(yy[:, m, :], bank_of(job)[:]).then_inc(bank_read(job), 1)
                    dve.wait_ge(bank_read(job), turn(job))
                    square_sum(yy[:, m, :], m == 0, ("m2", l) if m == DT - 1 else None)
                post_norm(l, "m2", "g_mix_post", ("m3", l))
                normed_inputs(("m3", l), cols_of(l, "g_ffn_pre"))
                for f in range(2):
                    for m in range(HALF):
                        mm = f * HALF + m
                        dve.wait_ge(*moved(("eg", l, mm)))
                        job = ("eu", l, mm)
                        h = hs2[mm % 2]
                        dve.wait_ge(*done(job))
                        tt(h[:, 1, :], h[:, 0, :], bank_of(job)[:], ALU.mult).then_inc(bank_read(job), 1)
                        dve.wait_ge(bank_read(job), turn(job))
                        split(h[:, 1, :], h2_hi[:, m, :], h2_lo[:, m, :], ("h2", l, f, m))
                    for m in range(DT):
                        job = ("ed", l, f, m)
                        dve.wait_ge(*done(job))
                        bank = bank_of(job)
                        if f:
                            tt(yy[:, m, :], yy[:, m, :], bank[:], ALU.add).then_inc(bank_read(job), 1)
                            dve.wait_ge(bank_read(job), turn(job))
                            square_sum(yy[:, m, :], m == 0, ("m4", l) if m == DT - 1 else None)
                        else:
                            dve.tensor_copy(yy[:, m, :], bank[:]).then_inc(bank_read(job), 1)
                            dve.wait_ge(bank_read(job), turn(job))
                for i in range(2):
                    split(sml[:, 1 + i, :], pp_hi[:, i, :], pp_lo[:, i, :], ("pp", l, i))
                post_norm(l, "m4", "g_ffn_post", "split")
                for m in range(DT):
                    dve.wait_ge(*moved(("pg", l, m)))
                    job = ("pe", l, m)
                    dve.wait_ge(*done(job))
                    tt(yy[:, m, :], mg2[m % 2][:], bank_of(job)[:], ALU.mult).then_inc(bank_read(job), 1)
                    dve.wait_ge(bank_read(job), turn(job))
                    square_sum(yy[:, m, :], m == 0, ("m5", l) if m == DT - 1 else None)
                post_norm(l, "m5", "g_ple_post", ("m1", 1) if l == 0 else "out")

            for l in range(DEPTH):
                block2(l)

        @block.gpsimd
        def _(pool):
            for s, (kind, blocks) in enumerate(slabs):
                if kind == "raw":
                    continue
                n = split_no[s]
                j, r = n % 2, s % 2
                pool.wait_ge(sem(f"slab_in{r}"), count(f"slab_in{r}", s))
                if n >= 2:
                    before = [q for q in split_no if split_no[q] == n - 2][0]
                    pool.wait_ge(*slab_end[before])
                pool.tensor_scalar(w_hi[j][:], raw[r][:], 1.0, 1.0, ALU.mult, ALU.mult).then_inc(sem("slab_hi"), 1)
                pool.wait_ge(sem("slab_hi"), n + 1)
                pool.tensor_tensor(w_lo[j][:], raw[r][:], w_hi[j][:].bitcast(F32), ALU.subtract).then_inc(
                    sem("slab_split"), 1)

        @block.sync
        def _(sp):
            for s, (kind, blocks) in enumerate(slabs):
                if s >= 2:
                    if slabs[s - 2][0] == "split":
                        sp.wait_ge(sem("slab_split"), split_no[s - 2] + 1)
                    else:
                        sp.wait_ge(*slab_end[s - 2])
                sp.dma_start(raw[s % 2][:], wstream[s]).then_inc(sem(f"slab_in{s % 2}"), 16)
                passed(f"slab_in{s % 2}", s, by=16)
            for i in range(DT):
                sp.wait_ge(sem("x_done"), count("x_done", i))
                sp.dma_start(out[:, i, :], x[:, i, :]).then_inc(sem("out_stored"), 16)
            sp.wait_ge(sem("out_stored"), 16 * DT)

        return {**sig.at}, slabs


def constants():
    f = np.float32
    i, j = np.arange(P)[:, None], np.arange(P)[None, :]
    mats = [i == j, np.ones((P, P)), i // HEAD == j // HEAD]
    rot = np.zeros((P, P))
    for out in range(P):
        if out % 64 < 32:
            rot[out + 32, out] = -1.0
        else:
            rot[out - 32, out] = 1.0
    mats += [rot, i < j, i <= j, i >= j]
    for b in LEVELS:
        mats.append((i // (2 * b) == j // (2 * b)) & (i % (2 * b) < b) & (j % (2 * b) >= b))
    mats = np.ascontiguousarray(np.stack([m.astype(f) for m in mats]).transpose(1, 0, 2))
    inv = f(10000.0) ** (-np.arange(0, 64, 2, dtype=f) / f(64))
    t = np.arange(T)
    ang = np.stack([(t // 64).astype(f)[None, :] * inv[:, None], (t % 64).astype(f)[None, :] * inv[:, None]])
    place = np.arange(P)
    full = ang[place // 64, place % 32]
    rope = np.ascontiguousarray(np.stack([np.cos(full), np.sin(full)], 1).astype(f))
    pos = np.arange(1, 17, dtype=f)
    cnt = np.stack([f(1) / np.minimum(pos, f(w)) for w in WINDOWS]).astype(f)
    return mats, rope, np.ascontiguousarray(np.broadcast_to(cnt, (P, 4, 16)))


def columns(vectors):
    parts = []
    for v in vectors:
        v = np.asarray(v).reshape(-1)
        parts.append(np.pad(v, (0, -v.size % P)).reshape(-1, P).T)
    return np.concatenate(parts, 1)


def kernel(**inputs):
    from concourse import bacc
    from concourse.bass_utils import run_bass_kernel_spmd

    a = {k: np.asarray(v) for k, v in inputs.items()}
    mats, rope, cnt = constants()
    feature_major = lambda t: np.ascontiguousarray(t.T.reshape(-1, P, t.shape[0]).transpose(1, 0, 2))
    z = lambda *s: np.zeros(s, np.float32)
    cols, small = [], []
    weights = {k: a[v] for k, v in {
        "ada_w": "ada_w", "proj_a": "proj_a", "proj_b": "proj_b", "w_out": "w_out", "w_gu": "w_gu",
        "w_down": "w_down", "w_o_gla": "w_o_gla_2", "w_o_attn": "w_o_attn_2", "w_out2": "w_out_2",
        "w_ffn_in": "w_ffn_in_2", "w_ffn_out": "w_ffn_out_2", "w_ple_proj": "w_ple_proj_2",
        "w_ple_gate": "w_ple_gate_2"}.items()}
    w_in, w_in2 = [], []
    for l in range(DEPTH):
        down = a["v_down"][l - 1] if l else z(D, 32)
        mu_v = a["mu_v"][l - 1] if l else z(32)
        v0 = a["v0"][l - 1] if l else z(D_R)
        v_up = a["v_up"][l - 1] if l else z(32, D_R)
        w = a["w_in"][l]
        n = 3 * D_R + 64 + 64 + 160
        w_in.append(np.concatenate([w[:, :n], down, z(D, 64), w[:, n:]], 1))
        mu = np.concatenate([a["mu_shift"][l], mu_v])
        cols.append(columns([a["ada_b"][l], a["norm1_g"][l], a["norm2_g"][l], mu, a["w0"][l], a["a0"][l], v0,
                             a["k_k"][l], a["k_a"][l], a["r_k"][l], a["lnx_g"][l], a["lnx_b"][l],
                             a["pool_scale"][l]]))
        small.append(np.stack([
            np.concatenate([a["w_up"][l], a["a_up"][l]]), a["g_up"][l][:P],
            np.concatenate([a["g_up"][l][P:], v_up, z(64, D_R)]),
            a["pool_w"][l].transpose(1, 0, 2).reshape(P, 512)], 1))
    cols.append(columns([a["final_g"]]))
    for l in range(DEPTH):
        w = a["w_in_2"][l]
        w_in2.append(np.concatenate([w[:, :3072], w[:, 3072:3088], z(D, 16), w[:, 3088:3104], z(D, 80), w[:, 3104:]], 1))
        cols.append(columns([a["g_mix_pre_2"][l], a["b_alpha_2"][l], a["g_gla_out_2"][l], a["g_q_norm_2"][l],
                             a["g_k_norm_2"][l], a["g_mix_post_2"][l], a["g_ffn_pre_2"][l], a["g_ffn_post_2"][l],
                             a["g_ple_post_2"][l]]))
        up = z(P, 512)
        up[0:16], up[32:48] = a["w_alpha_up_2"][l]
        small.append(np.concatenate([up[:, None], feature_major(a["p_2"][l, 0]), z(P, 1, 512)], 1))
    weights["w_in"], weights["w_in2"] = np.stack(w_in), np.stack(w_in2)

    def build(known, n_slabs):
        nc = bacc.Bacc("TRN2", target_bir_lowering=False, num_devices=1)
        shapes = {"weight_slabs": (n_slabs, P, SLAB, P), "x_in": (P, DT, T), "c_in": (P, DT), "cols": (P, NCOL),
                  "consts": (P, NK, P), "rope": (P, 2, T), "inv_count": (P, 4, 16), "small": (4, P, 4, 512)}
        args = [nc.dram_tensor(n, s, F32, kind="ExternalInput").ap() for n, s in shapes.items()]
        args.append(nc.dram_tensor("out", (P, DT, T), F32, kind="ExternalOutput").ap())
        counts, slabs = emit(nc, known, *args)
        return nc, counts, slabs

    _, counts, slabs = build(None, 400)
    nc, _, slabs = build(counts, len(slabs))
    stream = np.zeros((len(slabs), P, SLAB, P), np.float32)
    for s, (_, blocks) in enumerate(slabs):
        for i, (name, l, k, m) in enumerate(blocks):
            stream[s, :, i] = weights[name][l, k * P:(k + 1) * P, m * P:(m + 1) * P]
    arrays = {"weight_slabs": stream, "x_in": feature_major(a["x"][0]), "c_in": columns([a["c"]]),
              "cols": np.concatenate(cols, 1), "consts": mats, "rope": rope, "inv_count": cnt,
              "small": np.stack(small)}
    arrays = {k: np.ascontiguousarray(v, dtype=np.float32) for k, v in arrays.items()}
    r = run_bass_kernel_spmd(nc, [arrays], core_ids=[0])
    got = r.results[0]["out"]
    return np.ascontiguousarray(got.transpose(2, 1, 0).reshape(1, T, D))
```

```python
from contextlib import ExitStack

import numpy as np

import concourse.bass as bass
from concourse import mybir

F32 = mybir.dt.float32
F32R = mybir.dt.float32r
ALU = mybir.AluOpType
ACT = mybir.ActivationFunctionType
AX = mybir.AxisListType

P = 128
T = 512
NCH = T // P
D = 1024
DT = D // P
DEPTH = 2
SLAB = 16
D_R = 512
ZPAD = 8
RT = D_R // P
HEAD = 64
NH = D_R // HEAD
HID = 2816
HT = HID // P
HALF = HT // 2
WINDOWS = (2, 4, 8, 16)
EXP_MHALF = float(np.exp(np.float32(-0.5)))
EPS_RMS = 1e-6
EPS_GN = 64e-5
GH = 4
GDK = 128
GDV = 256
TAU = 16.0
QH = 8
KVH = 2
LEVELS = (1, 2, 4, 8, 16, 32, 64)

FILL_PREP = 32

WINDOW_SLAB = (1, 1, 2, 2)

C1 = {}
_at = 0
for _n, _w in (("ada_b", 48), ("norm1_g", 8), ("norm2_g", 8), ("mu", 15), ("w0", 4), ("a0", 4), ("v0", 4),
               ("k_k", 4), ("k_a", 4), ("r_k", 4), ("lnx_g", 4), ("lnx_b", 4), ("pool_scale", 4)):
    C1[_n] = _at
    _at += _w
W1C = _at
C2 = {}
_at = 0
for _n, _w in (("g_mix_pre", 8), ("b_alpha", 8), ("g_gla", 2), ("g_q", 1), ("g_k", 1), ("g_mix_post", 8),
               ("g_ffn_pre", 8), ("g_ffn_post", 8), ("g_ple_post", 8)):
    C2[_n] = _at
    _at += _w
W2C = _at
NCOL = 2 * W1C + 8 + 2 * W2C

K_ID, K_ONES, K_HEADS, K_ROT, K_STRICT, K_INCL, K_INCLREV, K_LEVEL = 0, 1, 2, 3, 4, 5, 6, 7
NK = K_LEVEL + len(LEVELS)

M_R, M_K, M_V, M_WA, M_GL, M_GLV, M_POOL, M_GA, M_GB = 0, 4, 8, 12, 13, 14, 15, 19, 27
N_GQ, N_GK, N_GV, N_GG, N_RA, N_AQ, N_AK, N_AV, N_GA, N_GB = 0, 4, 8, 16, 24, 25, 33, 35, 37, 45


class Signals:

    def __init__(self, nc, ctx, known):
        self.nc, self.ctx, self.known = nc, ctx, known
        self.sems, self.count, self.at = {}, {}, {}

    def sem(self, name):
        if name not in self.sems:
            self.sems[name] = self.ctx.enter_context(self.nc.semaphore(name))
            self.count[name] = 0
        return self.sems[name]

    def passed(self, name, key=None, by=1):
        self.sem(name)
        self.count[name] += by
        if key is not None:
            self.at[(name, key)] = self.count[name]
        return self.count[name]

    def value(self, name, key):
        return self.known[(name, key)] if self.known else 1


def emit(nc, known, wstream, ada_slabs, xT, c_rows, cols, consts, rope, inv_count, small, out):
    with ExitStack() as ctx:
        sig = Signals(nc, ctx, known)
        psum = [ctx.enter_context(nc.psum_tensor(f"psum{i}", [P, 512], F32)) for i in range(8)]
        place = [nc.sbuf_base + (-nc.sbuf_base) % 64]

        def fixed(name, shape, dt=F32):
            o = place[0]
            place[0] += (int(np.prod(shape[1:])) * 4 + 31) // 32 * 32
            return nc.alloc_sbuf_tensor_at(name, shape, dt, offset=o)

        x = fixed("x", [P, DT, T])
        in_hi = fixed("in_hi", [P, DT, T], F32R)
        in_lo = fixed("in_lo", [P, DT, T], F32R)
        raw = [fixed(f"raw{i}", [P, SLAB, P]) for i in range(2)]
        w_hi = [fixed(f"w_hi{i}", [P, SLAB, P], F32R) for i in range(2)]
        w_lo = [fixed(f"w_lo{i}", [P, SLAB, P], F32R) for i in range(2)]
        col = fixed("col", [P, NCOL])
        kst = fixed("kst", [P, NK, P])
        inv_cnt = fixed("inv_cnt", [P, 4, 16])
        sml = fixed("sml", [P, 4, 512])
        mod = fixed("mod", [P, 48])
        gsc = fixed("gsc", [P, 16])
        omk = fixed("omk", [P, 8])
        gate2 = fixed("gate2", [P, 8])
        root4 = fixed("root4", [P, NCH])
        eps = fixed("eps", [P, 4])
        order1 = [M_WA, M_GL, M_GLV] + [m + d for m in (M_K, M_R, M_V) for d in range(RT)]
        arena = place[0]

        def ar(name, kb, shape, dt=F32):
            o = arena + int(kb * 1024)
            assert o + int(np.prod(shape[1:])) * 4 <= nc.sbuf_usable_end, name
            return nc.alloc_sbuf_tensor_at(name, shape, dt, offset=o)

        qr = ar("qr", 0, [P, RT, 2, T])
        b_f = ar("b_f", 16, [P, RT, T])
        k_f = ar("k_f", 24, [P, RT, T])
        v_f = ar("v_f", 32, [P, RT, T])
        bonus = ar("bonus", 40, [P, RT, T])
        gl_s = ar("gl_s", 48, [P, 2, T])
        zbuf = [ar(f"zbuf{i}", 52 + 2.0625 * i, [P, ZPAD + T]) for i in range(2)]
        wa = ar("wa", 56.25, [P, T])
        lcum = ar("lcum", 58.25, [P, RT, T])
        sgw = ar("sgw", 66.25, [P, RT, T])
        tmp = ar("tmp", 74.25, [P, RT, T])
        gate_v = ar("gate_v", 82.25, [P, RT, T])
        lmid = ar("lmid", 94.25, [P, RT, NCH])
        sscal = ar("sscal", 94.375, [P, RT, NCH])
        units = ar("units", 52, [P, NH, 4, P])
        mt = [ar(f"mt{g}", 68 + 2 * g, [P, 4, P]) for g in range(2)]
        mi = [ar(f"mi{g}", 72 + 2 * g, [P, 4, P]) for g in range(2)]
        gm = [ar(f"gm{g}", 76 + 2 * g, [P, 4, P]) for g in range(2)]
        bm = [ar(f"bm{g}", 80 + 2 * g, [P, 4, P]) for g in range(2)]
        tok = [ar(f"tok{i}", 84 + 2 * i, [P, T]) for i in range(3)]
        u0 = ar("u0", 76, [P, T])
        u1 = ar("u1", 78, [P, T])
        st = ar("st", 90, [P, RT, P])
        ya_hi = ar("ya_hi", 52, [P, RT, T], F32R)
        ya_lo = ar("ya_lo", 60, [P, RT, T], F32R)
        yr = [ar(f"yr{i}", 80 + 2 * i, [P, T]) for i in range(2)]
        nv = ar("nv", 90.25, [P, T])
        gate_st = ar("gate_st", 92.25, [P, T])
        yt = [ar(f"yt{i}", 68 + 2 * i, [P, T]) for i in range(6)]
        zp = ar("zp", 84, [P, 4, 528])
        e_neg = [nv, gate_st]
        zs = [ar(f"zs{i}", 72 + 2.25 * i, [P, 528]) for i in range(2)]
        yb_hi = ar("yb_hi", 16, [P, 4, T], F32R)
        yb_lo = ar("yb_lo", 24, [P, 4, T], F32R)
        mx_lo = ar("mx_lo", 0, [P, DT, T], F32R)
        mx_hi = ar("mx_hi", 68, [P, DT, T], F32R)
        ssq = ar("ssq", 86.25, [P, T])
        sqt = ar("sqt", 88.25, [P, T])
        diag = ar("diag", 90.25, [P, NCH, P])
        nt = ar("nt", 92.25, [P, T])
        sq_ = [ssq, sqt]
        nts = [nt, sqt]
        gin = [[ar(f"gin{i}{j}", 40 + 4 * i + 2 * j, [P, T]) for j in range(2)] for i in range(2)]
        mt_ = [ar(f"mt_{i}", 48 + 2 * i, [P, T]) for i in range(2)]
        c_act = ar("c_act", 82.25, [P, D])
        ada_buf = {kb: ar(f"ada_at{kb}", kb, [P, 2, D]) for kb in (0, 8, 16, 24, 32, 40, 48, 56, 72)}
        ada_order = ([(0, m, 8 * m) for m in range(8)] + [(0, 8 + m, 32 if m in (0, 2, 4, 6, 8, 10, 12) else 40)
                                                              for m in range(16)]
                     + [(1, m, (24, 72)[m % 2]) for m in range(24)])
        hid_hi = ar("hid_hi", 0, [P, HALF, T], F32R)
        hid_lo = ar("hid_lo", 40, [P, HALF, T], F32R)
        hs = [ar(f"hs{i}", 64 + 4 * i, [P, 2, T]) for i in range(2)]

        rope_t = ar("rope_t", 0, [P, 2, T])
        go_hi = ar("go_hi", 4, [P, DT, T], F32R)
        go_lo = ar("go_lo", 20, [P, DT, T], F32R)
        ra = ar("ra", 36, [P, T])
        gq = [ar(f"gq{i}", 38 + 2 * i, [P, T]) for i in range(2)]
        gk = [ar(f"gk{i}", 42 + 2 * i, [P, T]) for i in range(2)]
        gv = [ar(f"gv{i}", 46 + 4 * i, [P, NCH, GDV]) for i in range(2)]
        sg = [ar(f"sg{i}", 54 + 4 * i, [P, 2, T]) for i in range(2)]
        la = [ar(f"la{i}", 62 + 2 * i, [P, NCH, P]) for i in range(2)]
        ln = [ar(f"ln{i}", 66 + 2 * i, [P, NCH, P]) for i in range(2)]
        qd = [ar(f"qd{i}", 70 + 4 * i, [P, NCH, P]) for i in range(2)]
        kd = [ar(f"kd{i}", 72 + 4 * i, [P, NCH, P]) for i in range(2)]
        kt_ = [ar(f"kt{i}", 78 + 2 * i, [P, NCH, P]) for i in range(2)]
        sc = ar("sc", 82, [P, NCH, P])
        sc2 = ar("sc2", 92, [P, NCH, P])
        gs = [ar(f"gs{i}", 84 + 3 * i, [P, NCH - 1, GDV]) for i in range(2)]
        osq = ar("osq", 78, [P, 2, T])
        rsg = ar("rsg", 82, [P, T])
        ot = ar("ot", 90, [P, T])
        mid = [ar(f"mid{i}", 94 + i / 16, [P, NCH]) for i in range(2)]
        dsc = [ar(f"dsc{i}", 94.25 + i / 16, [P, NCH]) for i in range(2)]
        gate_st2 = ar("gate_st2", 0, [P, T])
        ee = ar("ee", 36, [P, DT, T])
        ma = ar("ma", 36, [P, DT, T])
        ao_hi = ar("ao_hi", 4, [P, DT, T], F32R)
        ao_lo = ar("ao_lo", 20, [P, DT, T], F32R)
        ak = ar("ak", 52, [P, KVH, T])
        av = ar("av", 56, [P, NCH, KVH * P])
        aq = [ar(f"aq{i}", 60 + 2 * i, [P, T]) for i in range(2)]
        pr = ar("pr", 64, [P, NCH, T])
        prt = ar("prt", 72, [P, NCH, T])
        qraw = ar("qraw", 80, [P, T])
        asq = ar("asq", 82, [P, T])
        ars = ar("ars", 84, [P, T])
        qn = ar("qn", 86, [P, T])
        qt_ = ar("qt", 88, [P, T])
        stat = ar("stat", 90, [P, 3, NCH])
        m2_hi = ar("m2_hi", 52, [P, DT, T], F32R)
        m2_lo = ar("m2_lo", 68, [P, DT, T], F32R)
        mgs = [ar(f"mgs{i}", 84 + 2 * i, [P, T]) for i in range(2)]
        yy = ar("yy", 4, [P, DT, T])
        h2_hi = ar("h2_hi", 36, [P, HALF, T], F32R)
        h2_lo = ar("h2_lo", 58, [P, HALF, T], F32R)
        hs2 = [ar(f"hs2{i}", 80 + 4 * i, [P, 2, T]) for i in range(2)]
        mgt = ar("mgt", 88, [P, T])
        mg2 = [ar(f"mg2{i}", 80 + 2 * i, [P, T]) for i in range(2)]
        pp_hi = ar("pp_hi", 20, [P, 2, T], F32R)
        pp_lo = ar("pp_lo", 24, [P, 2, T], F32R)

        slabs = []
        slab_end = {}
        jobs = {}
        used = {"lin": 0, "bg": 0, "aux": 0}
        BANKS = {"lin": (0, 3), "bg": (3, 1), "aux": (4, 4)}
        closed = {}
        windows_at = []
        ada_issue = {}
        cursor = {"slab": None, "at": SLAB}
        spill = nc.dram_tensor("spill", (36 * DEPTH, P, T), F32).ap()

        def spilled(job):
            kind, l, m = job
            if kind == "p":
                return spill[36 * l + m - M_POOL]
            return spill[36 * l + {"ga": 4, "gb": 12, "g2a": 20, "g2b": 28}[kind] + m]

        sem, count, passed = sig.sem, sig.value, sig.passed

        def done(job):
            pool, n, _, _ = jobs[job]
            return sem(f"{pool}_done"), n + 1

        def bank_of(job):
            return psum[jobs[job][2]]

        def bank_read(job):
            return sem(f"bank{jobs[job][2]}_read")

        def turn(job):
            return jobs[job][3] + 1

        def moved(job):
            return bank_read(job), turn(job)

        def half(t, b, second):
            return t.rearrange("p (n s b) -> p n s b", s=2, b=b)[:, :, second, :]

        block = ctx.enter_context(nc.Block())

        @block.tensor
        def _(pe):
            seen = set()

            def begin(name, pool):
                n = used[pool]
                first, banks = BANKS[pool]
                b, uses = first + n % banks, n // banks
                if uses:
                    pe.wait_ge(sem(f"bank{b}_read"), uses)
                else:
                    sem(f"bank{b}_read")
                used[pool] += 1
                jobs[name] = (pool, n, b, uses)
                return psum[b]

            def done_sem(name):
                return sem(f"{jobs[name][0]}_done")

            def close(name):
                closed[name] = len(closed)
                for s in touched:
                    slab_end[s] = done(name)
                touched.clear()

            touched = set()

            def next_block(desc):
                if cursor["at"] == SLAB:
                    slabs.append([])
                    cursor["slab"], cursor["at"] = len(slabs) - 1, 0
                    pe.wait_ge(sem("slab_split"), len(slabs))
                s, i = cursor["slab"], cursor["at"]
                slabs[s].append(desc)
                cursor["at"] += 1
                touched.add(s)
                j = s % 2
                return w_hi[j][:, i, :], w_lo[j][:, i, :]

            def slab_left():
                touched.remove(cursor["slab"])
                slab_end[cursor["slab"]] = sem("slab_left"), passed("slab_left")

            def linear(name, blocks, hi, lo, ready):
                bank = begin(name, "lin")
                for i, desc in enumerate(blocks):
                    wh, wl = next_block(desc)
                    step = ready(i)
                    if step not in seen:
                        seen.add(step)
                        pe.wait_ge(sem(step[0]), count(*step))
                    pe.matmul(bank[:], wh, hi[:, i, :], start=(i == 0), stop=False)
                    pe.matmul(bank[:], wh, lo[:, i, :], start=False, stop=False)
                    ins = pe.matmul(bank[:], wl, hi[:, i, :], start=False, stop=(i == len(blocks) - 1))
                    if cursor["at"] == SLAB and i < len(blocks) - 1:
                        ins.then_inc(sem("slab_left"), 1)
                        slab_left()
                ins.then_inc(done_sem(name), 1)
                close(name)

            def projection(name, matrix, l, m, ready, kt=DT, hi=in_hi, lo=in_lo, k0=0):
                linear(name, [(matrix, l, k0 + k, m) for k in range(kt)], hi, lo, ready)

            def group(members, ready):
                banks = [begin(name, "lin") for name, _, _, _ in members]
                for k in range(DT):
                    pe.wait_ge(sem(ready(k)[0]), count(*ready(k)))
                    seen.add(ready(k))
                    for (name, matrix, l, m), bank in zip(members, banks):
                        wh, wl = next_block((matrix, l, k, m))
                        pe.matmul(bank[:], wh, in_hi[:, k, :], start=(k == 0), stop=False)
                        pe.matmul(bank[:], wh, in_lo[:, k, :], start=False, stop=False)
                        ins = pe.matmul(bank[:], wl, in_hi[:, k, :], start=False, stop=(k == DT - 1))
                        if k == DT - 1:
                            ins.then_inc(done_sem(name), 1)
                            close(name)
                        elif cursor["at"] == SLAB:
                            ins.then_inc(sem("slab_left"), 1)
                            slab_left()

            side = {"jobs": [], "at": 0, "bank": None}

            def side_jobs(members):
                side["jobs"], side["at"] = members, 0

            def fill(n):
                for at in range(side["at"], min(side["at"] + n, DT * len(side["jobs"]))):
                    name, matrix, l, m = side["jobs"][at // DT]
                    k = at % DT
                    if k == 0:
                        side["bank"] = begin(name, "bg")
                    bank = side["bank"]
                    wh, wl = next_block((matrix, l, k, m))
                    pe.matmul(bank[:], wh, in_hi[:, k, :], start=(k == 0), stop=False)
                    pe.matmul(bank[:], wh, in_lo[:, k, :], start=False, stop=False)
                    ins = pe.matmul(bank[:], wl, in_hi[:, k, :], start=False, stop=(k == DT - 1))
                    if k == DT - 1:
                        ins.then_inc(done_sem(name), 1)
                        close(name)
                    elif cursor["at"] == SLAB:
                        ins.then_inc(sem("slab_left"), 1)
                        slab_left()
                    side["at"] = at + 1

            def ones_sum(name, src, which, ready=None):
                bank = begin(name, "aux")
                if ready:
                    pe.wait_ge(sem(ready[0]), count(*ready))
                pe.matmul(bank[:], kst[:, which, :], src, start=True, stop=True).then_inc(done_sem(name), 1)
                close(name)

            def token_sums(bank, src, first, last):
                for t in range(NCH):
                    ins = pe.matmul(bank[:, t:t + 1], src[:, t * P:(t + 1) * P], kst[:, K_ONES, 0:1],
                                    start=(first and t == 0), stop=last, skip_group_check=True)
                return ins

            def norm_sum(key, parts=False):
                name = ("norm", key)
                bank = begin(name, "aux")
                if parts:
                    for i in range(DT):
                        pe.wait_ge(sem("sq_ready"), count("sq_ready", (key, i)))
                        ins = token_sums(bank, sq_[i % 2], i == 0, i == DT - 1)
                        if i < DT - 1:
                            ins.then_inc(sem("sq_used"), 1)
                            passed("sq_used", (key, i))
                else:
                    pe.wait_ge(sem("ssq_ready"), count("ssq_ready", key))
                    ins = token_sums(bank, ssq, True, True)
                ins.then_inc(done_sem(name), 1)
                close(name)
                name = ("rs", key)
                bank = begin(name, "aux")
                pe.wait_ge(sem("diag_ready"), count("diag_ready", key))
                pe.matmul(bank[:], kst[:, K_ONES, :], diag[:].rearrange("p c t -> p (c t)"),
                          start=True, stop=True).then_inc(done_sem(name), 1)
                close(name)

            def wkv_chunk(l, c):
                cs = slice(c * P, (c + 1) * P)
                for i, src in enumerate((b_f, k_f, v_f)):
                    name = ("tok", l, c, i)
                    bank = begin(name, "aux")
                    pe.wait_ge(sem("wkv_in"), count("wkv_in", l))
                    for d in range(RT):
                        ins = pe.transpose(bank[:, d * P:(d + 1) * P], src[:, d, cs], kst[:, K_ID, :])
                    ins.then_inc(done_sem(name), 1)
                    close(name)
                for h in range(NH):
                    name = ("score", l, c, h)
                    d, rows = h // 2, slice(64 * (h % 2), 64 * (h % 2) + 64)
                    bank = begin(name, "aux")
                    rhs = qr[rows, d, :, cs]
                    pe.matmul(bank[:, 0:256].rearrange("p (a t) -> p a t", a=2), b_f[rows, d, cs], rhs,
                              start=True, stop=True)
                    pe.matmul(bank[:, 256:512].rearrange("p (a t) -> p a t", a=2),
                                        k_f[rows, d, cs], rhs, start=True, stop=True).then_inc(done_sem(name), 1)
                    close(name)
                for g in range(2):
                    name = ("inv_t", l, c, g)
                    bank = begin(name, "aux")
                    if g == 0:
                        fill(3)
                    pe.wait_ge(sem("mt_ready"), count("mt_ready", (l, c, g)))
                    for j in range(4):
                        ins = pe.transpose(bank[:, j * P:(j + 1) * P], mt[g][:, j, :], kst[:, K_ID, :])
                    ins.then_inc(done_sem(name), 1)
                    close(name)
                for v in range(1, len(LEVELS)):
                    last = v == len(LEVELS) - 1
                    for g in range(2):
                        name = ("am", l, c, g, v)
                        fill(1)
                        bank = begin(name, "aux")
                        pe.wait_ge(sem("bm_ready"), count("bm_ready", (l, c, g, v)))
                        pe.wait_ge(*moved(("mam", l, c, g, v - 1) if v > 1 else ("inv_t", l, c, g)))
                        for j in range(4):
                            ins = pe.matmul(bank[:, j * P:(j + 1) * P], bm[g][:, j, :], mi[g][:, j, :],
                                            start=True, stop=True)
                        ins.then_inc(done_sem(name), 1)
                        close(name)
                    for g in range(2):
                        pe.wait_ge(*moved(("am", l, c, g, v)))
                        if v > 1:
                            pe.wait_ge(*moved(("mamt", l, c, g, v - 1)))
                        if not last:
                            name = ("mam", l, c, g, v)
                            bank = begin(name, "aux")
                            for j in range(4):
                                ins = pe.matmul(half(bank[:, j * P:(j + 1) * P], LEVELS[v], 0), mt[g][:, j, :],
                                                half(gm[g][:, j, :], LEVELS[v], 0), start=True, stop=True)
                            ins.then_inc(done_sem(name), 1)
                            close(name)
                        name = ("mamt", l, c, g, v)
                        bank = begin(name, "aux")
                        for j in range(4):
                            ins = pe.matmul(half(bank[:, j * P:(j + 1) * P], LEVELS[v], 1), gm[g][:, j, :],
                                            half(mt[g][:, j, :], LEVELS[v], 1), start=True, stop=True)
                        ins.then_inc(done_sem(name), 1)
                        close(name)
                fill(1)
                name = ("w0", l, c)
                bank = begin(name, "aux")
                pe.wait_ge(*moved(("tok", l, c, 2)))
                if c:
                    pe.wait_ge(sem("state_ready"), count("state_ready", (l, c)))
                for h in range(NH):
                    d, hc = h // 2, slice(64 * h, 64 * h + 64)
                    if c and h % 2 == 0:
                        pe.matmul(bank[:, d * P:(d + 1) * P], qr[:, d, 0, cs], st[:, d, :], start=True, stop=False)
                    ins = pe.matmul(bank[:, hc], units[:, h, 2, :], tok[2][:, hc], start=(c == 0),
                                    stop=(c == 0 or h % 2 == 1))
                ins.then_inc(done_sem(name), 1)
                close(name)
                name = ("u", l, c)
                fill(2)
                bank = begin(name, "aux")
                pe.wait_ge(*moved(("w0", l, c)))
                for g in range(2):
                    pe.wait_ge(*moved(("mamt", l, c, g, len(LEVELS) - 1)))
                for h in range(NH):
                    hc = slice(64 * h, 64 * h + 64)
                    ins = pe.matmul(bank[:, hc], mt[h // 4][:, h % 4, :], u0[:, hc], start=True, stop=True)
                ins.then_inc(done_sem(name), 1)
                close(name)
                fill(2)
                pe.wait_ge(*moved(("u", l, c)))
                if c < NCH - 1:
                    name = ("state", l, c)
                    bank = begin(name, "aux")
                    for h in range(NH):
                        d, rows, hc = h // 2, slice(64 * (h % 2), 64 * (h % 2) + 64), slice(64 * h, 64 * h + 64)
                        o = bank[rows, d * 64:d * 64 + 64]
                        pe.matmul(o, tok[0][:, hc], u1[:, hc], start=True, stop=False)
                        ins = pe.matmul(o, tok[1][:, hc], tok[2][:, hc], start=False, stop=True)
                    ins.then_inc(done_sem(name), 1)
                    close(name)
                name = ("y", l, c)
                bank = begin(name, "aux")
                for h in range(NH):
                    d, rows, hc = h // 2, slice(64 * (h % 2), 64 * (h % 2) + 64), slice(64 * h, 64 * h + 64)
                    o = bank[rows, d * P:(d + 1) * P]
                    if c and h % 2 == 0:
                        pe.matmul(bank[:, d * P:(d + 1) * P], st[:, d, :], qr[:, d, 1, cs], start=True, stop=False)
                    pe.matmul(o, u1[:, hc], units[:, h, 1, :], start=(c == 0), stop=False)
                    ins = pe.matmul(o, tok[2][:, hc], units[:, h, 3, :], start=False, stop=True)
                ins.then_inc(done_sem(name), 1)
                close(name)

            def block1(l):
                h_in = lambda i: ("split_ready", ("n1", l, i))
                norm_sum(("n1", l), parts=(l == 0))
                group([(("p", l, m), "w_in", l, m) for m in (M_WA, M_GL, M_GLV)], h_in)
                projection(("p", l, M_K), "w_in", l, M_K, h_in)
                pe.wait_ge(sem("small_in"), count("small_in", ("b1", l)))
                for d in range(RT):
                    for name, rows, ready in ((("zw", l, d), slice(0, 64), ("tanh_ready", l)),
                                              (("za", l, d), slice(64, 128), ("ps_ready", (l, M_WA)))):
                        bank = begin(name, "aux")
                        pe.wait_ge(sem(ready[0]), count(*ready))
                        pe.matmul(bank[:], sml[rows, 0, d * P:(d + 1) * P], wa[rows, :],
                                            start=True, stop=True).then_inc(done_sem(name), 1)
                        close(name)
                    if l:
                        name = ("zv", l, d)
                        bank = begin(name, "aux")
                        pe.wait_ge(sem("ps_ready"), count("ps_ready", (l, M_GLV)))
                        pe.matmul(bank[:], sml[32:64, 2, d * P:(d + 1) * P], gl_s[32:64, 1, :],
                                            start=True, stop=True).then_inc(done_sem(name), 1)
                        close(name)
                for m in range(M_K + 1, M_K + RT):
                    projection(("p", l, m), "w_in", l, m, h_in)
                for d in range(RT):
                    ones_sum(("kk", l, d), tmp[:, d, :], K_HEADS, ("kksq_ready", (l, d)))
                    projection(("p", l, M_R + d), "w_in", l, M_R + d, h_in)
                for d in range(RT):
                    projection(("p", l, M_V + d), "w_in", l, M_V + d, h_in)
                    ones_sum(("rk", l, d), tmp[:, d, :], K_HEADS, ("rk_ready", (l, d)))
                side_jobs([(("p", l, M_POOL + d), "w_in", l, M_POOL + d) for d in range(4)]
                          + [((n, l, m), "w_in", l, m0 + m) for m in range(DT) for n, m0 in (("ga", M_GA), ("gb", M_GB))])
                fill(FILL_PREP)
                for c in range(NCH):
                    wkv_chunk(l, c)
                windows_at.append(len(slabs))
                for d in range(RT):
                    pe.wait_ge(*moved(("y", l, NCH - 1)))
                    ones_sum(("mean", l, d), qr[:, d, 1, :], K_HEADS)
                    fill(10)
                    ones_sum(("var", l, d), yt[d % 2][:], K_HEADS, ("var_ready", (l, d)))
                    name = ("g", l, d)
                    bank = begin(name, "aux")
                    pe.wait_ge(sem("sgl_ready"), count("sgl_ready", l))
                    pe.matmul(bank[:], sml[:, 1, d * P:(d + 1) * P], gl_s[:, 0, :], start=True, stop=False)
                    pe.matmul(bank[:], sml[0:32, 2, d * P:(d + 1) * P], gl_s[0:32, 1, :],
                                        start=False, stop=True).then_inc(done_sem(name), 1)
                    close(name)
                for d in range(4):
                    name = ("pool", l, d)
                    bank = begin(name, "aux")
                    pe.wait_ge(sem("pooled_ready"), count("pooled_ready", (l, d)))
                    pe.matmul(bank[:], sml[:, 3, d * P:(d + 1) * P], zp[:, d, 16:528],
                                        start=True, stop=True).then_inc(done_sem(name), 1)
                    close(name)
                fill(4 * DT * (2 * DT + 4))
                for m in range(DT):
                    projection(("pa", l, m), "proj_a", l, m, lambda i: ("split_ready", ("ya", l, i)),
                               kt=RT, hi=ya_hi, lo=ya_lo)
                    projection(("pb", l, m), "proj_b", l, m, lambda i: ("split_ready", ("yb", l, i)),
                               kt=4, hi=yb_hi, lo=yb_lo)
                for m in range(DT):
                    projection(("wo", l, m), "w_out", l, m, lambda i: ("split_ready", ("mx", l, i)),
                               hi=mx_hi, lo=mx_lo)
                if l == 0:
                    ada_issue[1] = len(slabs)
                norm_sum(("n2", l))
                h_in = lambda i: ("split_ready", ("n2", l, i))
                group([(("fg", l, 0), "w_gu", l, 0), (("fu", l, 0), "w_gu", l, HT), (("fg", l, 1), "w_gu", l, 1)], h_in)
                for f in range(2):
                    for m in range(HALF):
                        mm = f * HALF + m
                        if mm > 1:
                            projection(("fg", l, mm), "w_gu", l, mm, h_in)
                        if mm:
                            projection(("fu", l, mm), "w_gu", l, HT + mm, h_in)
                    for m in range(DT):
                        projection(("fd", l, f, m), "w_down", l, m,
                                   lambda i: ("split_ready", ("hid", l, f, i)),
                                   kt=HALF, hi=hid_hi, lo=hid_lo, k0=f * HALF)

            for l in range(DEPTH):
                block1(l)
            norm_sum(("nf", 0))

            def token_major(name, l, matrix, m0):
                cursor["at"] = SLAB
                parts = [[next_block((matrix, l, k, m0 + j)) for j in range(2)] for k in range(DT)]
                s, j = cursor["slab"], cursor["slab"] % 2
                for t in range(NCH):
                    ts_ = slice(t * P, (t + 1) * P)
                    bank = begin(name + (t,), "lin")
                    for k in range(DT):
                        wh, wl = w_hi[j][:, 2 * k:2 * k + 2, :], w_lo[j][:, 2 * k:2 * k + 2, :]
                        o = bank[:, 0:256].rearrange("p (a c) -> p a c", a=2)
                        pe.matmul(o, in_hi[:, k, ts_], wh, start=(k == 0), stop=False)
                        pe.matmul(o, in_hi[:, k, ts_], wl, start=False, stop=False)
                        ins = pe.matmul(o, in_lo[:, k, ts_], wh, start=False, stop=(k == DT - 1))
                    touched.add(s)
                    ins.then_inc(done_sem(name + (t,)), 1)
                    close(name + (t,))

            def gla_in(l, h, h_in):
                if h:
                    projection(("gq", l, h), "w_in2", l, N_GQ + h, h_in)
                    projection(("gk", l, h), "w_in2", l, N_GK + h, h_in)
                token_major(("gv", l, h), l, "w_in2", N_GV + 2 * h)
                for j in range(2):
                    projection(("gg", l, h, j), "w_in2", l, N_GG + 2 * h + j, h_in)

            def gla_decay(l, h):
                pe.wait_ge(sem("small_in"), count("small_in", ("b2", l)))
                pe.wait_ge(*moved(("ra", l)))
                for i in range(2):
                    name = ("gz", l, h, i)
                    if i and h:
                        fill(3)
                    bank = begin(name, "lin")
                    rows = slice(32 * i, 32 * i + 16)
                    ins = pe.matmul(bank[:], sml[rows, 0, h * P:(h + 1) * P], ra[rows, :], start=True, stop=True)
                    ins.then_inc(done_sem(name), 1)
                    close(name)

            def gla_core(l, h):
                v = gv[h % 2]
                fill(8 if h < GH - 1 else 16)
                pe.wait_ge(sem("qd_ready"), count("qd_ready", (l, h)))
                for i in range(2):
                    name = ("gkt", l, h, i)
                    bank = begin(name, "aux")
                    for c in range(NCH):
                        ins = pe.transpose(bank[:, c * P:(c + 1) * P], kd[i][:, c, :], kst[:, K_ID, :])
                    ins.then_inc(done_sem(name), 1)
                    close(name)
                for i in range(2):
                    name = ("gsc", l, h, i)
                    bank = begin(name, "aux")
                    for c in range(NCH):
                        ins = pe.matmul(bank[:, c * P:(c + 1) * P], kd[i][:, c, :], qd[i][:, c, :],
                                        start=True, stop=True)
                    ins.then_inc(done_sem(name), 1)
                    close(name)
                pe.wait_ge(*moved(("gkt", l, h, 1)))
                pe.wait_ge(*moved(("gv", l, h, NCH - 1)))
                for n in range(NCH - 1):
                    name = ("gst", l, h, n)
                    bank = begin(name, "aux")
                    pe.matmul(bank[:, 0:GDV], kt_[0][:, n, :], v[:, n, :], start=True, stop=True)
                    c = NCH - 1 - n
                    ins = pe.matmul(bank[:, GDV:2 * GDV], kt_[1][:, c, :], v[:, c, :], start=True, stop=True)
                    ins.then_inc(done_sem(name), 1)
                    close(name)
                fill(3)
                pe.wait_ge(sem("sc_ready"), count("sc_ready", (l, h)))
                for j in range(2):
                    name = ("go", l, h, j)
                    vs = slice(j * P, (j + 1) * P)
                    bank = begin(name, "aux")
                    pe.wait_ge(sem("gs_ready"), count("gs_ready", (l, h)))
                    for c in range(NCH):
                        o = bank[:, c * P:(c + 1) * P]
                        pe.matmul(o, v[:, c, vs], sc[:, c, :], start=True, stop=False)
                        if c:
                            ins = pe.matmul(o, gs[0][:, c - 1, vs], qd[0][:, c, :], start=False, stop=(c == NCH - 1))
                        if c < NCH - 1:
                            ins = pe.matmul(o, gs[1][:, NCH - 2 - c, vs], qd[1][:, c, :], start=False, stop=True)
                    ins.then_inc(done_sem(name), 1)
                    close(name)
                name = ("gn", l, h)
                fill(2)
                bank = begin(name, "aux")
                pe.wait_ge(sem("osq_ready"), count("osq_ready", (l, h)))
                pe.matmul(bank[:], kst[:, K_ONES, :], osq[:, 0, :], start=True, stop=False)
                ins = pe.matmul(bank[:], kst[:, K_ONES, :], osq[:, 1, :], start=False, stop=True)
                ins.then_inc(done_sem(name), 1)
                close(name)

            def rope_sum(key):
                ones_sum(("qs",) + key, asq[:], K_ONES, ("asq_ready", key))

            def rope_turn(key):
                name = ("rot",) + key
                bank = begin(name, "aux")
                pe.wait_ge(sem("qn_ready"), count("qn_ready", key))
                pe.matmul(bank[:], kst[:, K_ROT, :], qn[:], start=True, stop=True).then_inc(done_sem(name), 1)
                close(name)

            def block2(l):
                h_in = lambda i: ("split_ready", ("m1", l, i))
                norm_sum(("m1", l), parts=True)
                group([(("ra", l), "w_in2", l, N_RA), (("gq", l, 0), "w_in2", l, N_GQ),
                       (("gk", l, 0), "w_in2", l, N_GK)], h_in)
                side_jobs([(("g2a", l, m), "w_in2", l, N_GA + m) for m in range(DT)])
                gla_in(l, 0, h_in)
                gla_decay(l, 0)
                for h in range(GH):
                    if h + 1 < GH:
                        gla_in(l, h + 1, h_in)
                    gla_core(l, h)
                    if h + 1 < GH:
                        gla_decay(l, h + 1)
                fill(DT * DT)
                for m in range(DT):
                    projection(("p2a", l, m), "w_o_gla", l, m, lambda i: ("split_ready", ("go", l, i)),
                               hi=go_hi, lo=go_lo)
                side_jobs([(("g2b", l, m), "w_in2", l, N_GB + m) for m in range(DT)])
                for i in range(KVH):
                    projection(("k", l, i), "w_in2", l, N_AK + i, h_in)
                    fill(1)
                    rope_sum(("k", l, i))
                    fill(5)
                    rope_turn(("k", l, i))
                token_major(("av", l), l, "w_in2", N_AV)
                projection(("q", l, 0), "w_in2", l, N_AQ, h_in)
                fill(1)
                rope_sum(("q", l, 0))
                fill(5)
                rope_turn(("q", l, 0))
                fill(2)
                for h in range(QH):
                    kv = h // (QH // KVH)
                    for t in range(NCH):
                        name = ("as", l, h, t)
                        bank = begin(name, "aux")
                        pe.wait_ge(sem("rope_ready"), count("rope_ready", ("q", l, h)))
                        pe.matmul(bank[:], aq[h % 2][:, t * P:(t + 1) * P], ak[:, kv, :],
                                            start=True, stop=True).then_inc(done_sem(name), 1)
                        close(name)
                    if h + 1 < QH:
                        projection(("q", l, h + 1), "w_in2", l, N_AQ + h + 1, h_in)
                        rope_sum(("q", l, h + 1))
                    for t in range(NCH):
                        name = ("pt", l, h, t)
                        fill(1)
                        bank = begin(name, "aux")
                        pe.wait_ge(sem("pr_ready"), count("pr_ready", (l, h, t)))
                        for k in range(NCH):
                            ins = pe.transpose(bank[:, k * P:(k + 1) * P], pr[:, t, k * P:(k + 1) * P],
                                               kst[:, K_ID, :])
                        ins.then_inc(done_sem(name), 1)
                        close(name)
                    if h + 1 < QH:
                        fill(2)
                        rope_turn(("q", l, h + 1))
                    name = ("pv", l, h)
                    bank = begin(name, "aux")
                    pe.wait_ge(*moved(("pt", l, h, NCH - 1)))
                    pe.wait_ge(*moved(("av", l, NCH - 1)))
                    for k in range(NCH):
                        ins = pe.matmul(bank[:], av[:, k, kv * P:(kv + 1) * P], prt[:, k, :],
                                        start=(k == 0), stop=(k == NCH - 1))
                    ins.then_inc(done_sem(name), 1)
                    close(name)
                fill(DT * DT)
                for m in range(DT):
                    projection(("p2b", l, m), "w_o_attn", l, m, lambda i: ("split_ready", ("ao", l, i)),
                               hi=ao_hi, lo=ao_lo)
                for m in range(DT):
                    projection(("wo2", l, m), "w_out2", l, m, lambda i: ("split_ready", ("m2", l, i)),
                               hi=m2_hi, lo=m2_lo)
                norm_sum(("m2", l))
                norm_sum(("m3", l), parts=True)
                h_in3 = lambda i: ("split_ready", ("m3", l, i))
                group([(("eg", l, 0), "w_ffn_in", l, 0), (("eu", l, 0), "w_ffn_in", l, HT),
                       (("eg", l, 1), "w_ffn_in", l, 1)], h_in3)
                for f in range(2):
                    for m in range(HALF):
                        mm = f * HALF + m
                        if mm > 1:
                            projection(("eg", l, mm), "w_ffn_in", l, mm, h_in3)
                        if mm:
                            projection(("eu", l, mm), "w_ffn_in", l, HT + mm, h_in3)
                    for m in range(DT):
                        projection(("ed", l, f, m), "w_ffn_out", l, m,
                                   lambda i: ("split_ready", ("h2", l, f, i)),
                                   kt=HALF, hi=h2_hi, lo=h2_lo, k0=f * HALF)
                for m in range(DT):
                    projection(("pe", l, m), "w_ple_proj", l, m, lambda i: ("split_ready", ("pp", l, i)),
                               kt=2, hi=pp_hi, lo=pp_lo)
                norm_sum(("m4", l))
                h_pl = lambda i: ("split_ready", ("pl", l, i))
                group([(("pg", l, m), "w_ple_gate", l, m) for m in range(3)], h_pl)
                for m in range(3, DT):
                    projection(("pg", l, m), "w_ple_gate", l, m, h_pl)
                norm_sum(("m5", l))

            for l in range(DEPTH):
                block2(l)

        @block.scalar
        def _(act):
            af = act.activation
            def load_small(l, which):
                act.dma_start(sml[:], small[l + 2 * which]).then_inc(sem("small_in"), 16)
                passed("small_in", (("b1", "b2")[which], l), by=16)

            act.dma_start(c_act[:], c_rows).then_inc(sem("const_in"), 16)
            act.dma_start(col[:], cols).then_inc(sem("const_in"), 16)
            act.dma_start(kst[:], consts).then_inc(sem("const_in"), 16)
            act.dma_start(inv_cnt[:], inv_count).then_inc(sem("const_in"), 16)
            act.wait_ge(sem("const_in"), 64)
            af(c_act[:], c_act[:], ACT.Silu).then_inc(sem("c_ready"), 1)
            act.wait_ge(sem("c_ready"), passed("c_ready", 0))
            load_small(0, 0)
            act.wait_ge(sem("eps_ready"), count("eps_ready", 0))

            def col1(l, name, i):
                o = l * W1C + C1[name] + i
                return col[:, o:o + 1]

            def col2(l, name, i):
                o = 2 * W1C + 8 + l * W2C + C2[name] + i
                return col[:, o:o + 1]

            def root(job, dst, scale, e):
                act.wait_ge(*done(job))
                af(dst, bank_of(job)[:], ACT.Sqrt, bias=eps[:, e:e + 1], scale=scale).then_inc(bank_read(job), 1)
                act.wait_ge(bank_read(job), turn(job))

            def norm_root(key):
                job = ("norm", key)
                act.wait_ge(*done(job))
                ins = af(root4[:], bank_of(job)[:, 0:NCH], ACT.Sqrt, bias=eps[:, 0:1], scale=1.0 / D)
                ins.then_inc(bank_read(job), 1)
                act.wait_ge(bank_read(job), turn(job))

            def high_parts(key, shift_of=None):
                for i in range(DT):
                    if i < DT - 1:
                        act.wait_ge(sem("nt_ready"), count("nt_ready", (key, i)))
                    else:
                        act.wait_ge(*moved(("rs", key)))
                    if shift_of:
                        ins = af(in_hi[:, i, :], nts[i % 2][:], ACT.Identity, bias=shift_of(i))
                    else:
                        ins = af(in_hi[:, i, :], nts[i % 2][:], ACT.Copy)
                    ins.then_inc(sem("hi_ready"), 1)
                    act.wait_ge(sem("hi_ready"), passed("hi_ready", (key, i)))

            def squares(key, last=None):
                for i in range(DT):
                    if key == ("n1", 0):
                        act.wait_ge(sem("x_in"), 16)
                    elif last and i == DT - 1:
                        act.wait_ge(*moved(last))
                    else:
                        act.wait_ge(sem("x_tile"), count("x_tile", (key, i)))
                    if i >= 2:
                        act.wait_ge(sem("sq_used"), count("sq_used", (key, i - 2)))
                    af(sq_[i % 2][:], x[:, i, :], ACT.Square).then_inc(sem("sq_ready"), 1)
                    act.wait_ge(sem("sq_ready"), passed("sq_ready", (key, i)))

            side_order = [job for job in closed if jobs[job][0] == "bg"]
            stored = [0]

            def gates_before(job, stage):
                while stored[0] < len(side_order) and closed[side_order[stored[0]]] < closed[job]:
                    gate = side_order[stored[0]]
                    act.wait_ge(*done(gate))
                    if stored[0]:
                        act.wait_ge(sem("gate_out"), 16 * stored[0])
                    ins = af(stage[:], bank_of(gate)[:], ACT.Copy if gate[0] == "p" else ACT.Sigmoid)
                    ins.then_inc(bank_read(gate), 1)
                    act.wait_ge(bank_read(gate), turn(gate))
                    act.dma_start(spilled(gate), stage[:]).then_inc(sem("gate_out"), 16)
                    passed("gate_out", gate, by=16)
                    stored[0] += 1

            def gate_back(dst, gate):
                which = f"gate_in{gate[2] % 2}"
                act.dma_start(dst, spilled(gate)).then_inc(sem(which), 16)
                passed(which, gate, by=16)

            def evac_shift(l, m, n):
                if n >= 2:
                    act.wait_ge(sem("ps_ready"), count("ps_ready", (l, order1[n - 2])))
                job = ("p", l, m)
                act.wait_ge(*done(job))
                af(zbuf[n % 2][:, ZPAD:ZPAD + T], bank_of(job)[:], ACT.Copy).then_inc(bank_read(job), 1)
                act.wait_ge(bank_read(job), turn(job))

            def block1(l):
                if l == 0:
                    squares(("n1", 0))
                norm_root(("n1", l))
                high_parts(("n1", l), lambda i: mod[:, i:i + 1])
                for n in range(3):
                    act.wait_ge(sem("zpad_ready"), count("zpad_ready", l))
                    evac_shift(l, order1[n], n)
                act.wait_ge(sem("ps_ready"), count("ps_ready", (l, M_WA)))
                af(wa[0:64, :], wa[0:64, :], ACT.Tanh).then_inc(sem("tanh_ready"), 1)
                act.wait_ge(sem("tanh_ready"), passed("tanh_ready", l))
                for d in range(RT):
                    job = ("zw", l, d)
                    act.wait_ge(*done(job))
                    af(sgw[:, d, :], bank_of(job)[:], ACT.Sigmoid, bias=col1(l, "w0", d)).then_inc(bank_read(job), 1)
                    act.wait_ge(bank_read(job), turn(job))
                    job = ("za", l, d)
                    act.wait_ge(*done(job))
                    af(b_f[:, d, :], bank_of(job)[:], ACT.Sigmoid, bias=col1(l, "a0", d)).then_inc(bank_read(job), 1)
                    act.wait_ge(bank_read(job), turn(job))
                    if l:
                        job = ("zv", l, d)
                        act.wait_ge(*done(job))
                        ins = af(gate_v[:, d, :], bank_of(job)[:], ACT.Sigmoid, bias=col1(l, "v0", d))
                        ins.then_inc(bank_read(job), 1)
                        act.wait_ge(bank_read(job), turn(job))
                act.wait_ge(sem("ps_ready"), count("ps_ready", (l, M_GLV)))
                af(gl_s[:, 0, :], gl_s[:, 0, :], ACT.Sigmoid).then_inc(sem("scalar_step"), 1)
                act.wait_ge(sem("scalar_step"), passed("scalar_step"))
                af(gl_s[0:32, 1, :], gl_s[0:32, 1, :], ACT.Sigmoid).then_inc(sem("sgl_ready"), 1)
                act.wait_ge(sem("sgl_ready"), passed("sgl_ready", l))
                for n in range(3, 7):
                    evac_shift(l, order1[n], n)
                act.wait_ge(sem("lcum_ready"), count("lcum_ready", l))
                af(sscal[:], sscal[:], ACT.Exp, scale=-EXP_MHALF).then_inc(sem("scalar_step"), 1)
                act.wait_ge(sem("scalar_step"), passed("scalar_step"))
                for d in range(RT):
                    root(("kk", l, d), tmp[:, d, :], 1.0, 3)
                    af(sgw[:, d, :], sgw[:, d, :], ACT.Exp, scale=-EXP_MHALF).then_inc(sem("scalar_step"), 1)
                    act.wait_ge(sem("scalar_step"), passed("scalar_step"))
                    if d >= 2:
                        act.wait_ge(sem("r_ready"), count("r_ready", (l, d - 2)))
                    ins = af(e_neg[d % 2][:], lcum[:, d, :], ACT.Exp, scale=-EXP_MHALF)
                    ins.then_inc(sem("scalar_step"), 1)
                    act.wait_ge(sem("scalar_step"), passed("scalar_step"))
                    ins = af(lcum[:, d, :], lcum[:, d, :], ACT.Exp, scale=EXP_MHALF)
                    ins.then_inc(sem("decay_ready"), 1)
                    act.wait_ge(sem("decay_ready"), passed("decay_ready", (l, d)))
                    evac_shift(l, order1[7 + d], 7 + d)
                for d in range(RT):
                    evac_shift(l, order1[11 + d], 11 + d)
                act.wait_ge(sem("r_ready"), count("r_ready", (l, RT - 1)))
                for c in range(NCH):
                    for i in range(3):
                        job = ("tok", l, c, i)
                        gates_before(job, gate_st)
                        act.wait_ge(*done(job))
                        bank = bank_of(job)
                        if i == 0 and c == 0:
                            act.wait_ge(sem("wkv_in"), count("wkv_in", l))
                        af(tok[i][:], bank[:], ACT.Copy).then_inc(bank_read(job), 1)
                        act.wait_ge(bank_read(job), turn(job))
                    for g in range(2):
                        job = ("inv_t", l, c, g)
                        gates_before(job, gate_st)
                        act.wait_ge(*done(job))
                        af(mi[g][:], bank_of(job)[:], ACT.Copy).then_inc(bank_read(job), 1)
                        act.wait_ge(bank_read(job), turn(job))
                    for v in range(1, len(LEVELS)):
                        for g in range(2):
                            job = ("am", l, c, g, v)
                            gates_before(job, gate_st)
                            act.wait_ge(*done(job))
                            af(gm[g][:], bank_of(job)[:], ACT.Copy).then_inc(bank_read(job), 1)
                            act.wait_ge(bank_read(job), turn(job))
                    job = ("w0", l, c)
                    gates_before(job, gate_st)
                    act.wait_ge(*done(job))
                    bank = bank_of(job)
                    af(u0[:], bank[:], ACT.Copy).then_inc(bank_read(job), 1)
                    act.wait_ge(bank_read(job), turn(job))
                    job = ("u", l, c)
                    gates_before(job, gate_st)
                    act.wait_ge(*done(job))
                    af(u1[:], bank_of(job)[:], ACT.Copy, scale=-1.0).then_inc(bank_read(job), 1)
                    act.wait_ge(bank_read(job), turn(job))
                    job = ("y", l, c)
                    gates_before(job, gate_st)
                    act.wait_ge(*done(job))
                    bank = bank_of(job)
                    ins = af(qr[:, :, 1, c * P:(c + 1) * P], bank[:].rearrange("p (d t) -> p d t", d=RT), ACT.Copy)
                    ins.then_inc(bank_read(job), 1)
                    act.wait_ge(bank_read(job), turn(job))
                act.wait_ge(sem("gate_out"), count("gate_out", ("p", l, M_POOL + 3)))
                for d in range(4):
                    act.dma_start(zp[:, d, 16:528], spilled(("p", l, M_POOL + d))).then_inc(sem("zp_in"), 16)
                    passed("zp_in", (l, d), by=16)
                for d in range(RT):
                    gates_before(("var", l, d), gate_st)
                    root(("var", l, d), yr[d % 2][:], 1.0 / HEAD, 1)
                gates_before(("pool", l, 0), gate_st)
                act.wait_ge(sem("split_ready"), count("split_ready", ("ya", l, RT - 1)))
                for d in range(4):
                    job = ("pool", l, d)
                    if d >= 2:
                        act.wait_ge(sem("split_ready"), count("split_ready", ("yb", l, d - 2)))
                    act.wait_ge(*done(job))
                    ins = af(mt_[d % 2][:], bank_of(job)[:], ACT.Copy, scale=col1(l, "pool_scale", d))
                    ins.then_inc(bank_read(job), 1)
                    act.wait_ge(bank_read(job), turn(job))
                load_small(*((1, 0) if l == 0 else (0, 1)))
                gates_before(("pa", l, 0), gate_st)
                act.wait_ge(sem("gate_out"), count("gate_out", ("gb", l, DT - 1)))
                for m in range(DT):
                    if m >= 2:
                        act.wait_ge(sem("split_ready"), count("split_ready", ("mx", l, m - 2)))
                    gate_back(gin[m % 2][0][:], ("ga", l, m))
                    gate_back(gin[m % 2][1][:], ("gb", l, m))
                if l == 0:
                    act.wait_ge(*done(("wo", l, DT - 1)))
                    act.dma_start(c_act[:], c_rows).then_inc(sem("c_in"), 16)
                norm_root(("n2", l))
                high_parts(("n2", l), lambda i: mod[:, 24 + i:25 + i])
                if l == 0:
                    act.wait_ge(sem("c_in"), 16)
                    af(c_act[:], c_act[:], ACT.Silu).then_inc(sem("c_ready"), 1)
                    act.wait_ge(sem("c_ready"), passed("c_ready", 1))
                ffn(l, "f", "hid")

            def ffn(l, tag, hid):
                for f in range(2):
                    for m in range(HALF):
                        mm = f * HALF + m
                        job = (tag + "g", l, mm)
                        if mm >= 2:
                            act.wait_ge(sem("split_ready"), count("split_ready", (hid, l, (mm - 2) // HALF, (mm - 2) % HALF)))
                        act.wait_ge(*done(job))
                        af(hs[mm % 2][:, 0, :], bank_of(job)[:], ACT.Silu).then_inc(bank_read(job), 1)
                        act.wait_ge(bank_read(job), turn(job))

            for l in range(DEPTH):
                block1(l)
            norm_root(("nf", 0))
            squares(("m1", 0), ("rs", ("nf", 0)))

            def gla_in(l, h):
                if h >= 2:
                    act.wait_ge(sem("qd_ready"), count("qd_ready", (l, h - 2)))
                for job, dst in ((("gq", l, h), gq[h % 2]), (("gk", l, h), gk[h % 2])):
                    gates_before(job, gate_st2)
                    act.wait_ge(*done(job))
                    af(dst[:], bank_of(job)[:], ACT.Copy).then_inc(bank_read(job), 1)
                    act.wait_ge(bank_read(job), turn(job))
                for t in range(NCH):
                    job = ("gv", l, h, t)
                    gates_before(job, gate_st2)
                    act.wait_ge(*done(job))
                    af(gv[h % 2][:, t, :], bank_of(job)[:, 0:GDV], ACT.Copy).then_inc(bank_read(job), 1)
                    act.wait_ge(bank_read(job), turn(job))
                if h >= 2:
                    act.wait_ge(sem("split_ready"), count("split_ready", ("go", l, 2 * (h - 2) + 1)))
                for j in range(2):
                    job = ("gg", l, h, j)
                    gates_before(job, gate_st2)
                    act.wait_ge(*done(job))
                    af(sg[h % 2][:, j, :], bank_of(job)[:], ACT.Silu).then_inc(bank_read(job), 1)
                    act.wait_ge(bank_read(job), turn(job))

            def gla_decay(l, h):
                flat = lambda t: t[:].rearrange("p c t -> p (c t)")
                for i in range(2):
                    gates_before(("gz", l, h, i), gate_st2)
                    act.wait_ge(*done(("gz", l, h, i)))
                    ins = af(flat(ln[i]), bank_of(("gz", l, h, i))[:], ACT.Abs, bias=col2(l, "b_alpha", 4 * i + h))
                    ins.then_inc(sem("abs_ready"), 1)
                    act.wait_ge(sem("abs_ready"), passed("abs_ready", (l, h, i)))
                for i in range(2):
                    af(ln[i][:], ln[i][:], ACT.Exp, scale=-1.0).then_inc(sem("scalar_step"), 1)
                    act.wait_ge(sem("scalar_step"), passed("scalar_step"))
                for i in range(2):
                    af(ln[i][:], ln[i][:], ACT.Ln, bias=eps[:, 2:3]).then_inc(sem("log_ready"), 1)
                    act.wait_ge(sem("log_ready"), passed("log_ready", (l, h, i)))

            def gla_core(l, h):
                if h == GH - 1:
                    gates_before(("gkt", l, h, 0), gate_st2)
                for i in range(2):
                    s = (1.0, -1.0)[i] / TAU
                    act.wait_ge(sem("cum_ready"), count("cum_ready", (l, h, i)))
                    af(la[i][:], ln[i][:], ACT.Exp, scale=s).then_inc(sem("scalar_step"), 1)
                    act.wait_ge(sem("scalar_step"), passed("scalar_step"))
                    af(ln[i][:], ln[i][:], ACT.Exp, scale=-s).then_inc(sem("scalar_step"), 1)
                    act.wait_ge(sem("scalar_step"), passed("scalar_step"))
                    af(dsc[i][:], dsc[i][:], ACT.Exp, scale=1.0 / TAU).then_inc(sem("ed_ready"), 1)
                    act.wait_ge(sem("ed_ready"), passed("ed_ready", (l, h, i)))
                for i in range(2):
                    job = ("gkt", l, h, i)
                    gates_before(job, gate_st2)
                    act.wait_ge(*done(job))
                    af(kt_[i][:].rearrange("p c t -> p (c t)"), bank_of(job)[:], ACT.Copy).then_inc(bank_read(job), 1)
                    act.wait_ge(bank_read(job), turn(job))
                for j in range(2):
                    gates_before(("go", l, h, j), gate_st2)
                    act.wait_ge(*done(("go", l, h, j)))
                    ins = af(osq[:, j, :], bank_of(("go", l, h, j))[:], ACT.Square)
                    if j:
                        ins.then_inc(sem("osq_ready"), 1)
                        act.wait_ge(sem("osq_ready"), passed("osq_ready", (l, h)))
                    else:
                        ins.then_inc(sem("scalar_step"), 1)
                        act.wait_ge(sem("scalar_step"), passed("scalar_step"))
                gates_before(("gn", l, h), gate_st2)
                root(("gn", l, h), rsg[:], 1.0 / GDV, 0)

            def rope_in(key, n, before):
                if before:
                    act.wait_ge(sem("qn_ready"), count("qn_ready", before))
                gates_before(key, nt)
                act.wait_ge(*done(key))
                af(qraw[:], bank_of(key)[:], ACT.Copy).then_inc(bank_read(key), 1)
                act.wait_ge(bank_read(key), turn(key))
                af(asq[:], qraw[:], ACT.Square).then_inc(sem("asq_ready"), 1)
                act.wait_ge(sem("asq_ready"), passed("asq_ready", key))
                gates_before(("qs",) + key, nt)
                root(("qs",) + key, ars[:], 1.0 / P, 0)

            def block2(l):
                norm_root(("m1", l))
                high_parts(("m1", l))
                job = ("ra", l)
                act.wait_ge(*done(job))
                af(ra[:], bank_of(job)[:], ACT.Copy).then_inc(bank_read(job), 1)
                act.wait_ge(bank_read(job), turn(job))
                gla_in(l, 0)
                gla_decay(l, 0)
                for h in range(GH):
                    if h + 1 < GH:
                        gla_in(l, h + 1)
                    gla_core(l, h)
                    if h + 1 < GH:
                        gla_decay(l, h + 1)
                gates_before(("p2a", l, 0), gate_st2)
                act.wait_ge(sem("gate_out"), count("gate_out", ("g2a", l, DT - 1)))
                act.dma_start(rope_t[:], rope).then_inc(sem("rope_in"), 16)
                act.wait_ge(sem("split_ready"), count("split_ready", ("go", l, DT - 1)))
                for m in range(DT):
                    if m >= 2:
                        act.wait_ge(*moved(("p2a", l, m - 2)))
                    gate_back(mgs[m % 2][:], ("g2a", l, m))
                act.wait_ge(*moved(("p2a", l, DT - 1)))
                rope_in(("k", l, 0), 0, None)
                rope_in(("k", l, 1), 1, ("k", l, 0))
                for t in range(NCH):
                    job = ("av", l, t)
                    gates_before(job, nt)
                    act.wait_ge(*done(job))
                    af(av[:, t, :], bank_of(job)[:, 0:256], ACT.Copy).then_inc(bank_read(job), 1)
                    act.wait_ge(bank_read(job), turn(job))
                rope_in(("q", l, 0), 2, ("k", l, 1))
                for h in range(QH):
                    for t in range(NCH):
                        job = ("as", l, h, t)
                        gates_before(job, nt)
                        act.wait_ge(sem("max_ready"), count("max_ready", (l, h, t)))
                        act.wait_ge(*done(job))
                        af(pr[:, t, :], bank_of(job)[:], ACT.Exp, bias=stat[:, 0, t:t + 1],
                                scale=P ** -0.5, accum_out=stat[:, 1, t:t + 1]).then_inc(bank_read(job), 1)
                        act.wait_ge(bank_read(job), turn(job))
                    if h + 1 < QH:
                        rope_in(("q", l, h + 1), 3 + h, ("q", l, h))
                    for t in range(NCH):
                        job = ("pt", l, h, t)
                        gates_before(job, nt)
                        act.wait_ge(*done(job))
                        bank = bank_of(job)
                        if h:
                            act.wait_ge(*moved(("pv", l, h - 1)))
                        af(prt[:, :, t * P:(t + 1) * P], bank[:].rearrange("p (k q) -> p k q", k=NCH),
                                ACT.Copy).then_inc(bank_read(job), 1)
                        act.wait_ge(bank_read(job), turn(job))
                gates_before(("p2b", l, 0), nt)
                act.wait_ge(sem("gate_out"), count("gate_out", ("g2b", l, DT - 1)))
                act.wait_ge(sem("split_ready"), count("split_ready", ("ao", l, DT - 1)))
                for m in range(DT):
                    if m >= 2:
                        act.wait_ge(*moved(("p2b", l, m - 2)))
                    gate_back(mgs[m % 2][:], ("g2b", l, m))
                norm_root(("m2", l))
                squares(("m3", l))
                norm_root(("m3", l))
                high_parts(("m3", l))
                for mm in range(HT):
                    job = ("eg", l, mm)
                    if mm >= 2:
                        act.wait_ge(sem("split_ready"), count("split_ready", ("h2", l, (mm - 2) // HALF, (mm - 2) % HALF)))
                    act.wait_ge(*done(job))
                    af(hs2[mm % 2][:, 0, :], bank_of(job)[:], ACT.Silu).then_inc(bank_read(job), 1)
                    act.wait_ge(bank_read(job), turn(job))
                for m in range(DT):
                    job = ("pe", l, m)
                    act.wait_ge(*done(job))
                    af(ee[:, m, :], bank_of(job)[:], ACT.Copy).then_inc(bank_read(job), 1)
                    act.wait_ge(bank_read(job), turn(job))
                if l == 0:
                    load_small(1, 1)
                norm_root(("m4", l))
                for i in range(DT):
                    act.wait_ge(sem("x_tile"), count("x_tile", (("pl", l), i)))
                    af(in_hi[:, i, :], x[:, i, :], ACT.Copy).then_inc(sem("hi_ready"), 1)
                    act.wait_ge(sem("hi_ready"), passed("hi_ready", (("pl", l), i)))
                for m in range(DT):
                    job = ("pg", l, m)
                    if m >= 2:
                        act.wait_ge(sem("pg_used"), count("pg_used", (l, m - 2)))
                    act.wait_ge(*done(job))
                    af(mg2[m % 2][:], bank_of(job)[:], ACT.Sigmoid).then_inc(bank_read(job), 1)
                    act.wait_ge(bank_read(job), turn(job))
                norm_root(("m5", l))
                if l == 0:
                    squares(("m1", 1))

            for l in range(DEPTH):
                block2(l)

        @block.vector
        def _(dve):
            tt, ts, stt = dve.tensor_tensor, dve.tensor_scalar, dve.scalar_tensor_tensor
            for i, e in enumerate((EPS_RMS, EPS_GN, 1.0, 0.0)):
                ins = dve.memset(eps[:, i:i + 1], e)
                if i == 3:
                    ins.then_inc(sem("eps_ready"), 1)
                    dve.wait_ge(sem("eps_ready"), passed("eps_ready", 0))
                else:
                    ins.then_inc(sem("vector_step"), 1)
                    dve.wait_ge(sem("vector_step"), passed("vector_step"))
            dve.wait_ge(sem("const_in"), 64)

            def col1(l, name, i, n=1):
                o = l * W1C + C1[name] + i
                return col[:, o:o + n]

            def col2(l, name, i, n=1):
                o = 2 * W1C + 8 + l * W2C + C2[name] + i
                return col[:, o:o + n]

            def split(src, hi, lo, key):
                dve.tensor_copy(hi, src).then_inc(sem("vector_step"), 1)
                dve.wait_ge(sem("vector_step"), passed("vector_step"))
                tt(lo, src, hi.bitcast(F32), ALU.subtract).then_inc(sem("split_ready"), 1)
                dve.wait_ge(sem("split_ready"), passed("split_ready", key))

            def square_sum(src, first, key=None):
                if first:
                    tt(ssq[:], src, src, ALU.mult).then_inc(sem("vector_step"), 1)
                    dve.wait_ge(sem("vector_step"), passed("vector_step"))
                else:
                    tt(sqt[:], src, src, ALU.mult).then_inc(sem("vector_step"), 1)
                    dve.wait_ge(sem("vector_step"), passed("vector_step"))
                    ins = tt(ssq[:], ssq[:], sqt[:], ALU.add)
                    if key:
                        ins.then_inc(sem("ssq_ready"), 1)
                        dve.wait_ge(sem("ssq_ready"), passed("ssq_ready", key))
                    else:
                        ins.then_inc(sem("vector_step"), 1)
                        dve.wait_ge(sem("vector_step"), passed("vector_step"))

            def inv_root(job, buf):
                dve.wait_ge(*moved(job))
                dve.reciprocal(buf, buf).then_inc(sem("vector_step"), 1)
                dve.wait_ge(sem("vector_step"), passed("vector_step"))

            def spread_root(key):
                dve.wait_ge(*moved(("norm", key)))
                dve.reciprocal(root4[:], root4[:]).then_inc(sem("vector_step"), 1)
                dve.wait_ge(sem("vector_step"), passed("vector_step"))
                ins = tt(diag[:], four(K_ID), root4[:].unsqueeze(2).to_broadcast([P, NCH, P]), ALU.mult)
                ins.then_inc(sem("diag_ready"), 1)
                dve.wait_ge(sem("diag_ready"), passed("diag_ready", key))
                dve.wait_ge(*done(("rs", key)))
                return bank_of(("rs", key))

            def normed_inputs(key, scale_of, shift_of=None):
                job = ("rs", key)
                rs = spread_root(key)
                for i in range(DT + 1):
                    if i < DT:
                        ins = stt(nts[i % 2][:], x[:, i, :], scale_of(i), rs[:], ALU.mult, ALU.mult)
                        if i < DT - 1:
                            ins.then_inc(sem("nt_ready"), 1)
                            dve.wait_ge(sem("nt_ready"), passed("nt_ready", (key, i)))
                        else:
                            ins.then_inc(bank_read(job), 1)
                            dve.wait_ge(bank_read(job), turn(job))
                    if i:
                        j = i - 1
                        dve.wait_ge(sem("hi_ready"), count("hi_ready", (key, j)))
                        hi = in_hi[:, j, :].bitcast(F32)
                        if shift_of:
                            ins = stt(in_lo[:, j, :], nts[j % 2][:], shift_of(j), hi, ALU.add, ALU.subtract)
                        else:
                            ins = tt(in_lo[:, j, :], nts[j % 2][:], hi, ALU.subtract)
                        ins.then_inc(sem("split_ready"), 1)
                        dve.wait_ge(sem("split_ready"), passed("split_ready", key + (j,)))

            ada_done = [0]

            def ada(pairs):
                for n in range(ada_done[0], ada_done[0] + pairs):
                    l, pair, kb = ada_order[n]
                    buf = ada_buf[kb]
                    dve.wait_ge(sem(f"ada_in{n % 8}"), 16 * (n // 8 + 1))
                    for j in range(2):
                        m = 2 * pair + j
                        ins = stt(buf[:, j, :], buf[:, j, :], 1.0, c_act[:], ALU.mult, ALU.mult,
                                  accum_out=mod[:, m:m + 1])
                        ins.then_inc(sem("ada_step"), 1)
                        dve.wait_ge(sem("ada_step"), passed("ada_step", (n, j)))
                    m = 2 * pair
                    tt(mod[:, m:m + 2], mod[:, m:m + 2], col1(l, "ada_b", m, 2), ALU.add).then_inc(sem("vector_step"), 1)
                    dve.wait_ge(sem("vector_step"), passed("vector_step"))
                ada_done[0] += pairs

            def block1(l):
                if l == 0:
                    dve.wait_ge(sem("c_ready"), count("c_ready", 0))
                    ada(8)
                    dve.wait_ge(sem("x_in"), 16)
                ins = stt(gsc[:, 0:8], mod[:, 8:16], 1.0, col1(l, "norm1_g", 0, 8), ALU.add, ALU.mult)
                ins.then_inc(sem("vector_step"), 1)
                dve.wait_ge(sem("vector_step"), passed("vector_step"))
                ts(omk[:, 0:4], col1(l, "k_a", 0, 4), -1.0, 1.0, ALU.mult, ALU.add).then_inc(sem("vector_step"), 1)
                dve.wait_ge(sem("vector_step"), passed("vector_step"))
                ts(omk[:, 4:8], col1(l, "lnx_g", 0, 4), -1.0, None, ALU.mult).then_inc(sem("vector_step"), 1)
                dve.wait_ge(sem("vector_step"), passed("vector_step"))
                for i in range(2):
                    ins = dve.memset(zbuf[i][:, 0:ZPAD], 0.0)
                    if i:
                        ins.then_inc(sem("zpad_ready"), 1)
                        dve.wait_ge(sem("zpad_ready"), passed("zpad_ready", l))
                    else:
                        ins.then_inc(sem("vector_step"), 1)
                        dve.wait_ge(sem("vector_step"), passed("vector_step"))
                normed_inputs(("n1", l), lambda i: gsc[:, i:i + 1], lambda i: mod[:, i:i + 1])

                def shift(m, n, dst):
                    dve.wait_ge(*moved(("p", l, m)))
                    z = zbuf[n % 2]
                    tt(dst, z[:, ZPAD - 1:ZPAD - 1 + T], z[:, ZPAD:ZPAD + T], ALU.subtract).then_inc(sem("vector_step"), 1)
                    dve.wait_ge(sem("vector_step"), passed("vector_step"))
                    stt(dst, dst, col1(l, "mu", m), z[:, ZPAD:ZPAD + T], ALU.mult, ALU.add).then_inc(sem("ps_ready"), 1)
                    dve.wait_ge(sem("ps_ready"), passed("ps_ready", (l, m)))

                shift(M_WA, 0, wa[:])
                shift(M_GL, 1, gl_s[:, 0, :])
                shift(M_GLV, 2, gl_s[:, 1, :])
                for d in range(RT):
                    shift(M_K + d, 3 + d, k_f[:, d, :])
                    dve.wait_ge(*moved(("za", l, d)))
                    ins = ts(qr[:, d, 0, :], k_f[:, d, :], col1(l, "k_k", d), None, ALU.mult)
                    ins.then_inc(sem("vector_step"), 1)
                    dve.wait_ge(sem("vector_step"), passed("vector_step"))
                    tt(tmp[:, d, :], qr[:, d, 0, :], qr[:, d, 0, :], ALU.mult).then_inc(sem("kksq_ready"), 1)
                    dve.wait_ge(sem("kksq_ready"), passed("kksq_ready", (l, d)))
                    ins = ts(nv[:], b_f[:, d, :], col1(l, "k_a", d), omk[:, d:d + 1], ALU.mult, ALU.add)
                    ins.then_inc(sem("vector_step"), 1)
                    dve.wait_ge(sem("vector_step"), passed("vector_step"))
                    tt(k_f[:, d, :], k_f[:, d, :], nv[:], ALU.mult).then_inc(sem("vector_step"), 1)
                    dve.wait_ge(sem("vector_step"), passed("vector_step"))
                    for c in range(NCH):
                        cs = slice(c * P, (c + 1) * P)
                        dve.tensor_tensor_scan(lcum[:, d, cs], kst[:, K_ONES, :], sgw[:, d, cs], 0.0,
                                                  ALU.mult, ALU.add).then_inc(sem("vector_step"), 1)
                        dve.wait_ge(sem("vector_step"), passed("vector_step"))
                    lcd = lcum[:, d, :].rearrange("p (c t) -> p c t", c=NCH)
                    dve.tensor_copy(lmid[:, d, :], lcd[:, :, 63]).then_inc(sem("vector_step"), 1)
                    dve.wait_ge(sem("vector_step"), passed("vector_step"))
                    ins = tt(lcd, lcd, lmid[:, d, :].unsqueeze(2).to_broadcast([P, NCH, P]), ALU.subtract)
                    ins.then_inc(sem("vector_step"), 1)
                    dve.wait_ge(sem("vector_step"), passed("vector_step"))
                    ins = tt(sgw[:, d, :], lcum[:, d, :], sgw[:, d, :], ALU.subtract)
                    ins.then_inc(sem("vector_step"), 1)
                    dve.wait_ge(sem("vector_step"), passed("vector_step"))
                    if l == 0:
                        ada(1 if d else 2)
                lc = lcum[:].rearrange("p d (c t) -> p d c t", c=NCH)
                ins = tt(sscal[:, :, 0:NCH - 1], lc[:, :, 0:NCH - 1, P - 1], lmid[:, :, 1:NCH], ALU.add)
                ins.then_inc(sem("vector_step"), 1)
                dve.wait_ge(sem("vector_step"), passed("vector_step"))
                dve.memset(sscal[:, :, NCH - 1:NCH], 0.0).then_inc(sem("lcum_ready"), 1)
                dve.wait_ge(sem("lcum_ready"), passed("lcum_ready", l))
                for d in range(RT):
                    inv = tmp[:, d, :]
                    dve.wait_ge(*moved(("kk", l, d)))
                    ts(inv, inv, 1e-12, None, ALU.max).then_inc(sem("vector_step"), 1)
                    dve.wait_ge(sem("vector_step"), passed("vector_step"))
                    dve.reciprocal(inv, inv).then_inc(sem("vector_step"), 1)
                    dve.wait_ge(sem("vector_step"), passed("vector_step"))
                    tt(qr[:, d, 0, :], qr[:, d, 0, :], inv, ALU.mult).then_inc(sem("vector_step"), 1)
                    dve.wait_ge(sem("vector_step"), passed("vector_step"))
                    tt(b_f[:, d, :], b_f[:, d, :], qr[:, d, 0, :], ALU.mult).then_inc(sem("vector_step"), 1)
                    dve.wait_ge(sem("vector_step"), passed("vector_step"))
                    dve.wait_ge(sem("decay_ready"), count("decay_ready", (l, d)))
                    tt(qr[:, d, 0, :], qr[:, d, 0, :], sgw[:, d, :], ALU.mult).then_inc(sem("vector_step"), 1)
                    dve.wait_ge(sem("vector_step"), passed("vector_step"))
                    r = qr[:, d, 1, :]
                    shift(M_R + d, 7 + d, r)
                    stt(tmp[:, d, :], r, col1(l, "r_k", d), k_f[:, d, :], ALU.mult, ALU.mult).then_inc(sem("rk_ready"), 1)
                    dve.wait_ge(sem("rk_ready"), passed("rk_ready", (l, d)))
                    tt(r, r, e_neg[d % 2][:], ALU.mult).then_inc(sem("r_ready"), 1)
                    dve.wait_ge(sem("r_ready"), passed("r_ready", (l, d)))
                    if l == 0:
                        ada(2)
                for d in range(RT):
                    tt(b_f[:, d, :], b_f[:, d, :], lcum[:, d, :], ALU.mult).then_inc(sem("vector_step"), 1)
                    dve.wait_ge(sem("vector_step"), passed("vector_step"))
                    tt(k_f[:, d, :], k_f[:, d, :], lcum[:, d, :], ALU.mult).then_inc(sem("vector_step"), 1)
                    dve.wait_ge(sem("vector_step"), passed("vector_step"))
                    if l:
                        shift(M_V + d, 11 + d, nv[:])
                        tt(v_f[:, d, :], v_f[:, d, :], nv[:], ALU.subtract).then_inc(sem("vector_step"), 1)
                        dve.wait_ge(sem("vector_step"), passed("vector_step"))
                        tt(v_f[:, d, :], v_f[:, d, :], gate_v[:, d, :], ALU.mult).then_inc(sem("vector_step"), 1)
                        dve.wait_ge(sem("vector_step"), passed("vector_step"))
                        tt(v_f[:, d, :], v_f[:, d, :], nv[:], ALU.add).then_inc(sem("vector_step"), 1)
                        dve.wait_ge(sem("vector_step"), passed("vector_step"))
                    else:
                        shift(M_V + d, 11 + d, v_f[:, d, :])
                        if d < RT - 1:
                            ada(1)
                dve.memset(st[:], 0.0).then_inc(sem("wkv_in"), 1)
                dve.wait_ge(sem("wkv_in"), passed("wkv_in", l))
                for d in range(RT):
                    job = ("rk", l, d)
                    dve.wait_ge(*done(job))
                    tt(bonus[:, d, :], bank_of(job)[:], v_f[:, d, :], ALU.mult).then_inc(bank_read(job), 1)
                    dve.wait_ge(bank_read(job), turn(job))
                for c in range(NCH):
                    wkv_chunk(l, c)
                for d in range(RT):
                    y = qr[:, d, 1, :]
                    job = ("mean", l, d)
                    dve.wait_ge(*done(job))
                    stt(y, bank_of(job)[:], 1.0 / HEAD, y, ALU.mult, ALU.subtract).then_inc(bank_read(job), 1)
                    dve.wait_ge(bank_read(job), turn(job))
                    tt(yt[d % 2][:], y, y, ALU.mult).then_inc(sem("var_ready"), 1)
                    dve.wait_ge(sem("var_ready"), passed("var_ready", (l, d)))
                    inv_root(("var", l, d), yr[d % 2][:])
                    tt(y, y, yr[d % 2][:], ALU.mult).then_inc(sem("vector_step"), 1)
                    dve.wait_ge(sem("vector_step"), passed("vector_step"))
                    ins = ts(y, y, omk[:, 4 + d:5 + d], col1(l, "lnx_b", d), ALU.mult, ALU.add)
                    ins.then_inc(sem("vector_step"), 1)
                    dve.wait_ge(sem("vector_step"), passed("vector_step"))
                    tt(y, y, bonus[:, d, :], ALU.add).then_inc(sem("vector_step"), 1)
                    dve.wait_ge(sem("vector_step"), passed("vector_step"))
                    job = ("g", l, d)
                    dve.wait_ge(*done(job))
                    tt(y, y, bank_of(job)[:], ALU.mult).then_inc(bank_read(job), 1)
                    dve.wait_ge(bank_read(job), turn(job))
                    split(y, ya_hi[:, d, :], ya_lo[:, d, :], ("ya", l, d))
                for d in range(4):
                    dve.wait_ge(*moved(("pool", l, d)))
                    split(mt_[d % 2][:], yb_hi[:, d, :], yb_lo[:, d, :], ("yb", l, d))
                for m in range(DT):
                    dve.wait_ge(sem(f"gate_in{m % 2}"), count(f"gate_in{m % 2}", ("gb", l, m)))
                    for i, pn in enumerate(("pa", "pb")):
                        job = (pn, l, m)
                        dve.wait_ge(*done(job))
                        tt(mt_[i][:], gin[m % 2][i][:], bank_of(job)[:], ALU.mult).then_inc(bank_read(job), 1)
                        dve.wait_ge(bank_read(job), turn(job))
                    tt(mt_[0][:], mt_[0][:], mt_[1][:], ALU.add).then_inc(sem("vector_step"), 1)
                    dve.wait_ge(sem("vector_step"), passed("vector_step"))
                    split(mt_[0][:], mx_hi[:, m, :], mx_lo[:, m, :], ("mx", l, m))
                for m in range(DT):
                    job = ("wo", l, m)
                    dve.wait_ge(*done(job))
                    ins = stt(x[:, m, :], bank_of(job)[:], mod[:, 16 + m:17 + m], x[:, m, :], ALU.mult, ALU.add)
                    ins.then_inc(bank_read(job), 1)
                    dve.wait_ge(bank_read(job), turn(job))
                    square_sum(x[:, m, :], m == 0, ("n2", l) if m == DT - 1 else None)
                ins = stt(gsc[:, 8:16], mod[:, 32:40], 1.0, col1(l, "norm2_g", 0, 8), ALU.add, ALU.mult)
                ins.then_inc(sem("vector_step"), 1)
                dve.wait_ge(sem("vector_step"), passed("vector_step"))
                normed_inputs(("n2", l), lambda i: gsc[:, 8 + i:9 + i], lambda i: mod[:, 24 + i:25 + i])
                dve.tensor_copy(gate2[:], mod[:, 40:48]).then_inc(sem("vector_step"), 1)
                dve.wait_ge(sem("vector_step"), passed("vector_step"))
                if l == 0:
                    dve.wait_ge(sem("c_ready"), count("c_ready", 1))
                for f in range(2):
                    for m in range(HALF):
                        mm = f * HALF + m
                        dve.wait_ge(*moved(("fg", l, mm)))
                        job = ("fu", l, mm)
                        h = hs[mm % 2]
                        dve.wait_ge(*done(job))
                        tt(h[:, 1, :], h[:, 0, :], bank_of(job)[:], ALU.mult).then_inc(bank_read(job), 1)
                        dve.wait_ge(bank_read(job), turn(job))
                        split(h[:, 1, :], hid_hi[:, m, :], hid_lo[:, m, :], ("hid", l, f, m))
                        if l == 0:
                            ada(1 if mm < HT - 2 else 2)
                    for m in range(DT):
                        job = ("fd", l, f, m)
                        dve.wait_ge(*done(job))
                        ins = stt(x[:, m, :], bank_of(job)[:], gate2[:, m:m + 1], x[:, m, :], ALU.mult, ALU.add)
                        ins.then_inc(bank_read(job), 1)
                        dve.wait_ge(bank_read(job), turn(job))
                        if f:
                            key = ("n1", 1) if l == 0 else ("nf", 0)
                            square_sum(x[:, m, :], m == 0, key if m == DT - 1 else None)

            def wkv_chunk(l, c):
                pair = kst[:, K_STRICT:K_INCL + 1, :]
                for h in range(NH):
                    job = ("score", l, c, h)
                    dve.wait_ge(*done(job))
                    bank = bank_of(job)
                    for i in range(2):
                        ins = tt(units[:, h, 2 * i:2 * i + 2, :],
                                 bank[:, 256 * i:256 * i + 256].rearrange("p (a t) -> p a t", a=2), pair, ALU.mult)
                        if i:
                            ins.then_inc(bank_read(job), 1)
                            dve.wait_ge(bank_read(job), turn(job))
                        else:
                            ins.then_inc(sem("vector_step"), 1)
                            dve.wait_ge(sem("vector_step"), passed("vector_step"))
                for g in range(2):
                    ins = tt(mt[g][:], units[:, 4 * g:4 * g + 4, 0, :], four(K_LEVEL), ALU.mult)
                    ins.then_inc(sem("vector_step"), 1)
                    dve.wait_ge(sem("vector_step"), passed("vector_step"))
                    tt(mt[g][:], four(K_ID), mt[g][:], ALU.subtract).then_inc(sem("mt_ready"), 1)
                    dve.wait_ge(sem("mt_ready"), passed("mt_ready", (l, c, g)))
                for v in range(1, len(LEVELS)):
                    for g in range(2):
                        ins = tt(bm[g][:], units[:, 4 * g:4 * g + 4, 0, :], four(K_LEVEL + v), ALU.mult)
                        ins.then_inc(sem("bm_ready"), 1)
                        dve.wait_ge(sem("bm_ready"), passed("bm_ready", (l, c, g, v)))
                    for g in range(2):
                        flat = lambda t: t[:].rearrange("p j t -> p (j t)")
                        if v < len(LEVELS) - 1:
                            job = ("mam", l, c, g, v)
                            dve.wait_ge(*done(job))
                            bank = bank_of(job)
                            dve.wait_ge(*moved(("inv_t", l, c, g)))
                            part = half(flat(mi[g]), LEVELS[v], 0)
                            ins = tt(part, part, half(bank[:], LEVELS[v], 0), ALU.subtract)
                            ins.then_inc(bank_read(job), 1)
                            dve.wait_ge(bank_read(job), turn(job))
                        job = ("mamt", l, c, g, v)
                        dve.wait_ge(*done(job))
                        bank = bank_of(job)
                        part = half(flat(mt[g]), LEVELS[v], 1)
                        tt(part, part, half(bank[:], LEVELS[v], 1), ALU.subtract).then_inc(bank_read(job), 1)
                        dve.wait_ge(bank_read(job), turn(job))
                if c < NCH - 1:
                    job = ("state", l, c)
                    dve.wait_ge(*done(job))
                    bank = bank_of(job)
                    dve.wait_ge(*done(("y", l, c)))
                    for i in range(2):
                        rows = slice(64 * i, 64 * i + 64)
                        o = bank[rows, 0:RT * HEAD].rearrange("p (d v) -> p d v", d=RT)
                        s = st[rows, :, rows]
                        ins = tt(s, o, s, ALU.add)
                        if i:
                            ins.then_inc(bank_read(job), 1)
                            dve.wait_ge(bank_read(job), turn(job))
                        else:
                            ins.then_inc(sem("vector_step"), 1)
                            dve.wait_ge(sem("vector_step"), passed("vector_step"))
                    ins = tt(st[:], st[:], sscal[:, :, c:c + 1].to_broadcast([P, RT, P]), ALU.mult)
                    ins.then_inc(sem("state_ready"), 1)
                    dve.wait_ge(sem("state_ready"), passed("state_ready", (l, c + 1)))

            def four(k):
                return kst[:, k, :].unsqueeze(1).to_broadcast([P, 4, P])

            for l in range(DEPTH):
                block1(l)
            rs = spread_root(("nf", 0))
            for i in range(DT):
                o = 2 * W1C + i
                ins = stt(x[:, i, :], x[:, i, :], col[:, o:o + 1], rs[:], ALU.mult, ALU.mult)
                if i < DT - 1:
                    ins.then_inc(sem("x_tile"), 1)
                    dve.wait_ge(sem("x_tile"), passed("x_tile", (("m1", 0), i)))
                else:
                    job = ("rs", ("nf", 0))
                    ins.then_inc(bank_read(job), 1)
                    dve.wait_ge(bank_read(job), turn(job))

            def cols_of(l, name):
                return lambda i: col2(l, name, i)

            def gla_decay(l, h):
                for i in range(2):
                    job = ("gz", l, h, i)
                    dve.wait_ge(*done(job))
                    bank = bank_of(job)
                    dve.wait_ge(sem("abs_ready"), count("abs_ready", (l, h, i)))
                    ts(la[i][:].rearrange("p c t -> p (c t)"), bank[:], col2(l, "b_alpha", 4 * i + h), 0.0,
                            ALU.add, ALU.min).then_inc(bank_read(job), 1)
                    dve.wait_ge(bank_read(job), turn(job))
                for i in range(2):
                    dve.wait_ge(sem("log_ready"), count("log_ready", (l, h, i)))
                    tt(la[i][:], la[i][:], ln[i][:], ALU.subtract).then_inc(sem("vector_step"), 1)
                    dve.wait_ge(sem("vector_step"), passed("vector_step"))
                    for c in range(NCH):
                        dve.tensor_tensor_scan(ln[i][:, c, :], kst[:, K_ONES, :], la[i][:, c, :], 0.0,
                                                  ALU.mult, ALU.add).then_inc(sem("vector_step"), 1)
                        dve.wait_ge(sem("vector_step"), passed("vector_step"))
                    last = ln[i][:, :, P - 1]
                    n = NCH - 1
                    if i:
                        dve.tensor_copy(dsc[1][:, 0:NCH], last).then_inc(sem("vector_step"), 1)
                        dve.wait_ge(sem("vector_step"), passed("vector_step"))
                        tt(ln[1][:], ln[1][:], la[1][:], ALU.subtract).then_inc(sem("vector_step"), 1)
                        dve.wait_ge(sem("vector_step"), passed("vector_step"))
                    dve.tensor_copy(mid[i][:], ln[i][:, :, 63]).then_inc(sem("vector_step"), 1)
                    dve.wait_ge(sem("vector_step"), passed("vector_step"))
                    if i:
                        tt(dsc[1][:, 0:n], dsc[1][:, 0:n], mid[1][:, 1:NCH], ALU.add).then_inc(sem("vector_step"), 1)
                        dve.wait_ge(sem("vector_step"), passed("vector_step"))
                        ins = tt(dsc[1][:, 0:n], dsc[1][:, 0:n], mid[1][:, 0:n], ALU.subtract)
                        ins.then_inc(sem("vector_step"), 1)
                        dve.wait_ge(sem("vector_step"), passed("vector_step"))
                    ins = tt(ln[i][:], ln[i][:], mid[i][:].unsqueeze(2).to_broadcast([P, NCH, P]), ALU.subtract)
                    ins.then_inc(sem("vector_step"), 1)
                    dve.wait_ge(sem("vector_step"), passed("vector_step"))
                    if not i:
                        ins = tt(dsc[0][:, 0:n], ln[0][:, 0:n, P - 1], mid[0][:, 1:NCH], ALU.add)
                        ins.then_inc(sem("vector_step"), 1)
                        dve.wait_ge(sem("vector_step"), passed("vector_step"))
                        dve.memset(dsc[0][:, n:NCH], 0.0).then_inc(sem("cum_ready"), 1)
                        dve.wait_ge(sem("cum_ready"), passed("cum_ready", (l, h, i)))
                    else:
                        dve.memset(dsc[1][:, n:NCH], 0.0).then_inc(sem("cum_ready"), 1)
                        dve.wait_ge(sem("cum_ready"), passed("cum_ready", (l, h, i)))

            def gla_core(l, h):
                q3 = gq[h % 2][:].rearrange("p (c t) -> p c t", c=NCH)
                k3 = gk[h % 2][:].rearrange("p (c t) -> p c t", c=NCH)
                dve.wait_ge(*moved(("gk", l, h)))
                for i in range(2):
                    dve.wait_ge(sem("ed_ready"), count("ed_ready", (l, h, i)))
                    stt(qd[i][:].rearrange("p c t -> p (c t)"), gq[h % 2][:], GDK ** -0.5,
                           la[i][:].rearrange("p c t -> p (c t)"), ALU.mult, ALU.mult).then_inc(sem("vector_step"), 1)
                    dve.wait_ge(sem("vector_step"), passed("vector_step"))
                    ins = tt(kd[i][:], k3, ln[i][:], ALU.mult)
                    if i:
                        ins.then_inc(sem("qd_ready"), 1)
                        dve.wait_ge(sem("qd_ready"), passed("qd_ready", (l, h)))
                    else:
                        ins.then_inc(sem("vector_step"), 1)
                        dve.wait_ge(sem("vector_step"), passed("vector_step"))
                job = ("gsc", l, h, 0)
                dve.wait_ge(*done(job))
                bank = bank_of(job)
                ins = tt(sc[:], bank[:].rearrange("p (c t) -> p c t", c=NCH), four(K_INCL), ALU.mult)
                ins.then_inc(bank_read(job), 1)
                dve.wait_ge(bank_read(job), turn(job))
                job = ("gsc", l, h, 1)
                dve.wait_ge(*done(job))
                bank = bank_of(job)
                ins = tt(sc2[:], bank[:].rearrange("p (c t) -> p c t", c=NCH), four(K_INCLREV), ALU.mult)
                ins.then_inc(bank_read(job), 1)
                dve.wait_ge(bank_read(job), turn(job))
                tt(sc[:], sc[:], sc2[:], ALU.add).then_inc(sem("sc_ready"), 1)
                dve.wait_ge(sem("sc_ready"), passed("sc_ready", (l, h)))
                for n in range(NCH - 1):
                    job = ("gst", l, h, n)
                    dve.wait_ge(*done(job))
                    bank = bank_of(job)
                    for i in range(2):
                        part = bank[:, i * GDV:(i + 1) * GDV]
                        c = n if i == 0 else NCH - 2 - n
                        src = part
                        if n:
                            ins = tt(gs[i][:, n, :], gs[i][:, n - 1, :], part, ALU.add)
                            if i:
                                ins.then_inc(bank_read(job), 1)
                                dve.wait_ge(bank_read(job), turn(job))
                            else:
                                ins.then_inc(sem("vector_step"), 1)
                                dve.wait_ge(sem("vector_step"), passed("vector_step"))
                            src = gs[i][:, n, :]
                        ins = ts(gs[i][:, n, :], src, dsc[i][:, c:c + 1], None, ALU.mult)
                        if n == 0 and i:
                            ins.then_inc(bank_read(job), 1)
                            dve.wait_ge(bank_read(job), turn(job))
                        elif n == NCH - 2 and i:
                            ins.then_inc(sem("gs_ready"), 1)
                            dve.wait_ge(sem("gs_ready"), passed("gs_ready", (l, h)))
                        else:
                            ins.then_inc(sem("vector_step"), 1)
                            dve.wait_ge(sem("vector_step"), passed("vector_step"))
                inv_root(("gn", l, h), rsg[:])
                for j in range(2):
                    job = ("go", l, h, j)
                    dve.wait_ge(*done(job))
                    ins = stt(ot[:], bank_of(job)[:], col2(l, "g_gla", j), rsg[:], ALU.mult, ALU.mult)
                    ins.then_inc(bank_read(job), 1)
                    dve.wait_ge(bank_read(job), turn(job))
                    dve.wait_ge(*moved(("gg", l, h, j)))
                    tt(ot[:], ot[:], sg[h % 2][:, j, :], ALU.mult).then_inc(sem("vector_step"), 1)
                    dve.wait_ge(sem("vector_step"), passed("vector_step"))
                    split(ot[:], go_hi[:, 2 * h + j, :], go_lo[:, 2 * h + j, :], ("go", l, 2 * h + j))

            def rope_norm(key, l, gain):
                inv_root(("qs",) + key, ars[:])
                stt(qn[:], qraw[:], col2(l, gain, 0), ars[:], ALU.mult, ALU.mult).then_inc(sem("qn_ready"), 1)
                dve.wait_ge(sem("qn_ready"), passed("qn_ready", key))

            def rope_out(key, dst):
                tt(qt_[:], qn[:], rope_t[:, 0, :], ALU.mult).then_inc(sem("vector_step"), 1)
                dve.wait_ge(sem("vector_step"), passed("vector_step"))
                job = ("rot",) + key
                dve.wait_ge(*done(job))
                tt(dst, bank_of(job)[:], rope_t[:, 1, :], ALU.mult).then_inc(bank_read(job), 1)
                dve.wait_ge(bank_read(job), turn(job))
                tt(dst, dst, qt_[:], ALU.add).then_inc(sem("rope_ready"), 1)
                dve.wait_ge(sem("rope_ready"), passed("rope_ready", key))

            def post_norm(l, key, gain, then):
                job = ("rs", (key, l))
                rs = spread_root((key, l))
                for i in range(DT + 1):
                    if i < DT:
                        ins = stt(nt[:], yy[:, i, :], col2(l, gain, i), rs[:], ALU.mult, ALU.mult)
                        if i < DT - 1:
                            ins.then_inc(sem("vector_step"), 1)
                            dve.wait_ge(sem("vector_step"), passed("vector_step"))
                        else:
                            ins.then_inc(bank_read(job), 1)
                            dve.wait_ge(bank_read(job), turn(job))
                        ins = tt(x[:, i, :], x[:, i, :], nt[:], ALU.add)
                        if then == "out":
                            ins.then_inc(sem("x_done"), 1)
                            dve.wait_ge(sem("x_done"), passed("x_done", i))
                        else:
                            ins.then_inc(sem("x_tile"), 1)
                            dve.wait_ge(sem("x_tile"), passed("x_tile", (then, i)))
                    if i and then == ("pl", l):
                        j = i - 1
                        dve.wait_ge(sem("hi_ready"), count("hi_ready", (then, j)))
                        ins = tt(in_lo[:, j, :], x[:, j, :], in_hi[:, j, :].bitcast(F32), ALU.subtract)
                        ins.then_inc(sem("split_ready"), 1)
                        dve.wait_ge(sem("split_ready"), passed("split_ready", then + (j,)))

            def block2(l):
                normed_inputs(("m1", l), cols_of(l, "g_mix_pre"))
                gla_decay(l, 0)
                for h in range(GH):
                    gla_core(l, h)
                    if h + 1 < GH:
                        gla_decay(l, h + 1)
                for m in range(DT):
                    dve.wait_ge(sem(f"gate_in{m % 2}"), count(f"gate_in{m % 2}", ("g2a", l, m)))
                    job = ("p2a", l, m)
                    dve.wait_ge(*done(job))
                    tt(ma[:, m, :], mgs[m % 2][:], bank_of(job)[:], ALU.mult).then_inc(bank_read(job), 1)
                    dve.wait_ge(bank_read(job), turn(job))
                dve.wait_ge(sem("rope_in"), 16 * (l + 1))
                for i in range(KVH):
                    rope_norm(("k", l, i), l, "g_k")
                    rope_out(("k", l, i), ak[:, i, :])
                rope_norm(("q", l, 0), l, "g_q")
                rope_out(("q", l, 0), aq[0][:])
                for h in range(QH):
                    for t in range(NCH):
                        dve.wait_ge(*done(("as", l, h, t)))
                        bank = bank_of(("as", l, h, t))
                        dve.tensor_reduce(stat[:, 2, t:t + 1], bank[:], AX.X, ALU.max).then_inc(sem("vector_step"), 1)
                        dve.wait_ge(sem("vector_step"), passed("vector_step"))
                        ins = ts(stat[:, 0, t:t + 1], stat[:, 2, t:t + 1], -(P ** -0.5), None, ALU.mult)
                        ins.then_inc(sem("max_ready"), 1)
                        dve.wait_ge(sem("max_ready"), passed("max_ready", (l, h, t)))
                    for t in range(NCH):
                        dve.wait_ge(*moved(("as", l, h, t)))
                        dve.reciprocal(stat[:, 2, t:t + 1], stat[:, 1, t:t + 1]).then_inc(sem("vector_step"), 1)
                        dve.wait_ge(sem("vector_step"), passed("vector_step"))
                        ts(pr[:, t, :], pr[:, t, :], stat[:, 2, t:t + 1], None, ALU.mult).then_inc(sem("pr_ready"), 1)
                        dve.wait_ge(sem("pr_ready"), passed("pr_ready", (l, h, t)))
                    if h + 1 < QH:
                        rope_norm(("q", l, h + 1), l, "g_q")
                        rope_out(("q", l, h + 1), aq[(h + 1) % 2][:])
                    job = ("pv", l, h)
                    dve.wait_ge(*done(job))
                    bank = bank_of(job)
                    dve.tensor_copy(qt_[:], bank[:]).then_inc(bank_read(job), 1)
                    dve.wait_ge(bank_read(job), turn(job))
                    split(qt_[:], ao_hi[:, h, :], ao_lo[:, h, :], ("ao", l, h))
                for m in range(DT):
                    dve.wait_ge(sem(f"gate_in{m % 2}"), count(f"gate_in{m % 2}", ("g2b", l, m)))
                    job = ("p2b", l, m)
                    dve.wait_ge(*done(job))
                    tt(mgt[:], mgs[m % 2][:], bank_of(job)[:], ALU.mult).then_inc(bank_read(job), 1)
                    dve.wait_ge(bank_read(job), turn(job))
                    tt(mgt[:], mgt[:], ma[:, m, :], ALU.add).then_inc(sem("vector_step"), 1)
                    dve.wait_ge(sem("vector_step"), passed("vector_step"))
                    split(mgt[:], m2_hi[:, m, :], m2_lo[:, m, :], ("m2", l, m))
                for m in range(DT):
                    job = ("wo2", l, m)
                    dve.wait_ge(*done(job))
                    dve.tensor_copy(yy[:, m, :], bank_of(job)[:]).then_inc(bank_read(job), 1)
                    dve.wait_ge(bank_read(job), turn(job))
                    square_sum(yy[:, m, :], m == 0, ("m2", l) if m == DT - 1 else None)
                post_norm(l, "m2", "g_mix_post", ("m3", l))
                normed_inputs(("m3", l), cols_of(l, "g_ffn_pre"))
                for i in range(2):
                    split(sml[:, 1 + i, :], pp_hi[:, i, :], pp_lo[:, i, :], ("pp", l, i))
                for f in range(2):
                    for m in range(HALF):
                        mm = f * HALF + m
                        dve.wait_ge(*moved(("eg", l, mm)))
                        job = ("eu", l, mm)
                        h = hs2[mm % 2]
                        dve.wait_ge(*done(job))
                        tt(h[:, 1, :], h[:, 0, :], bank_of(job)[:], ALU.mult).then_inc(bank_read(job), 1)
                        dve.wait_ge(bank_read(job), turn(job))
                        split(h[:, 1, :], h2_hi[:, m, :], h2_lo[:, m, :], ("h2", l, f, m))
                    for m in range(DT):
                        job = ("ed", l, f, m)
                        dve.wait_ge(*done(job))
                        bank = bank_of(job)
                        if f:
                            tt(yy[:, m, :], yy[:, m, :], bank[:], ALU.add).then_inc(bank_read(job), 1)
                            dve.wait_ge(bank_read(job), turn(job))
                            square_sum(yy[:, m, :], m == 0, ("m4", l) if m == DT - 1 else None)
                        else:
                            dve.tensor_copy(yy[:, m, :], bank[:]).then_inc(bank_read(job), 1)
                            dve.wait_ge(bank_read(job), turn(job))
                post_norm(l, "m4", "g_ffn_post", ("pl", l))
                for m in range(DT):
                    dve.wait_ge(*moved(("pg", l, m)))
                    tt(yy[:, m, :], mg2[m % 2][:], ee[:, m, :], ALU.mult).then_inc(sem("pg_used"), 1)
                    dve.wait_ge(sem("pg_used"), passed("pg_used", (l, m)))
                    square_sum(yy[:, m, :], m == 0, ("m5", l) if m == DT - 1 else None)
                post_norm(l, "m5", "g_ple_post", ("m1", 1) if l == 0 else "out")

            for l in range(DEPTH):
                block2(l)

        @block.gpsimd
        def _(pool):
            tt, ts = pool.tensor_tensor, pool.tensor_scalar

            def pool_window(l, d, win):
                if d == 0:
                    pool.wait_ge(*done(("y", l, NCH - 1)))
                    for part in (zp[:, :, 0:16], zs[0][:, 0:16], zs[1][:, 0:16]):
                        pool.memset(part, 0.0).then_inc(sem("pool_step"), 1)
                        pool.wait_ge(sem("pool_step"), passed("pool_step"))
                    pool.wait_ge(sem("zp_in"), count("zp_in", (l, 3)))
                src, span, n = zp[:, d, :], 1, 0
                while span < win:
                    dst = zs[n % 2]
                    ins = tt(dst[:, 16:528], src[:, 16:528], src[:, 16 - span:528 - span], ALU.add)
                    ins.then_inc(sem("pool_step"), 1)
                    pool.wait_ge(sem("pool_step"), passed("pool_step"))
                    src, span, n = dst, 2 * span, n + 1
                tt(src[:, 16:32], src[:, 16:32], inv_cnt[:, d, :], ALU.mult).then_inc(sem("pool_step"), 1)
                pool.wait_ge(sem("pool_step"), passed("pool_step"))
                ts(src[:, 32:528], src[:, 32:528], 1.0 / win, 1.0, ALU.mult, ALU.mult).then_inc(sem("pool_step"), 1)
                pool.wait_ge(sem("pool_step"), passed("pool_step"))
                ins = tt(zp[:, d, 16:528], src[:, 16:528], zp[:, d, 16:528], ALU.subtract)
                ins.then_inc(sem("pooled_ready"), 1)
                pool.wait_ge(sem("pooled_ready"), passed("pooled_ready", (l, d)))

            for s in range(len(slabs)):
                for l in range(DEPTH):
                    for d, win in enumerate(WINDOWS):
                        if s == windows_at[l] + WINDOW_SLAB[d]:
                            pool_window(l, d, win)
                j = s % 2
                pool.wait_ge(sem(f"slab_in{j}"), 16 * (s // 2 + 1))
                if s >= 2:
                    pool.wait_ge(*slab_end[s - 2])
                pool.tensor_scalar(w_hi[j][:], raw[j][:], 1.0, 1.0, ALU.mult, ALU.mult).then_inc(sem("slab_hi"), 1)
                pool.wait_ge(sem("slab_hi"), s + 1)
                pool.tensor_tensor(w_lo[j][:], raw[j][:], w_hi[j][:].bitcast(F32), ALU.subtract).then_inc(
                    sem("slab_split"), 1)

        @block.sync
        def _(sp):
            def load_ada(n):
                l, pair, kb = ada_order[n]
                before = [i for i in range(n) if ada_order[i][2] == kb]
                if before:
                    sp.wait_ge(sem("ada_step"), count("ada_step", (before[-1], 1)))
                if l == 1 and n < 26:
                    sp.wait_ge(*done(("wo", 0, DT - 1)))
                sp.dma_start(ada_buf[kb][:], ada_slabs[l, pair]).then_inc(sem(f"ada_in{n % 8}"), 16)

            ada_before = [0] * 8 + [2, 2, 5, 5, 6, 6, 7, 7, 7, 8, 8, 8, 8, 9, 9, 10]
            ada_before += [ada_issue[1] + min(3 + n + (6 if n >= 12 else 0), 29) for n in range(24)]
            n = 0
            for s in range(len(slabs)):
                while n < len(ada_order) and ada_before[n] <= s:
                    load_ada(n)
                    n += 1
                if s == 0:
                    sp.dma_start(x[:], xT).then_inc(sem("x_in"), 16)
                if s >= 2:
                    sp.wait_ge(sem("slab_split"), s - 1)
                sp.dma_start(raw[s % 2][:], wstream[s]).then_inc(sem(f"slab_in{s % 2}"), 16)
            for i in range(DT):
                sp.wait_ge(sem("x_done"), count("x_done", i))
                sp.dma_start(out[:, i, :], x[:, i, :]).then_inc(sem("out_stored"), 16)
            sp.wait_ge(sem("out_stored"), 16 * DT)

        return {**sig.at}, slabs


def constants():
    f = np.float32
    i, j = np.arange(P)[:, None], np.arange(P)[None, :]
    mats = [i == j, np.ones((P, P)), i // HEAD == j // HEAD]
    rot = np.zeros((P, P))
    for out in range(P):
        if out % 64 < 32:
            rot[out + 32, out] = -1.0
        else:
            rot[out - 32, out] = 1.0
    mats += [rot, i < j, i <= j, i >= j]
    for b in LEVELS:
        mats.append((i // (2 * b) == j // (2 * b)) & (i % (2 * b) < b) & (j % (2 * b) >= b))
    mats = np.ascontiguousarray(np.stack([m.astype(f) for m in mats]).transpose(1, 0, 2))
    inv = f(10000.0) ** (-np.arange(0, 64, 2, dtype=f) / f(64))
    t = np.arange(T)
    ang = np.stack([(t // 64).astype(f)[None, :] * inv[:, None], (t % 64).astype(f)[None, :] * inv[:, None]])
    place = np.arange(P)
    full = ang[place // 64, place % 32]
    rope = np.ascontiguousarray(np.stack([np.cos(full), np.sin(full)], 1).astype(f))
    pos = np.arange(1, 17, dtype=f)
    cnt = np.stack([f(1) / np.minimum(pos, f(w)) for w in WINDOWS]).astype(f)
    return mats, rope, np.ascontiguousarray(np.broadcast_to(cnt, (P, 4, 16)))


def columns(vectors):
    parts = []
    for v in vectors:
        v = np.asarray(v).reshape(-1)
        parts.append(np.pad(v, (0, -v.size % P)).reshape(-1, P).T)
    return np.concatenate(parts, 1)


def kernel(**inputs):
    from concourse import bacc
    from concourse.bass_utils import run_bass_kernel_spmd

    a = {k: np.asarray(v) for k, v in inputs.items()}
    mats, rope, cnt = constants()
    feature_major = lambda t: np.ascontiguousarray(t.T.reshape(-1, P, t.shape[0]).transpose(1, 0, 2))
    z = lambda *s: np.zeros(s, np.float32)
    cols, small = [], []
    weights = {k: a[v] for k, v in {
        "proj_a": "proj_a", "proj_b": "proj_b", "w_out": "w_out", "w_gu": "w_gu",
        "w_down": "w_down", "w_o_gla": "w_o_gla_2", "w_o_attn": "w_o_attn_2", "w_out2": "w_out_2",
        "w_ffn_in": "w_ffn_in_2", "w_ffn_out": "w_ffn_out_2", "w_ple_proj": "w_ple_proj_2",
        "w_ple_gate": "w_ple_gate_2"}.items()}
    w_in, w_in2 = [], []
    for l in range(DEPTH):
        down = a["v_down"][l - 1] if l else z(D, 32)
        mu_v = a["mu_v"][l - 1] if l else z(32)
        v0 = a["v0"][l - 1] if l else z(D_R)
        v_up = a["v_up"][l - 1] if l else z(32, D_R)
        w = a["w_in"][l]
        n = 3 * D_R + 64 + 64 + 160
        w_in.append(np.concatenate([w[:, :n], down, z(D, 64), w[:, n:]], 1))
        mu = np.concatenate([a["mu_shift"][l], mu_v])
        cols.append(columns([a["ada_b"][l], a["norm1_g"][l], a["norm2_g"][l], mu, a["w0"][l], a["a0"][l], v0,
                             a["k_k"][l], a["k_a"][l], a["r_k"][l], a["lnx_g"][l], a["lnx_b"][l],
                             a["pool_scale"][l]]))
        small.append(np.stack([
            np.concatenate([a["w_up"][l], a["a_up"][l]]), a["g_up"][l][:P],
            np.concatenate([a["g_up"][l][P:], v_up, z(64, D_R)]),
            a["pool_w"][l].transpose(1, 0, 2).reshape(P, 512)], 1))
    cols.append(columns([a["final_g"]]))
    for l in range(DEPTH):
        w = a["w_in_2"][l]
        w_in2.append(np.concatenate([w[:, :3072], w[:, 3072:3088], z(D, 16), w[:, 3088:3104], z(D, 80), w[:, 3104:]], 1))
        cols.append(columns([a["g_mix_pre_2"][l], a["b_alpha_2"][l], a["g_gla_out_2"][l], a["g_q_norm_2"][l],
                             a["g_k_norm_2"][l], a["g_mix_post_2"][l], a["g_ffn_pre_2"][l], a["g_ffn_post_2"][l],
                             a["g_ple_post_2"][l]]))
        up = z(P, 512)
        up[0:16], up[32:48] = a["w_alpha_up_2"][l]
        small.append(np.concatenate([up[:, None], feature_major(a["p_2"][l, 0]), z(P, 1, 512)], 1))
    weights["w_in"], weights["w_in2"] = np.stack(w_in), np.stack(w_in2)

    def build(known, n_slabs):
        nc = bacc.Bacc("TRN2", target_bir_lowering=False, num_devices=1)
        shapes = {"weight_slabs": (n_slabs, P, SLAB, P), "ada_slabs": (DEPTH, 24, P, 2, D), "x_in": (P, DT, T), "c_in": (P, D), "cols": (P, NCOL),
                  "consts": (P, NK, P), "rope": (P, 2, T), "inv_count": (P, 4, 16), "small": (4, P, 4, 512)}
        args = [nc.dram_tensor(n, s, F32, kind="ExternalInput").ap() for n, s in shapes.items()]
        args.append(nc.dram_tensor("out", (P, DT, T), F32, kind="ExternalOutput").ap())
        counts, slabs = emit(nc, known, *args)
        return nc, counts, slabs

    _, counts, slabs = build(None, 400)
    nc, _, slabs = build(counts, len(slabs))
    stream = np.zeros((len(slabs), P, SLAB, P), np.float32)
    for s, blocks in enumerate(slabs):
        for i, (name, l, k, m) in enumerate(blocks):
            stream[s, :, i] = weights[name][l, k * P:(k + 1) * P, m * P:(m + 1) * P]
    ada = a["ada_w"].reshape(DEPTH, D, 24, 2, P).transpose(0, 2, 4, 3, 1)
    arrays = {"weight_slabs": stream, "ada_slabs": ada, "x_in": feature_major(a["x"][0]), "c_in": np.broadcast_to(a["c"], (P, D)),
              "cols": np.concatenate(cols, 1), "consts": mats, "rope": rope, "inv_count": cnt,
              "small": np.stack(small)}
    arrays = {k: np.ascontiguousarray(v, dtype=np.float32) for k, v in arrays.items()}
    r = run_bass_kernel_spmd(nc, [arrays], core_ids=[0])
    got = r.results[0]["out"]
    return np.ascontiguousarray(got.transpose(2, 1, 0).reshape(1, T, D))
```
